# Optimizing a Trainium2 kernel written in Bass

```python
import math
import jax, jax.numpy as jnp
from jax import lax
import numpy as np

D_MODEL = 1024
BATCH = 1
SEQ = 256
DEPTH = 2

N_A_LAYERS = DEPTH // 2
N_B_LAYERS = DEPTH - N_A_LAYERS
N_DENSE_LAYERS = (DEPTH + 1) // 2
N_MOE_LAYERS = DEPTH // 2

MLA_HEADS = 8
MLA_NOPE = 64
MLA_ROPE = 32
MLA_V = 64
MLA_QK = MLA_NOPE + MLA_ROPE
MLA_Q_LORA = 384
MLA_KV_LORA = 256
ROPE_BASE = 10000.0

SB_HEADS = 16
SB_KV_HEADS = 4
SB_GROUP = SB_HEADS // SB_KV_HEADS
SB_HEAD_DIM = 64

D_FF = 2816
N_EXPERTS = 8
TOP_K = 2
D_FF_EXPERT = 2816
PLE_DIM = 256
Q_BLOCK = 128
EPS = 1e-6

kernel_name = "yoco_mla_stickbreaking_moe_ple"

def rmsnorm(x, g):
    xf = x.astype(jnp.float32)
    y = xf * lax.rsqrt(jnp.mean(xf * xf, axis=-1, keepdims=True) + EPS) * g.astype(jnp.float32)
    return y.astype(x.dtype)

def rope(x, cos, sin):
    half = x.shape[-1] // 2
    x1, x2 = x[..., :half], x[..., half:]
    return jnp.concatenate([x1 * cos - x2 * sin, x2 * cos + x1 * sin], axis=-1)

def block_sweep(fn, q):
    b, s = q.shape[0], q.shape[1]
    nb = s // Q_BLOCK
    qb = jnp.moveaxis(q.reshape((b, nb, Q_BLOCK) + q.shape[2:]), 1, 0)
    out = lax.map(fn, (qb, jnp.arange(nb)))
    out = jnp.moveaxis(out, 0, 1)
    return out.reshape((b, s) + out.shape[3:])

def mla_attend(q, k, v):
    scale = 1.0 / math.sqrt(MLA_QK)
    key_idx = jnp.arange(k.shape[1])

    def blk(args):
        qb, i = args
        qpos = i * Q_BLOCK + jnp.arange(Q_BLOCK)
        s = jnp.einsum('bqhd,bshd->bhqs', qb, k) * scale
        mask = key_idx[None, :] <= qpos[:, None]
        w = jax.nn.softmax(jnp.where(mask, s, -jnp.inf), axis=-1)
        return jnp.einsum('bhqs,bshd->bqhd', w, v)

    return block_sweep(blk, q)

def stick_breaking_attend(q, k, v):
    scale = 1.0 / math.sqrt(SB_HEAD_DIM)
    key_idx = jnp.arange(k.shape[1])

    def blk(args):
        qb, i = args
        qpos = i * Q_BLOCK + jnp.arange(Q_BLOCK)
        z = jnp.einsum('bqkgd,bskd->bkgqs', qb, k) * scale
        mask = key_idx[None, :] < qpos[:, None]
        log_not = jnp.where(mask, jax.nn.log_sigmoid(-z), 0.0)
        rest = lax.cumsum(log_not, axis=4, reverse=True) - log_not
        a = jnp.where(mask, jnp.exp(jax.nn.log_sigmoid(z) + rest), 0.0)
        return jnp.einsum('bkgqs,bskd->bqkgd', a, v)

    return block_sweep(blk, q)

def mla_mixer(h, cos, sin, norm_attn, w_in, norm_q_lat, norm_kv_lat, w_q_up, w_kv_up,
              qk_norm_q, qk_norm_k, w_out):
    b, s, _ = h.shape
    hn = rmsnorm(h, norm_attn)
    a = hn @ w_in
    c_q = rmsnorm(a[..., :MLA_Q_LORA], norm_q_lat)
    c_kv = rmsnorm(a[..., MLA_Q_LORA:MLA_Q_LORA + MLA_KV_LORA], norm_kv_lat)
    k_pe = a[..., MLA_Q_LORA + MLA_KV_LORA:]
    q = (c_q @ w_q_up).reshape(b, s, MLA_HEADS, MLA_QK)
    kv = (c_kv @ w_kv_up).reshape(b, s, MLA_HEADS, MLA_NOPE + MLA_V)
    k_nope, v = kv[..., :MLA_NOPE], kv[..., MLA_NOPE:]
    k = jnp.concatenate([k_nope, jnp.broadcast_to(k_pe[:, :, None, :], (b, s, MLA_HEADS, MLA_ROPE))], axis=-1)
    q = rmsnorm(q, qk_norm_q).astype(jnp.float32)
    k = rmsnorm(k, qk_norm_k).astype(jnp.float32)
    c4, s4 = cos[:, :, None, :], sin[:, :, None, :]
    q = jnp.concatenate([q[..., :MLA_NOPE], rope(q[..., MLA_NOPE:], c4, s4)], axis=-1)
    k = jnp.concatenate([k[..., :MLA_NOPE], rope(k[..., MLA_NOPE:], c4, s4)], axis=-1)
    o = mla_attend(q, k, v.astype(jnp.float32))
    return o.reshape(b, s, MLA_HEADS * MLA_V).astype(h.dtype) @ w_out

def sb_mixer(h, shared_k, shared_v, norm_attn, w_q, w_o):
    b, s, _ = h.shape
    hn = rmsnorm(h, norm_attn)
    q = (hn @ w_q).reshape(b, s, SB_KV_HEADS, SB_GROUP, SB_HEAD_DIM).astype(jnp.float32)
    o = stick_breaking_attend(q, shared_k, shared_v)
    return o.reshape(b, s, SB_HEADS * SB_HEAD_DIM).astype(h.dtype) @ w_o

def dense_swiglu(x, w_gu, w_down):
    gu = x @ w_gu
    g, u = gu[..., :D_FF], gu[..., D_FF:]
    return (jax.nn.silu(g) * u) @ w_down

def moe_swiglu(x, w_router, w_gu, w_down):
    b, s, d = x.shape
    xt = x.reshape(b * s, d)
    logits = (xt @ w_router).astype(jnp.float32)
    top_vals, top_idx = lax.top_k(logits, TOP_K)
    gates = jax.nn.softmax(top_vals, axis=-1)
    combine = jnp.sum(jax.nn.one_hot(top_idx, N_EXPERTS, dtype=jnp.float32) * gates[..., None], axis=1)
    y = jnp.zeros((b * s, d), jnp.float32)
    for e in range(N_EXPERTS):
        gu = xt @ w_gu[e]
        g, u = gu[..., :D_FF_EXPERT], gu[..., D_FF_EXPERT:]
        y = y + combine[:, e:e + 1] * ((jax.nn.silu(g) * u) @ w_down[e]).astype(jnp.float32)
    return y.astype(x.dtype).reshape(b, s, d)

def setup_inputs(seed: int = 0) -> dict:
    key = jax.random.key(seed)
    ks = iter(jax.random.split(key, 40))

    def w(shape, fan_in):
        return jax.random.normal(next(ks), shape, jnp.float32) * (fan_in ** -0.5)

    def gain(shape):
        return 1.0 + 0.02 * jax.random.normal(next(ks), shape, jnp.float32)

    x = jax.random.normal(next(ks), (BATCH, SEQ, D_MODEL), jnp.float32)
    p = jax.random.normal(next(ks), (DEPTH, BATCH, SEQ, PLE_DIM), jnp.float32)
    offset = jax.random.randint(next(ks), (BATCH, 1), 0, 1024, dtype=jnp.int32)
    positions = (offset + jnp.arange(SEQ, dtype=jnp.int32)[None, :]).astype(jnp.int32)
    a_in = MLA_Q_LORA + MLA_KV_LORA + MLA_ROPE
    return {
        "x": x,
        "p": p,
        "positions": positions,
        "norm_attn_a": gain((N_A_LAYERS, D_MODEL)),
        "w_a_in": w((N_A_LAYERS, D_MODEL, a_in), D_MODEL),
        "norm_q_lat": gain((N_A_LAYERS, MLA_Q_LORA)),
        "norm_kv_lat": gain((N_A_LAYERS, MLA_KV_LORA)),
        "w_q_up": w((N_A_LAYERS, MLA_Q_LORA, MLA_HEADS * MLA_QK), MLA_Q_LORA),
        "w_kv_up": w((N_A_LAYERS, MLA_KV_LORA, MLA_HEADS * (MLA_NOPE + MLA_V)), MLA_KV_LORA),
        "qk_norm_q": gain((N_A_LAYERS, MLA_QK)),
        "qk_norm_k": gain((N_A_LAYERS, MLA_QK)),
        "w_a_out": w((N_A_LAYERS, MLA_HEADS * MLA_V, D_MODEL), MLA_HEADS * MLA_V),
        "norm_kv_shared": gain((D_MODEL,)),
        "w_kv_shared": w((D_MODEL, 2 * SB_KV_HEADS * SB_HEAD_DIM), D_MODEL),
        "norm_attn_b": gain((N_B_LAYERS, D_MODEL)),
        "w_q_b": w((N_B_LAYERS, D_MODEL, SB_HEADS * SB_HEAD_DIM), D_MODEL),
        "w_o_b": w((N_B_LAYERS, SB_HEADS * SB_HEAD_DIM, D_MODEL), SB_HEADS * SB_HEAD_DIM),
        "norm_ffn": gain((DEPTH, D_MODEL)),
        "w_ffn_gu": w((N_DENSE_LAYERS, D_MODEL, 2 * D_FF), D_MODEL),
        "w_ffn_down": w((N_DENSE_LAYERS, D_FF, D_MODEL), D_FF),
        "w_router": w((N_MOE_LAYERS, D_MODEL, N_EXPERTS), D_MODEL),
        "w_exp_gu": w((N_MOE_LAYERS, N_EXPERTS, D_MODEL, 2 * D_FF_EXPERT), D_MODEL),
        "w_exp_down": w((N_MOE_LAYERS, N_EXPERTS, D_FF_EXPERT, D_MODEL), D_FF_EXPERT),
        "norm_ple": gain((DEPTH, D_MODEL)),
        "w_ple_gate": w((DEPTH, D_MODEL, D_MODEL), D_MODEL),
        "w_ple_up": w((DEPTH, PLE_DIM, D_MODEL), PLE_DIM),
    }

def reference(x, p, positions, norm_attn_a, w_a_in, norm_q_lat, norm_kv_lat, w_q_up, w_kv_up,
              qk_norm_q, qk_norm_k, w_a_out, norm_kv_shared, w_kv_shared, norm_attn_b, w_q_b, w_o_b,
              norm_ffn, w_ffn_gu, w_ffn_down, w_router, w_exp_gu, w_exp_down,
              norm_ple, w_ple_gate, w_ple_up):
    b, s, _ = x.shape
    half = MLA_ROPE // 2
    inv_freq = jnp.exp(-math.log(ROPE_BASE) * jnp.arange(half, dtype=jnp.float32) / half)
    ang = positions.astype(jnp.float32)[..., None] * inv_freq
    cos, sin = jnp.cos(ang), jnp.sin(ang)

    h = x
    shared_k = None
    shared_v = None
    for i in range(DEPTH):
        if i < N_A_LAYERS:
            h = h + mla_mixer(h, cos, sin, norm_attn_a[i], w_a_in[i], norm_q_lat[i], norm_kv_lat[i],
                              w_q_up[i], w_kv_up[i], qk_norm_q[i], qk_norm_k[i], w_a_out[i])
        else:
            j = i - N_A_LAYERS
            h = h + sb_mixer(h, shared_k, shared_v, norm_attn_b[j], w_q_b[j], w_o_b[j])
        hn = rmsnorm(h, norm_ffn[i])
        if i % 2 == 0:
            h = h + dense_swiglu(hn, w_ffn_gu[i // 2], w_ffn_down[i // 2])
        else:
            h = h + moe_swiglu(hn, w_router[i // 2], w_exp_gu[i // 2], w_exp_down[i // 2])
        gate = jax.nn.sigmoid(rmsnorm(h, norm_ple[i]) @ w_ple_gate[i])
        h = h + gate * (p[i].astype(h.dtype) @ w_ple_up[i])
        if i == N_A_LAYERS - 1:
            kv = (rmsnorm(h, norm_kv_shared) @ w_kv_shared).reshape(b, s, 2, SB_KV_HEADS, SB_HEAD_DIM)
            shared_k = kv[:, :, 0].astype(jnp.float32)
            shared_v = kv[:, :, 1].astype(jnp.float32)
    return h


_drawn_inputs = setup_inputs


def setup_inputs(seed=0):
    import zlib

    import numpy as np

    out = dict(_drawn_inputs(seed))
    spreads = {}
    factors = {'norm_attn_a': 3.229,
     'norm_q_lat': 5.058,
     'norm_kv_lat': 3.849,
     'qk_norm_q': 7.534,
     'qk_norm_k': 5.089,
     'norm_attn_b': 37.427,
     'norm_ple': 29.024,
     'norm_kv_shared': 8.0,
     'norm_ffn': 5.708}
    for name, (base, spread) in spreads.items():
        noise = np.random.default_rng([zlib.crc32(name.encode()), seed]).standard_normal(out[name].shape)
        drawn = base * np.exp(spread * noise) if base else spread * noise
        out[name] = __import__('jax').numpy.asarray(drawn.astype(out[name].dtype))
    for name, factor in factors.items():
        out[name] = (out[name] * factor).astype(out[name].dtype)
    return out
```

```python
from contextlib import ExitStack
import math

import numpy as np
import concourse.bass as bass
from concourse import mybir

F32 = mybir.dt.float32
I32 = mybir.dt.int32
ALU = mybir.AluOpType
ACT = mybir.ActivationFunctionType
AX = mybir.AxisListType

P = 128
D = 1024
T = 256
NT = T // P
KD = D // P
EPS = 1e-6

HA, NOPE, ROPE, VD = 8, 64, 32, 64
HALF = ROPE // 2
QK = NOPE + ROPE
QL, KVL = 384, 256
NLAT = (QL + KVL) // P
ROPE_BASE = 10000.0

HB, G, HD = 16, 4, 64

FF = 2816
GW = 256
NG = FF // GW
NF = FF // P
E = 8
CAP = 128

SLOT = 2048
NSLOT = 11
NEG = -1.0e30

G_ATTN_A, G_FFN, G_PLE, G_KVS, G_ATTN_B, G_LAT = 0, 8, 24, 40, 48, 56
NGAIN = G_LAT + NLAT


def ring_plan():
    order = [("a_in", u) for u in range(3)] + [("q_up", 0), ("q_up", 1), ("kv_up", 0)]
    order += [("a_out", u) for u in range(2)]
    for g in range(NG):
        order += [("ffn_gu", 2 * g), ("ffn_gu", 2 * g + 1), ("ffn_down", g)]
    order += [("ple_gate0", u) for u in range(4)] + [("ple_up0", 0)]
    order += [("kv_shared", u) for u in range(2)] + [("q_b", u) for u in range(4)]
    order += [("o_b", u) for u in range(4)]
    front = len(order)
    expert = []
    for g in range(NG):
        expert += [("gu", 2 * g), ("gu", 2 * g + 1)]
        if g:
            expert.append(("down", g - 1))
    expert.append(("down", NG - 1))
    assert len(expert) % NSLOT == 0
    tail = [("ple_gate1", u) for u in range(4)] + [("ple_up1", 0)]
    return order, expert, tail, front


def build(nc, a, out):
    order, expert_units, tail, FRONT = ring_plan()
    UNITS = len(expert_units)
    place = {k: i for i, k in enumerate(order)}
    eplace = {k: i for i, k in enumerate(expert_units)}
    tplace = {k: i for i, k in enumerate(tail)}

    es = ExitStack()

    def sb(name, shape, dt=F32, stack=None):
        return (stack or es).enter_context(nc.sbuf_tensor(name, shape, dt))

    def sem(name):
        return es.enter_context(nc.semaphore(name))

    ps = es.enter_context(nc.psum_tensor("ps", [P, 8, 512], F32))

    ring = sb("ring", [P, NSLOT, SLOT])
    h = sb("h", [P, NT, D])
    hs = sb("hs", [P, NT, D])
    hnT = sb("hnT", [P, KD, T])
    junk = sb("junk", [P, D])
    ident = sb("ident", [P, P])
    lower = sb("lower", [P, P])
    before = sb("before", [P, P])
    ones = sb("ones", [P, P])
    slot_no_i = sb("slot_no_i", [P, 2 * P], I32)
    slot_no = sb("slot_no", [P, 2 * P])
    earlier = sb("earlier", [P, E, E])
    gains_raw = sb("gains_raw", [NGAIN, P])
    gainT = sb("gainT", [P, NGAIN])
    p_in = sb("p_in", [P, 2, NT, 256])
    pT = sb("pT", [P, 2, 2, T])
    wr = sb("wr", [P, KD, E])
    sumsq = sb("sumsq", [P, 6, NT])
    rstd = sb("rstd", [P, 6, NT])
    mean_sq = sb("mean_sq", [P, 8, 2 * NT * HA])
    newton = sb("newton", [P, 2 * NT * HA])

    ph = ExitStack()
    maskA = sb("maskA", [P, 3 * P], F32, ph)
    gq = sb("gq", [P, 2, QK], F32, ph)
    pos_i = sb("pos_i", [P, NT], I32, ph)
    pos_f = sb("pos_f", [P, NT], F32, ph)
    invf = sb("invf", [P, HALF], F32, ph)
    ang = sb("ang", [P, NT, HALF], F32, ph)
    trn = sb("trn", [P, 2, NT, HALF], F32, ph)
    red = sb("red", [P, 2, NT, HALF], F32, ph)
    sincos = sb("sincos", [P, 2, NT, HALF], F32, ph)
    lat_sq = sb("lat_sq", [P, 2, NT], F32, ph)
    lat_rstd = sb("lat_rstd", [P, 2, NT], F32, ph)
    lat = sb("lat", [P, NT, QL + KVL], F32, ph)
    latT = sb("latT", [P, NLAT, T], F32, ph)
    kpe = sb("kpe", [P, NT, ROPE], F32, ph)
    qk = sb("qk", [P, 2, NT, HA, QK], F32, ph)
    va = sb("va", [P, NT, HA, VD], F32, ph)
    qk_sq = sb("qk_sq", [P, 2, NT, HA], F32, ph)
    qk_rstd = sb("qk_rstd", [P, 2, NT, HA], F32, ph)
    sq_heads = sb("sq_heads", [P, HA * QK], F32, ph)
    rot = sb("rot", [P, 4, NT, HA, HALF], F32, ph)
    qkT = sb("qkT", [QK, 2, HA, T], F32, ph)
    probs = sb("probs", [P, 2, 2, 3 * P], F32, ph)
    row_max = sb("row_max", [P, 4, 2, 2], F32, ph)
    neg_max = sb("neg_max", [P, 4, 2, 2], F32, ph)
    row_sum = sb("row_sum", [P, 4, 2, 2], F32, ph)
    row_inv = sb("row_inv", [P, 4, 2, 2], F32, ph)
    probsT = sb("probsT", [P, 2, 2, 3 * P], F32, ph)
    oTA = sb("oTA", [P, 4, T], F32, ph)
    ph.close()
    ph = ExitStack()
    d_silu = sb("d_silu", [P, 2, T], F32, ph)
    d_hT = sb("d_hT", [P, 4, T], F32, ph)
    ph.close()
    ph = ExitStack()
    sig = sb("sig", [P, NT, D], F32, ph)
    ph.close()
    ph = ExitStack()
    hnT2 = sb("hnT2", [P, KD, T], F32, ph)
    negT = sb("negT", [P, P], F32, ph)
    qTB = sb("qTB", [P, KD, T], F32, ph)
    kTB = sb("kTB", [P, G, T], F32, ph)
    vB = sb("vB", [P, NT, G * HD], F32, ph)
    zm = sb("zm", [P, 2, 1536], F32, ph)
    sp = sb("sp", [P, 2, 1536], F32, ph)
    oTB = sb("oTB", [P, KD, T], F32, ph)
    ph.close()
    ph = ExitStack()
    lg = sb("lg", [P, NT, E], F32, ph)
    cmp_gt = sb("cmp_gt", [P, NT, E, E], F32, ph)
    cmp_eq = sb("cmp_eq", [P, NT, E, E], F32, ph)
    rank = sb("rank", [P, NT, E], F32, ph)
    top = sb("top", [P, NT], F32, ph)
    ntop = sb("ntop", [P, NT], F32, ph)
    picked = sb("picked", [P, NT, E], F32, ph)
    gexp = sb("gexp", [P, NT, E], F32, ph)
    gsum = sb("gsum", [P, NT], F32, ph)
    gate = sb("gate", [P, NT, E], F32, ph)
    slot_of = sb("slot_of", [P, NT, E], F32, ph)
    counts = sb("counts", [P, E], I32, ph)
    pick = sb("pick", [P, NT, P], F32, ph)
    pick_g = sb("pick_g", [P, NT, P], F32, ph)
    pick_gT = sb("pick_gT", [P, T], F32, ph)
    xgT = sb("xgT", [P, KD, P], F32, ph)
    e_silu = sb("e_silu", [P, 2, GW], F32, ph)
    e_h = sb("e_h", [P, 2, GW], F32, ph)
    e_hT = sb("e_hT", [P, 2, GW], F32, ph)
    ye = sb("ye", [P, D], F32, ph)
    ph.close()

    x_in, gains_in, qkg_in, pos_in, p_inS, wr_in = map(sem, ("x_in", "gains_in", "qkg_in", "pos_in", "p_arrived", "wr_in"))
    landed = [sem(f"landed{i}") for i in range(NSLOT)]
    pool_chain, dve_chain, act_chain = map(sem, ("pool_chain", "dve_chain", "act_chain"))
    ident_ready, consts_ready, masks_b_ready = map(sem, ("ident_ready", "consts_ready", "masks_b_ready"))
    small_T, pT_done = map(sem, ("small_T", "pT_done"))
    sq_done, mean_ready, seed_ready, hs_done, hT_done, hnT_done, h_updated = map(
        sem, ("sq_done", "mean_ready", "seed_ready", "hs_done", "hT_done", "hnT_done", "h_updated"))
    angles_done, trig_done = map(sem, ("angles_done", "trig_done"))
    a_ready, lat_sq_done, lat_scaled, lat_T, latT_done = map(
        sem, ("a_ready", "lat_sq_done", "lat_scaled", "lat_T", "latT_done"))
    q_done, kv_done, kpe_spread, qkv_copied, qk_ready = map(
        sem, ("q_done", "kv_done", "kpe_spread", "qkv_copied", "qk_ready"))
    qk_T, qT_done, kT_done = map(sem, ("qk_T", "qT_done", "kT_done"))
    sc_ready, sc_read, exp_done, probs_ready, probs_T, probsT_done, oA_ready, oTA_done, a_out_ready, o_b_ready = map(
        sem, ("sc_ready", "sc_read", "exp_done", "probs_ready", "probs_T", "probsT_done", "oA_ready", "oTA_done", "a_out_ready", "o_b_ready"))
    d_gu, d_silu_done, d_act_done, d_down = map(sem, ("d_gu", "d_silu_done", "d_act_done", "d_down"))
    gate_ready, up_ready, sig_done = map(sem, ("gate_ready", "up_ready", "sig_done"))
    kv_ready, qB_ready, kTB_done, vB_done, qTB_done = map(sem, ("kv_ready", "qB_ready", "kTB_done", "vB_done", "qTB_done"))
    z_ready, zm_done, ln_done, sp_done, sum_ready, w_done, att_done, oB_ready, oTB_done = map(
        sem, ("z_ready", "zm_done", "ln_done", "sp_done", "sum_ready", "w_done", "att_done", "oB_ready", "oTB_done"))
    lg_ready, top_done, gexp_done, picked_done, pos_ready, route_done = map(
        sem, ("lg_ready", "top_done", "gexp_done", "picked_done", "pos_ready", "route_done"))
    e_pick, e_pickT, e_pickT_done, e_xg, e_xg_done, e_gu_half, e_gu, e_silu_done, e_act_done = map(
        sem, ("e_pick", "e_pickT", "e_pickT_done", "e_xg", "e_xg_done", "e_gu_half", "e_gu", "e_silu_done", "e_act_done"))
    e_T, e_hT_done, e_down, e_y_low, e_y_high, e_scat, e_added = map(
        sem, ("e_T", "e_hT_done", "e_down", "e_y_low", "e_y_high", "e_scat", "e_added"))
    out_sem = sem("out_stored")

    def slot_of_unit(pos):
        return ring[:, pos % NSLOT, :]

    def view(pos, k, n):
        return slot_of_unit(pos)[:, 0:k * n].rearrange("p (k n) -> p k n", k=k)

    def rows(w, k0, k1):
        return w.rearrange("(k p) n -> p k n", p=P)[:, k0:k1, :]

    def gu_rows(w, u):
        g, k0 = u // 2, (u % 2) * 4
        return w.rearrange("(k p) (s n) -> p k s n", p=P, s=2)[:, k0:k0 + 4, :, g * GW:(g + 1) * GW]

    def arrivals(units, slot, first=0):
        return sum(16 * (2 if name in ("ffn_gu", "gu") else 1) for i, (name, _) in enumerate(units) if (first + i) % NSLOT == slot)

    def unit_dma(sp_, name, u, pos, e=None):
        src3 = {
            "a_in": (a["w_a_in"][0], 3, QL + KVL + ROPE, KD), "q_up": (a["w_q_up"][0], 2, HA * QK, 3),
            "kv_up": (a["w_kv_up"][0], 2, HA * (NOPE + VD), 2), "a_out": (a["w_a_out"][0], 2, D, 4),
            "ffn_down": (a["w_ffn_down"][0], 2, D, NF), "ple_gate0": (a["w_ple_gate"][0], 2, D, KD),
            "ple_gate1": (a["w_ple_gate"][1], 2, D, KD), "ple_up0": (a["w_ple_up"][0], 2, D, 2),
            "ple_up1": (a["w_ple_up"][1], 2, D, 2), "kv_shared": (a["w_kv_shared"], 4, 2 * G * HD, KD),
            "q_b": (a["w_q_b"][0], 2, D, KD), "o_b": (a["w_o_b"][0], 2, D, KD),
        }
        if name in ("ffn_gu", "gu"):
            w = a["w_ffn_gu"][0] if name == "ffn_gu" else a["w_exp_gu"][0, bass.ds(e, 1)].rearrange("e k n -> (e k) n")
            dst, src = view(pos, 4, 2 * GW), gu_rows(w, u)
            for s in range(2):
                sp_.dma_start(dst[:, :, s * GW:(s + 1) * GW], src[:, :, s, :]).then_inc(landed[pos % NSLOT], 16)
            return
        elif name == "down":
            w = a["w_exp_down"][0, bass.ds(e, 1)].rearrange("e k n -> (e k) n")
            dst, src = view(pos, 2, D), rows(w, 2 * u, 2 * u + 2)
        else:
            w, per, n, kk = src3[name]
            k0, k1 = per * u, min(per * (u + 1), kk)
            dst, src = view(pos, k1 - k0, n), rows(w, k0, k1)
        sp_.dma_start(dst, src).then_inc(landed[pos % NSLOT], 16)

    def released(name, u):
        return {
            "a_in": (a_ready, u + 1), "q_up": (q_done, 1), "kv_up": (kv_done, 1), "a_out": (a_out_ready, u + 1),
            "ffn_gu": (d_gu, 2 * (u // 2) + 2), "ffn_down": (d_down, 2 * u + 2), "ple_gate0": (gate_ready, u + 1),
            "ple_up0": (up_ready, 1), "kv_shared": (kv_ready, 2), "q_b": (qB_ready, 4), "o_b": (o_b_ready, u + 1),
            "gu": (e_gu if u % 2 else e_gu_half, u // 2 + 1), "down": (e_down, u + 1),
        }[name]

    def bc(ap, shape):
        return ap.to_broadcast(shape)

    def banks(b0, b1):
        return ps[:, b0:b1, :].rearrange("p b n -> p (b n)")

    block = es.enter_context(nc.Block())

    RS_NORM, RS_LAT, RS_QK = (0, 3, 4, 5, 6, 7), 1, 2

    def epos(name, u):
        return FRONT + eplace[(name, u)]

    @block.sync
    def _(sp_):
        for t in range(NT):
            sp_.dma_start(h[:, t, :], a["x"][0, t * P:(t + 1) * P, :]).then_inc(x_in, 16)
        for u in range(6):
            unit_dma(sp_, *order[u], u)
        for i, (w, n, r0) in enumerate((
            ("norm_attn_a", 8, G_ATTN_A), ("norm_ffn", 16, G_FFN), ("norm_ple", 16, G_PLE), ("norm_attn_b", 8, G_ATTN_B),
            ("norm_q_lat", 3, G_LAT), ("norm_kv_lat", 2, G_LAT + 3),
        )):
            sp_.dma_start(gains_raw[r0:r0 + n, :], a[w].rearrange("l (k d) -> (l k) d", d=P)).then_inc(gains_in, 16)
        sp_.dma_start(gains_raw[G_KVS:G_KVS + 8, :], a["norm_kv_shared"].rearrange("(k d) -> k d", d=P)).then_inc(gains_in, 16)
        sp_.dma_start(pos_i[:, :], a["positions"].rearrange("b (t p) -> p (b t)", p=P), allow_slow_non_contiguous=True).then_inc(pos_in, 16)
        sp_.dma_start(gq[:, 0, :], a["qk_norm_q"].to_broadcast([P, QK])).then_inc(qkg_in, 16)
        sp_.dma_start(gq[:, 1, :], a["qk_norm_k"].to_broadcast([P, QK])).then_inc(qkg_in, 16)
        for i in range(2):
            sp_.dma_start(p_in[:, i], a["p"][i, 0].rearrange("(t p) c -> p t c", p=P)).then_inc(p_inS, 16)
        sp_.dma_start(wr[:, :, :], a["w_router"][0].rearrange("(k p) e -> p k e", p=P)).then_inc(wr_in, 16)
        for pos in range(6, FRONT):
            if pos >= NSLOT:
                sp_.wait_ge(*released(*order[pos - NSLOT]))
            unit_dma(sp_, *order[pos], pos)

        def expert_loads(m, e):
            for i, (name, u) in enumerate(expert_units):
                s, count = released(*expert_units[i - NSLOT])
                sp_.wait_ge(s, m * NG + (count if i < NSLOT else count + NG))
                unit_dma(sp_, name, u, FRONT + i, e)

        for i, (name, u) in enumerate(expert_units):
            sp_.wait_ge(*released(*(order[i - NSLOT] if i < NSLOT else expert_units[i - NSLOT])))
            unit_dma(sp_, name, u, FRONT + i, 0)
        with sp_.Fori(0, E - 1) as m:
            expert_loads(m, m + 1)
        sp_.wait_ge(route_done, 1)
        before_last = sp_.alloc_register("before_last_sp")
        sp_.reg_mov(before_last, E - 1)
        with sp_.Fori(0, E) as e:
            many = sp_.value_load(counts[0:1, bass.ds(e, 1)], min_val=0, max_val=T)
            with sp_.If(many > CAP):
                expert_loads(sp_.snap(before_last), e)
                sp_.reg_add(before_last, before_last, 1)
        m = sp_.snap(before_last)
        for i, (name, u) in enumerate(tail):
            s, count = released(*expert_units[i - NSLOT])
            sp_.wait_ge(s, m * NG + count)
            unit_dma(sp_, name, u, FRONT + i)
        for t in range(NT):
            sp_.wait_ge(h_updated, 8 + t + 1)
            sp_.dma_start(out[0, t * P:(t + 1) * P, :], h[:, t, :]).then_inc(out_sem, 16)
        sp_.wait_ge(out_sem, 16 * NT)

    @block.gpsimd
    def _(pool):
        chain = [0]

        def link(ins):
            chain[0] += 1
            ins.then_inc(pool_chain, 1)
            pool.wait_ge(pool_chain, chain[0])

        link(pool.memset(ident[:], 0.0))
        pool.affine_select(out=ident[:], in_=ident[:], compare_op=ALU.not_equal, fill=1.0, base=0,
                           pattern=[[-1, P]], channel_multiplier=1).then_inc(ident_ready, 1)
        link(pool.memset(ones[:], 1.0))
        link(pool.affine_select(out=lower[:], in_=ones[:], compare_op=ALU.is_ge, fill=0.0, base=0,
                                pattern=[[-1, P]], channel_multiplier=1))
        link(pool.tensor_scalar(before[:], lower[:], -1.0, 1.0, ALU.mult, ALU.add))
        link(pool.memset(maskA[:], 0.0))
        for c in (0, 2):
            link(pool.affine_select(out=maskA[:, c * P:(c + 1) * P], in_=maskA[:, c * P:(c + 1) * P],
                                    compare_op=ALU.is_ge, fill=NEG, base=0, pattern=[[-1, P]], channel_multiplier=1))
        for i in range(HALF):
            f = np.exp(np.float32(np.float32(-math.log(ROPE_BASE)) * np.float32(i) / np.float32(HALF)), dtype=np.float32)
            link(pool.memset(invf[:, i:i + 1], float(f)))
        link(pool.iota(slot_no_i[:], pattern=[[1, 2 * P]], base=0, channel_multiplier=0))
        link(pool.tensor_copy(slot_no[:], slot_no_i[:]))
        link(pool.memset(earlier[:], 1.0))
        pool.affine_select(out=earlier[:], in_=earlier[:], compare_op=ALU.is_ge, fill=0.0, base=-1,
                           pattern=[[1, E], [-1, E]], channel_multiplier=0).then_inc(consts_ready, 1)

        pool.wait_ge(h_updated, 4)
        link(pool.memset(negT[:], 0.0))
        pool.affine_select(out=negT[:], in_=negT[:], compare_op=ALU.is_gt, fill=NEG, base=0,
                           pattern=[[1, P]], channel_multiplier=-1).then_inc(masks_b_ready, 1)

    @block.scalar
    def _(act):
        chain = [0]

        def link(ins):
            chain[0] += 1
            ins.then_inc(act_chain, 1)
            act.wait_ge(act_chain, chain[0])

        def rsqrt_seed(r, dst):
            act.wait_ge(mean_ready, r + 1)
            link(act.activation(dst, mean_sq[:, r, 0:dst.shape[1]], ACT.Ln))
            act.activation(dst, dst, ACT.Exp, scale=-0.5).then_inc(seed_ready, 1)

        def norm(k):
            for t in range(NT):
                if k == 0:
                    act.wait_ge(x_in, 16 * NT)
                elif k <= 4:
                    act.wait_ge(h_updated, 2 * (k - 1) + t + 1) if k != 4 else act.wait_ge(h_updated, 6 + t + 1)
                if NT * k + t:
                    act.wait_ge(sq_done, NT * k + t)
                act.activation(junk[:], h[:, t, :], ACT.Square, accum_out=sumsq[:, k, t:t + 1]).then_inc(sq_done, 1)
            rsqrt_seed(RS_NORM[k], rstd[:, k, :])

        norm(0)
        act.wait_ge(angles_done, 1)
        act.activation(sincos[:].rearrange("p s t i -> p (s t i)"), red[:].rearrange("p s t i -> p (s t i)"), ACT.Sin).then_inc(trig_done, 1)
        for i in range(2):
            act.wait_ge(small_T, 2 + i)
            act.copy(pT[:, i].rearrange("p c t -> p (c t)"), ps[:, 1 + i, :]).then_inc(pT_done, 1)
        act.wait_ge(a_ready, 3)
        for t in range(NT):
            if t:
                act.wait_ge(lat_sq_done, 2)
            act.activation(junk[:, 0:QL], ps[:, 2 * t, 0:QL], ACT.Square, accum_out=lat_sq[:, 0, t:t + 1]).then_inc(lat_sq_done, 1)
            act.activation(junk[:, QL:QL + KVL], ps[:, 2 * t + 1, 0:KVL], ACT.Square, accum_out=lat_sq[:, 1, t:t + 1]).then_inc(lat_sq_done, 1)
        rsqrt_seed(RS_LAT, lat_rstd[:].rearrange("p a t -> p (a t)"))
        act.wait_ge(q_done, 1)
        for t in range(NT):
            act.copy(qk[:, 0, t].rearrange("p (b h) c -> p b (h c)", b=2), ps[:, 2 * t:2 * t + 2, 0:4 * QK])\
               .then_inc(qkv_copied, 1)
        act.wait_ge(kv_done, 1)
        for t in range(NT):
            kv = banks(4 + 2 * t, 6 + 2 * t).rearrange("p (h c) -> p h c", c=NOPE + VD)
            act.copy(qk[:, 1, t, :, 0:NOPE], kv[:, :, 0:NOPE])
            act.copy(va[:, t], kv[:, :, NOPE:]).then_inc(qkv_copied, 1)
        rsqrt_seed(RS_QK, qk_rstd[:].rearrange("p a t h -> p (a t h)"))
        act.wait_ge(qk_T, 4)
        for j in range(4):
            act.copy(qkT[:, 0, 2 * j:2 * j + 2, :].rearrange("p h t -> p (h t)"), ps[0:QK, j, :]).then_inc(qT_done, 1)

        scale = 1.0 / math.sqrt(QK)

        def probs_copy(j):
            act.wait_ge(probs_T, j + 1)
            if j >= 2:
                act.wait_ge(oA_ready, j - 1)
            act.copy(probsT[:, j % 2], ps[:, 4:6, 0:3 * P]).then_inc(probsT_done, 1)

        for j in range(4):
            act.wait_ge(sc_read, 2 * j + 2)
            for hh in range(2):
                for t, (c0, c1) in enumerate(((0, P), (P, 3 * P))):
                    s = probs[:, j % 2, hh, c0:c1]
                    ins = act.activation(s, s, ACT.Exp, bias=neg_max[:, j, t, hh:hh + 1], scale=scale,
                                         accum_out=row_sum[:, j, t, hh:hh + 1])
            ins.then_inc(exp_done, 1)
            if j:
                probs_copy(j - 1)
        probs_copy(3)
        act.wait_ge(oA_ready, 4)
        for b in range(2):
            act.copy(oTA[:, 2 * b:2 * b + 2, :].rearrange("p c t -> p (c t)"), ps[:, 6 + b, :]).then_inc(oTA_done, 1)
        norm(1)
        for i in range(NF):
            act.wait_ge(d_gu, i + 1)
            if i >= 2:
                act.wait_ge(d_act_done, i - 1)
            act.activation(d_silu[:, i % 2, :], ps[:, 4 + i % 4, 0:T], ACT.Silu).then_inc(d_silu_done, 1)
        norm(2)

        def sigmoids(i):
            act.wait_ge(gate_ready, 4 * i + 4)
            for t in range(NT):
                act.activation(sig[:, t, :], banks(2 * t, 2 * t + 2), ACT.Sigmoid).then_inc(sig_done, 1)

        sigmoids(0)
        norm(3)
        act.wait_ge(kv_ready, 2)
        act.copy(vB[:].rearrange("p t d -> p (t d)"), ps[:, 1, :]).then_inc(vB_done, 1)
        for b in range(4):
            act.wait_ge(qB_ready, b + 1)
            act.mul(qTB[:, 2 * b:2 * b + 2, :].rearrange("p c t -> p (c t)"), ps[:, 4 + b, :], HD ** -0.5).then_inc(qTB_done, 1)

        def soft(g):
            act.wait_ge(zm_done, g + 1)
            if g >= 2:
                act.wait_ge(oB_ready, g - 1)
            link(act.activation(sp[:, g % 2], zm[:, g % 2], ACT.Abs))
            link(act.activation(sp[:, g % 2], sp[:, g % 2], ACT.Exp, scale=-1.0))
            act.activation(sp[:, g % 2], sp[:, g % 2], ACT.Ln, bias=1.0).then_inc(ln_done, 1)

        def weights_of(g):
            act.wait_ge(w_done, g + 1)
            act.activation(sp[:, g % 2], zm[:, g % 2], ACT.Exp).then_inc(att_done, 1)

        for g in range(G + 1):
            if g < G:
                soft(g)
            if g:
                weights_of(g - 1)
        norm(4)
        act.wait_ge(top_done, 1)
        for t in range(NT):
            act.activation(gexp[:, t, :], lg[:, t, :], ACT.Exp, bias=ntop[:, t:t + 1]).then_inc(gexp_done, 1)

        def expert_pass(n):
            act.wait_ge(e_pickT, n + 1)
            act.copy(pick_gT[:, :], ps[:, 7, 0:T]).then_inc(e_pickT_done, 1)

            def hT_copy(g):
                act.wait_ge(e_T, n * NG + (g + 1))
                if g >= 2:
                    act.wait_ge(e_down, n * NG + (g - 1))
                act.copy(e_hT[:, g % 2, :], ps[:, 6, 0:GW]).then_inc(e_hT_done, 1)

            for g in range(NG):
                if g:
                    hT_copy(g - 1)
                act.wait_ge(e_gu, n * NG + (g + 1))
                if g >= 2:
                    act.wait_ge(e_act_done, n * NG + (g - 1))
                act.activation(e_silu[:, g % 2, :], ps[:, 4 + g % 2, 0:GW], ACT.Silu).then_inc(e_silu_done, 1)
            hT_copy(NG - 1)
            act.wait_ge(e_down, n * NG + NG)
            act.copy(ye[:, 0:512], ps[:, 0, :]).then_inc(e_y_low, 1)

        with act.Fori(0, E) as e:
            expert_pass(e)
        act.wait_ge(route_done, 1)
        passes = act.alloc_register("passes_act")
        act.reg_mov(passes, E)
        with act.Fori(0, E) as e:
            many = act.value_load(counts[0:1, bass.ds(e, 1)], min_val=0, max_val=T)
            with act.If(many > CAP):
                expert_pass(act.snap(passes))
                act.reg_add(passes, passes, 1)
        act.wait_ge(e_added, act.snap(passes) * 2)
        norm(5)
        sigmoids(1)

    @block.vector
    def _(dve):
        chain = [0]

        def link(ins):
            chain[0] += 1
            ins.then_inc(dve_chain, 1)
            dve.wait_ge(dve_chain, chain[0])

        dve.wait_ge(pos_in, 16)
        dve.wait_ge(consts_ready, 1)
        link(dve.tensor_copy(pos_f[:], pos_i[:]))
        for t in range(NT):
            link(dve.tensor_scalar(ang[:, t, :], invf[:], pos_f[:, t:t + 1], None, ALU.mult))
        PI1, PI2 = 6.28125, float(np.float32(0.0019340515136718750))
        PI3 = float(np.float32(2 * math.pi - PI1 - PI2))
        MAGIC = 1.5 * 2 ** 23
        af = ang[:].rearrange("p t i -> p (t i)")
        for s, quarter in enumerate((0.0, 0.25)):
            n = trn[:, s].rearrange("p t i -> p (t i)")
            r = red[:, s].rearrange("p t i -> p (t i)")
            link(dve.tensor_scalar(n, af, 1.0 / (2 * math.pi), quarter, ALU.mult, ALU.add))
            link(dve.tensor_scalar(n, n, MAGIC, None, ALU.add))
            link(dve.tensor_scalar(n, n, MAGIC, None, ALU.subtract))
            link(dve.scalar_tensor_tensor(out=r, in0=n, scalar=-PI1, in1=af, op0=ALU.mult, op1=ALU.add))
            link(dve.scalar_tensor_tensor(out=r, in0=n, scalar=-PI2, in1=r, op0=ALU.mult, op1=ALU.add))
            link(dve.scalar_tensor_tensor(out=r, in0=n, scalar=-PI3, in1=r, op0=ALU.mult, op1=ALU.add))
            if s:
                link(dve.tensor_scalar(r, r, math.pi / 2, None, ALU.add))
        rf = red[:].rearrange("p s t i -> p (s t i)")
        PIF = 3.1415925
        dve.tensor_scalar(rf, rf, PIF, -PIF, ALU.min, ALU.max).then_inc(angles_done, 1)

        dve.wait_ge(small_T, 1)
        link(dve.tensor_copy(gainT[:], ps[:, 0, 0:NGAIN]))

        def means(r, parts):
            c = 0
            for src, width in parts:
                n = src.shape[1]
                ins = dve.tensor_scalar(mean_sq[:, r, c:c + n], src, 1.0 / width, EPS, ALU.mult, ALU.add)
                c += n
            ins.then_inc(mean_ready, 1)

        def refine(r, y):
            m, w = mean_sq[:, r, 0:y.shape[1]], newton[:, 0:y.shape[1]]
            dve.wait_ge(seed_ready, r + 1)
            link(dve.tensor_tensor(w, y, y, ALU.mult))
            link(dve.tensor_tensor(w, w, m, ALU.mult))
            link(dve.tensor_scalar(w, w, -0.5, 1.5, ALU.mult, ALU.add))
            link(dve.tensor_tensor(y, y, w, ALU.mult))

        def norm(k, gain, dst=hnT, gain2=None):
            dve.wait_ge(sq_done, NT * (k + 1))
            means(RS_NORM[k], ((sumsq[:, k, :], D),))
            refine(RS_NORM[k], rstd[:, k, :])
            for t in range(NT):
                dve.tensor_scalar(hs[:, t, :], h[:, t, :], rstd[:, k, t:t + 1], None, ALU.mult).then_inc(hs_done, 1)
            for t in range(NT):
                for half in range(2):
                    f = 2 * t + half
                    dve.wait_ge(hT_done, 4 * k + f + 1)
                    src = ps[:, 4 + f, :].rearrange("p (c n) -> p c n", c=4)
                    for d, g in ((dst, gain), (hnT2, gain2)):
                        if g is None:
                            continue
                        gg = bc(gainT[:, g + 4 * half:g + 4 * half + 4].unsqueeze(2), [P, 4, P])
                        ins = dve.tensor_tensor(d[:, 4 * half:4 * half + 4, t * P:(t + 1) * P], src, gg, ALU.mult)
                    ins.then_inc(hnT_done, 1)

        norm(0, G_ATTN_A)
        dve.wait_ge(lat_sq_done, 2 * NT)
        means(RS_LAT, ((lat_sq[:, 0, :], QL), (lat_sq[:, 1, :], KVL)))
        refine(RS_LAT, lat_rstd[:].rearrange("p a t -> p (a t)"))
        for t in range(NT):
            dve.tensor_scalar(lat[:, t, 0:QL], ps[:, 2 * t, 0:QL], lat_rstd[:, 0, t:t + 1], None, ALU.mult)
            dve.tensor_scalar(lat[:, t, QL:], ps[:, 2 * t + 1, 0:KVL], lat_rstd[:, 1, t:t + 1], None, ALU.mult)
            dve.tensor_copy(kpe[:, t, :], ps[:, 2 * t + 1, KVL:KVL + ROPE]).then_inc(lat_scaled, 1)
        dve.wait_ge(lat_scaled, NT)
        dve.tensor_copy(qk[:, 1, :, :, NOPE:], bc(kpe[:, :, :].unsqueeze(2), [P, NT, HA, ROPE])).then_inc(kpe_spread, 1)
        for t in range(NT):
            dve.wait_ge(lat_T, t + 1)
            dve.tensor_tensor(latT[:, 0:4, t * P:(t + 1) * P], ps[:, 4 + 2 * t, :].rearrange("p (c n) -> p c n", c=4),
                              bc(gainT[:, G_LAT:G_LAT + 4].unsqueeze(2), [P, 4, P]), ALU.mult)
            dve.tensor_scalar(latT[:, 4, t * P:(t + 1) * P], ps[:, 5 + 2 * t, 0:P], gainT[:, G_LAT + 4:G_LAT + 5], None,
                              ALU.mult).then_inc(latT_done, 1)
        dve.wait_ge(kpe_spread, 1)
        for w in range(2):
            dve.wait_ge(qkv_copied, 2 * w + 2)
            for t in range(NT):
                sq = sq_heads[:].rearrange("p (h c) -> p h c", c=QK)
                link(dve.tensor_tensor(sq, qk[:, w, t], qk[:, w, t], ALU.mult))
                link(dve.tensor_reduce(qk_sq[:, w, t, :], sq, AX.X, ALU.add))
        means(RS_QK, ((qk_sq[:].rearrange("p a t h -> p (a t h)"), QK),))
        refine(RS_QK, qk_rstd[:].rearrange("p a t h -> p (a t h)"))
        dve.wait_ge(qkg_in, 32)
        dve.wait_ge(trig_done, 1)
        for w in range(2):
            x = qk[:, w].rearrange("p t h c -> p (t h) c")
            link(dve.tensor_tensor(x, x, bc(qk_rstd[:, w].rearrange("p t h -> p (t h)").unsqueeze(2), [P, NT * HA, QK]), ALU.mult))
            link(dve.tensor_tensor(x, x, bc(gq[:, w, :].unsqueeze(1), [P, NT * HA, QK]), ALU.mult))
            x1, x2 = qk[:, w, :, :, NOPE:NOPE + HALF], qk[:, w, :, :, NOPE + HALF:]
            sn = bc(sincos[:, 0].unsqueeze(2), [P, NT, HA, HALF])
            cs = bc(sincos[:, 1].unsqueeze(2), [P, NT, HA, HALF])
            dve.tensor_tensor(rot[:, 0], x1, cs, ALU.mult)
            dve.tensor_tensor(rot[:, 1], x2, sn, ALU.mult)
            dve.tensor_tensor(rot[:, 2], x2, cs, ALU.mult)
            link(dve.tensor_tensor(rot[:, 3], x1, sn, ALU.mult))
            dve.tensor_tensor(x1, rot[:, 0], rot[:, 1], ALU.subtract)
            dve.tensor_tensor(x2, rot[:, 2], rot[:, 3], ALU.add).then_inc(qk_ready, 1)
        for j in range(4):
            dve.wait_ge(qk_T, 5 + j)
            dve.tensor_copy(qkT[:, 1, 2 * j:2 * j + 2, :].rearrange("p h t -> p (h t)"), ps[0:QK, 4 + j, :]).then_inc(kT_done, 1)

        def mask_max(j):
            dve.wait_ge(sc_ready, j + 1)
            if j >= 2:
                dve.wait_ge(probs_T, j - 1)
            b = 2 * (j % 2)
            s = probs[:, j % 2]
            dve.tensor_tensor(s, ps[:, b:b + 2, 0:3 * P], bc(maskA[:].unsqueeze(1), [P, 2, 3 * P]), ALU.add).then_inc(sc_read, 1)
            dve.wait_ge(sc_read, 2 * j + 1)
            dve.tensor_reduce(row_max[:, j, 0, :], s[:, :, 0:P], AX.X, ALU.max)
            link(dve.tensor_reduce(row_max[:, j, 1, :], s[:, :, P:], AX.X, ALU.max))
            dve.tensor_scalar(neg_max[:, j], row_max[:, j], -1.0 / math.sqrt(QK), None, ALU.mult).then_inc(sc_read, 1)

        def normalise(j):
            dve.wait_ge(exp_done, j + 1)
            link(dve.reciprocal(row_inv[:, j], row_sum[:, j]))
            for hh in range(2):
                for t, (c0, c1) in enumerate(((0, P), (P, 3 * P))):
                    s = probs[:, j % 2, hh, c0:c1]
                    ins = dve.tensor_scalar(s, s, row_inv[:, j, t, hh:hh + 1], None, ALU.mult)
            ins.then_inc(probs_ready, 1)

        for j in range(5):
            if j < 4:
                mask_max(j)
            if j:
                normalise(j - 1)

        def add_to_h(ready, count):
            dve.wait_ge(ready, count)
            for t in range(NT):
                dve.tensor_tensor(h[:, t, :], h[:, t, :], banks(2 * t, 2 * t + 2), ALU.add).then_inc(h_updated, 1)

        add_to_h(a_out_ready, 2)
        norm(1, G_FFN)
        for i in range(NF):
            dve.wait_ge(d_silu_done, i + 1)
            if i >= 4:
                dve.wait_ge(d_down, i - 3)
            dve.tensor_tensor(d_hT[:, i % 4, :], d_silu[:, i % 2, :], ps[:, 4 + i % 4, T:2 * T], ALU.mult).then_inc(d_act_done, 1)
        add_to_h(d_down, NF)
        norm(2, G_PLE)

        def ple(i):
            dve.wait_ge(up_ready, i + 1)
            for t in range(NT):
                dve.wait_ge(sig_done, 2 * i + t + 1)
                link(dve.tensor_tensor(sig[:, t, :], sig[:, t, :], banks(4 + 2 * t, 6 + 2 * t), ALU.mult))
                dve.tensor_tensor(h[:, t, :], h[:, t, :], sig[:, t, :], ALU.add).then_inc(h_updated, 1)

        ple(0)
        norm(3, G_ATTN_B, hnT, G_KVS)
        dve.wait_ge(kv_ready, 1)
        for g in range(G):
            src = ps[HD * (g % 2):HD * (g % 2) + HD, 0, (g // 2) * T:(g // 2 + 1) * T]
            dve.tensor_copy(kTB[0:HD, g, :], src)
            ins = dve.tensor_copy(kTB[HD:2 * HD, g, :], src)
        ins.then_inc(kTB_done, 1)
        dve.wait_ge(masks_b_ready, 1)

        def mask_z(g):
            dve.wait_ge(z_ready, g + 1)
            if g >= 2:
                dve.wait_ge(att_done, g - 1)
            dve.tensor_tensor(zm[:, g % 2, 0:1024].rearrange("p (b q) -> p b q", q=P), banks(0, 2).rearrange("p (b q) -> p b q", q=P),
                              bc(negT[:].unsqueeze(1), [P, 8, P]), ALU.add)
            dve.tensor_copy(zm[:, g % 2, 1024:].rearrange("p (b q) -> p b q", b=2), ps[:, 2:4, 0:256]).then_inc(zm_done, 1)

        def softplus(g):
            dve.wait_ge(ln_done, g + 1)
            dve.scalar_tensor_tensor(out=sp[:, g % 2], in0=zm[:, g % 2], scalar=0.0, in1=sp[:, g % 2],
                                     op0=ALU.max, op1=ALU.add).then_inc(sp_done, 1)

        def log_weights(g):
            dve.wait_ge(sum_ready, g + 1)
            dve.tensor_tensor(zm[:, g % 2, :], zm[:, g % 2, :], banks(4, 7), ALU.subtract).then_inc(w_done, 1)

        def out_heads(g):
            dve.wait_ge(oB_ready, g + 1)
            for t in range(NT):
                ins = dve.tensor_copy(oTB[:, 2 * g:2 * g + 2, t * P:(t + 1) * P],
                                      ps[:, 7, t * 256:(t + 1) * 256].rearrange("p (c q) -> p c q", c=2))
            ins.then_inc(oTB_done, 1)

        for g in range(G + 1):
            if g < G:
                mask_z(g)
            if g:
                log_weights(g - 1)
            if g < G:
                softplus(g)
            if g:
                out_heads(g - 1)
        add_to_h(o_b_ready, 4)
        norm(4, G_FFN + 8)

        dve.wait_ge(lg_ready, 1)
        link(dve.tensor_copy(lg[:].rearrange("p t e -> p (t e)"), ps[:, 0, 0:NT * E]))
        for t in range(NT):
            other = bc(lg[:, t, :].unsqueeze(1), [P, E, E])
            own = bc(lg[:, t, :].unsqueeze(2), [P, E, E])
            dve.tensor_tensor(cmp_gt[:, t], other, own, ALU.is_gt)
            link(dve.tensor_tensor(cmp_eq[:, t], other, own, ALU.is_equal))
            link(dve.tensor_tensor(cmp_eq[:, t], cmp_eq[:, t], earlier[:], ALU.mult))
            link(dve.tensor_tensor(cmp_gt[:, t], cmp_gt[:, t], cmp_eq[:, t], ALU.add))
            dve.tensor_reduce(rank[:, t, :], cmp_gt[:, t], AX.X, ALU.add)
        link(dve.tensor_reduce(top[:], lg[:], AX.X, ALU.max))
        dve.tensor_scalar(ntop[:], top[:], -1.0, None, ALU.mult).then_inc(top_done, 1)
        dve.tensor_scalar(picked[:], rank[:], 2.0, None, ALU.is_lt).then_inc(picked_done, 1)
        dve.wait_ge(gexp_done, NT)
        dve.wait_ge(picked_done, 1)
        link(dve.tensor_tensor(gexp[:], gexp[:], picked[:], ALU.mult))
        link(dve.tensor_reduce(gsum[:], gexp[:], AX.X, ALU.add))
        link(dve.reciprocal(gsum[:], gsum[:]))
        dve.tensor_tensor(gate[:], gexp[:], bc(gsum[:].unsqueeze(2), [P, NT, E]), ALU.mult)
        dve.wait_ge(pos_ready, 1)
        link(dve.scalar_tensor_tensor(out=slot_of[:].rearrange("p t e -> p (t e)"), in0=ps[:, 1, 0:NT * E], scalar=1.0,
                                      in1=picked[:].rearrange("p t e -> p (t e)"), op0=ALU.add, op1=ALU.mult))
        link(dve.tensor_scalar(slot_of[:], slot_of[:], -1.0, None, ALU.add))
        dve.tensor_copy(counts[:], ps[:, 2, 0:E]).then_inc(route_done, 1)

        def expert_pass(n, e, base):
            for t in range(NT):
                so = slot_of[:, t, bass.ds(e, 1)]
                dve.tensor_scalar(pick[:, t, 0:CAP], slot_no[:, base:base + CAP], so, None, ALU.is_equal)
                ins = dve.tensor_scalar(pick_g[:, t, 0:CAP], slot_no[:, base:base + CAP], so, gate[:, t, bass.ds(e, 1)],
                                        ALU.is_equal, ALU.mult)
            ins.then_inc(e_pick, 1)
            dve.wait_ge(e_xg, n + 1)
            for half in range(2):
                gg = bc(gainT[:, G_FFN + 8 + 4 * half:G_FFN + 12 + 4 * half].unsqueeze(2), [P, 4, P])
                ins = dve.tensor_tensor(xgT[:, 4 * half:4 * half + 4, :], ps[:, 2 + half, :].rearrange("p (c n) -> p c n", c=4), gg, ALU.mult)
            ins.then_inc(e_xg_done, 1)
            for g in range(NG):
                dve.wait_ge(e_silu_done, n * NG + (g + 1))
                if g >= 2:
                    dve.wait_ge(e_T, n * NG + (g - 1))
                dve.tensor_tensor(e_h[:, g % 2, :], e_silu[:, g % 2, :], ps[:, 4 + g % 2, GW:2 * GW], ALU.mult).then_inc(e_act_done, 1)
            dve.wait_ge(e_down, n * NG + NG)
            dve.tensor_copy(ye[:, 512:], ps[:, 1, :]).then_inc(e_y_high, 1)
            for t in range(NT):
                dve.wait_ge(e_scat, n * 2 + (t + 1))
                b = (2, 6)[t]
                dve.tensor_tensor(h[:, t, :], h[:, t, :], banks(b, b + 2), ALU.add).then_inc(e_added, 1)

        dve.wait_ge(route_done, 1)
        with dve.Fori(0, E) as e:
            expert_pass(e, e, 0)
        passes = dve.alloc_register("passes_dve")
        dve.reg_mov(passes, E)
        with dve.Fori(0, E) as e:
            many = dve.value_load(counts[0:1, bass.ds(e, 1)], min_val=0, max_val=T)
            with dve.If(many > CAP):
                expert_pass(dve.snap(passes), e, CAP)
                dve.reg_add(passes, passes, 1)
        norm(5, G_PLE + 8)
        ple(1)

    @block.tensor
    def _(pe):
        def wait_unit(pos, n=None, units=expert_units):
            slot = pos % NSLOT
            if n is None:
                pe.wait_ge(landed[slot], arrivals(order[:pos + 1], slot))
            else:
                pe.wait_ge(landed[slot], n * arrivals(expert_units, slot, FRONT)
                           + (arrivals(order, slot) + arrivals(units[:pos - FRONT + 1], slot, FRONT)))

        pe.wait_ge(ident_ready, 1)
        pe.wait_ge(gains_in, 16 * 7)
        pe.transpose(ps[:, 0, 0:NGAIN], gains_raw[:, :], ident[0:NGAIN, 0:NGAIN]).then_inc(small_T, 1)
        pe.wait_ge(p_inS, 32)
        for i in range(2):
            for c in range(2):
                for t in range(NT):
                    ins = pe.transpose(ps[:, 1 + i, c * T + t * P:c * T + (t + 1) * P], p_in[:, i, t, c * P:(c + 1) * P], ident[:])
            ins.then_inc(small_T, 1)

        def norm(k):
            for t in range(NT):
                pe.wait_ge(hs_done, NT * k + t + 1)
                for half in range(2):
                    for c in range(4):
                        kk = 4 * half + c
                        ins = pe.transpose(ps[:, 4 + 2 * t + half, c * P:(c + 1) * P], hs[:, t, kk * P:(kk + 1) * P], ident[:])
                    ins.then_inc(hT_done, 1)
            pe.wait_ge(hnT_done, 4 * (k + 1))

        norm(0)
        pe.wait_ge(pT_done, 2)
        for u in range(3):
            pos = place[("a_in", u)]
            wait_unit(pos)
            nk = min(3, KD - 3 * u)
            w = view(pos, nk, QL + KVL + ROPE)
            for kk in range(nk):
                k = 3 * u + kk
                for t in range(NT):
                    lhsT = hnT[:, k, t * P:(t + 1) * P]
                    pe.matmul(ps[:, 2 * t, 0:QL], lhsT, w[:, kk, 0:QL], start=(k == 0), stop=(k == KD - 1))
                    ins = pe.matmul(ps[:, 2 * t + 1, 0:KVL + ROPE], lhsT, w[:, kk, QL:], start=(k == 0), stop=(k == KD - 1))
            ins.then_inc(a_ready, 1)
        for t in range(NT):
            pe.wait_ge(lat_scaled, t + 1)
            for c in range(NLAT):
                b = 4 + 2 * t + c // 4
                ins = pe.transpose(ps[:, b, (c % 4) * P:(c % 4 + 1) * P], lat[:, t, c * P:(c + 1) * P], ident[:])
            ins.then_inc(lat_T, 1)
        pe.wait_ge(latT_done, NT)
        pq = [place[("q_up", 0)], place[("q_up", 1)]]
        wait_unit(pq[0])
        wait_unit(pq[1])
        wq = [view(pq[0], 2, HA * QK)[:, 0], view(pq[0], 2, HA * QK)[:, 1], view(pq[1], 1, HA * QK)[:, 0]]
        for t in range(NT):
            for half in range(2):
                for k in range(3):
                    ins = pe.matmul(ps[:, 2 * t + half, 0:4 * QK], latT[:, k, t * P:(t + 1) * P],
                                    wq[k][:, half * 4 * QK:(half + 1) * 4 * QK], start=(k == 0), stop=(k == 2))
        ins.then_inc(q_done, 1)
        pk = place[("kv_up", 0)]
        wait_unit(pk)
        wkv = view(pk, 2, HA * (NOPE + VD))
        for t in range(NT):
            for half in range(2):
                for k in range(2):
                    ins = pe.matmul(ps[:, 4 + 2 * t + half, :], latT[:, 3 + k, t * P:(t + 1) * P],
                                    wkv[:, k, half * 512:(half + 1) * 512], start=(k == 0), stop=(k == 1))
        ins.then_inc(kv_done, 1)
        for w in range(2):
            pe.wait_ge(qk_ready, w + 1)
            for j in range(4):
                for hh in range(2):
                    for t in range(NT):
                        ins = pe.transpose(ps[0:QK, 4 * w + j, (2 * hh + t) * P:(2 * hh + t + 1) * P], qk[:, w, t, 2 * j + hh, :], ident[:])
                ins.then_inc(qk_T, 1)

        def scores(j):
            pe.wait_ge(qT_done, max(2 * (j % 2) + 2, j + 1))
            pe.wait_ge(kT_done, j + 1)
            if j >= 2:
                pe.wait_ge(sc_read, 2 * (j - 2) + 1)
            for hh in range(2):
                hd, b = 2 * j + hh, 2 * (j % 2) + hh
                pe.matmul(ps[:, b, 0:P], qkT[:, 0, hd, 0:P], qkT[:, 1, hd, 0:P], start=True, stop=True)
                ins = pe.matmul(ps[:, b, P:3 * P], qkT[:, 0, hd, P:], qkT[:, 1, hd, :], start=True, stop=True)
            ins.then_inc(sc_ready, 1)

        scores(0)
        scores(1)
        for j in range(4):
            pe.wait_ge(probs_ready, j + 1)
            if j:
                pe.wait_ge(probsT_done, j)
            else:
                pe.wait_ge(kT_done, 4)
            for hh in range(2):
                for c in range(3):
                    ins = pe.transpose(ps[:, 4 + hh, c * P:(c + 1) * P], probs[:, j % 2, hh, c * P:(c + 1) * P], ident[:])
            ins.then_inc(probs_T, 1)
            if j + 2 < 4:
                scores(j + 2)
            pe.wait_ge(probsT_done, j + 1)
            b, col = 6 + j // 2, (j % 2) * T
            for hh in range(2):
                hd = 2 * j + hh
                o = ps[hh * VD:(hh + 1) * VD, b, col:col + T]
                pt = probsT[:, j % 2, hh]
                pe.matmul(o[:, 0:P], va[:, 0, hd, :], pt[:, 0:P], start=True, stop=True)
                pe.matmul(o[:, P:], va[:, 0, hd, :], pt[:, P:2 * P], start=True, stop=False)
                ins = pe.matmul(o[:, P:], va[:, 1, hd, :], pt[:, 2 * P:], start=False, stop=True)
            ins.then_inc(oA_ready, 1)

        def project(name, units, src, nk, ready):
            for u in range(units):
                pos = place[(name, u)]
                wait_unit(pos)
                w = view(pos, 2, D)
                for kk in range(2):
                    k = 2 * u + kk
                    for t in range(NT):
                        for half in range(2):
                            ins = pe.matmul(ps[:, 2 * t + half, :], src[:, k, t * P:(t + 1) * P], w[:, kk, half * 512:(half + 1) * 512],
                                            start=(k == 0), stop=(k == nk - 1))
                ins.then_inc(ready, 1)

        pe.wait_ge(sc_read, 8)
        pe.wait_ge(oTA_done, 2)
        project("a_out", 2, oTA, 4, a_out_ready)

        norm(1)

        def d_gate_up(i):
            g, f = i // 2, i % 2
            pu = [place[("ffn_gu", 2 * g)], place[("ffn_gu", 2 * g + 1)]]
            if f == 0:
                wait_unit(pu[0])
                wait_unit(pu[1])
            if i >= 4:
                pe.wait_ge(d_act_done, i - 3)
            for s in range(2):
                for k in range(KD):
                    w = view(pu[k // 4], 4, 2 * GW)[:, k % 4, s * GW + f * P:s * GW + (f + 1) * P]
                    ins = pe.matmul(ps[:, 4 + i % 4, s * T:(s + 1) * T], w, hnT[:, k, :], start=(k == 0), stop=(k == KD - 1))
            ins.then_inc(d_gu, 1)

        def d_down_part(i):
            g, f = i // 2, i % 2
            pos = place[("ffn_down", g)]
            if f == 0:
                wait_unit(pos)
            pe.wait_ge(d_act_done, i + 1)
            w = view(pos, 2, D)
            for t in range(NT):
                for half in range(2):
                    ins = pe.matmul(ps[:, 2 * t + half, :], d_hT[:, i % 4, t * P:(t + 1) * P], w[:, f, half * 512:(half + 1) * 512],
                                    start=(i == 0), stop=(i == NF - 1))
            ins.then_inc(d_down, 1)

        for i in range(NF + 1):
            if i < NF:
                d_gate_up(i)
            if i:
                if i == 1:
                    pe.wait_ge(h_updated, 2)
                d_down_part(i - 1)

        def ple(i, n=None):
            norm(2 if i == 0 else 5)
            where = place if i == 0 else {k: FRONT + v for k, v in tplace.items()}
            if i == 0:
                pe.wait_ge(h_updated, 4)
            for u in range(4):
                pos = where[(f"ple_gate{i}", u)]
                wait_unit(pos, n, tail)
                w = view(pos, 2, D)
                for kk in range(2):
                    k = 2 * u + kk
                    for t in range(NT):
                        for half in range(2):
                            ins = pe.matmul(ps[:, 2 * t + half, :], hnT[:, k, t * P:(t + 1) * P], w[:, kk, half * 512:(half + 1) * 512],
                                            start=(k == 0), stop=(k == KD - 1))
                ins.then_inc(gate_ready, 1)
            pos = where[(f"ple_up{i}", 0)]
            wait_unit(pos, n, tail)
            w = view(pos, 2, D)
            for t in range(NT):
                for half in range(2):
                    for c in range(2):
                        ins = pe.matmul(ps[:, 4 + 2 * t + half, :], pT[:, i, c, t * P:(t + 1) * P], w[:, c, half * 512:(half + 1) * 512],
                                        start=(c == 0), stop=(c == 1))
            ins.then_inc(up_ready, 1)

        ple(0)
        norm(3)
        pkv = [place[("kv_shared", u)] for u in range(2)]
        pe.wait_ge(sig_done, 2)
        wait_unit(pkv[0])
        wait_unit(pkv[1])
        for c in range(2):
            for k in range(KD):
                ins = pe.matmul(ps[:, 0, c * T:(c + 1) * T], view(pkv[k // 4], 4, 512)[:, k % 4, c * P:(c + 1) * P], hnT2[:, k, :],
                                start=(k == 0), stop=(k == KD - 1))
        ins.then_inc(kv_ready, 1)
        for t in range(NT):
            for k in range(KD):
                ins = pe.matmul(ps[:, 1, t * 256:(t + 1) * 256], hnT2[:, k, t * P:(t + 1) * P], view(pkv[k // 4], 4, 512)[:, k % 4, 256:512],
                                start=(k == 0), stop=(k == KD - 1))
        ins.then_inc(kv_ready, 1)
        pqb = [place[("q_b", u)] for u in range(4)]
        for u in range(4):
            wait_unit(pqb[u])
        for c in range(KD):
            for k in range(KD):
                ins = pe.matmul(ps[:, 4 + c // 2, (c % 2) * T:(c % 2 + 1) * T], view(pqb[k // 2], 2, D)[:, k % 2, c * P:(c + 1) * P],
                                hnT[:, k, :], start=(k == 0), stop=(k == KD - 1))
            if c % 2:
                ins.then_inc(qB_ready, 1)

        def z_scores(g):
            if g:
                pe.wait_ge(zm_done, g)
            for t in range(NT):
                for par in range(2):
                    r = slice(par * HD, (par + 1) * HD)
                    pe.matmul(ps[:, par, t * 256:(t + 1) * 256], kTB[r, g, t * P:(t + 1) * P], qTB[r, 2 * g:2 * g + 2, t * P:(t + 1) * P],
                              start=True, stop=True)
            for par in range(2):
                r = slice(par * HD, (par + 1) * HD)
                ins = pe.matmul(ps[:, 2 + par, 0:256], kTB[r, g, 0:P], qTB[r, 2 * g:2 * g + 2, P:T], start=True, stop=True)
            ins.then_inc(z_ready, 1)

        def key_sums(g):
            pe.wait_ge(sp_done, g + 1)
            s = sp[:, g % 2]
            for par in range(2):
                pe.matmul(ps[:, 4 + par, :], lower[:], s[:, par * 512:(par + 1) * 512], start=True, stop=True)
            for par in range(2):
                pe.matmul(ps[:, 6, par * 256:(par + 1) * 256], lower[:], s[:, 1024 + par * 256:1024 + (par + 1) * 256], start=True, stop=False)
                ins = pe.matmul(ps[:, 6, par * 256:(par + 1) * 256], ones[:], s[:, par * 512 + 256:(par + 1) * 512], start=False, stop=True)
            ins.then_inc(sum_ready, 1)

        def heads(g):
            pe.wait_ge(att_done, g + 1)
            if g:
                pe.wait_ge(oTB_done, g)
            s = sp[:, g % 2]
            vt = [vB[:, t, g * HD:(g + 1) * HD] for t in range(NT)]
            for par in range(2):
                r = slice(par * HD, (par + 1) * HD)
                pe.matmul(ps[r, 7, 0:256], vt[0], s[:, par * 512:par * 512 + 256], start=True, stop=True)
                pe.matmul(ps[r, 7, 256:512], vt[1], s[:, par * 512 + 256:(par + 1) * 512], start=True, stop=False)
                ins = pe.matmul(ps[r, 7, 256:512], vt[0], s[:, 1024 + par * 256:1024 + (par + 1) * 256], start=False, stop=True)
            ins.then_inc(oB_ready, 1)

        pe.wait_ge(kTB_done, 1)
        pe.wait_ge(vB_done, 1)
        pe.wait_ge(qTB_done, 4)
        for g in range(G + 1):
            if g < G:
                z_scores(g)
            if g:
                heads(g - 1)
            if g < G:
                key_sums(g)
        pe.wait_ge(oTB_done, G)
        pe.wait_ge(zm_done, G)
        project("o_b", 4, oTB, KD, o_b_ready)

        norm(4)
        pe.wait_ge(wr_in, 16)
        pe.wait_ge(h_updated, 8)
        for t in range(NT):
            for k in range(KD):
                ins = pe.matmul(ps[:, 0, t * E:(t + 1) * E], hnT[:, k, t * P:(t + 1) * P], wr[:, k, :], start=(k == 0), stop=(k == KD - 1))
        ins.then_inc(lg_ready, 1)
        pe.wait_ge(consts_ready, 1)
        pe.wait_ge(picked_done, 1)
        pe.matmul(ps[:, 1, 0:E], before[:], picked[:, 0, :], start=True, stop=True)
        pe.matmul(ps[:, 1, E:2 * E], before[:], picked[:, 1, :], start=True, stop=False)
        pe.matmul(ps[:, 1, E:2 * E], ones[:], picked[:, 0, :], start=False, stop=True)
        pe.matmul(ps[:, 2, 0:E], ones[:], picked[:, 0, :], start=True, stop=False)
        pe.matmul(ps[:, 2, 0:E], ones[:], picked[:, 1, :], start=False, stop=True).then_inc(pos_ready, 1)
        pe.wait_ge(route_done, 1)

        def expert_pass(n):
            pe.wait_ge(e_pick, n + 1)
            for t in range(NT):
                ins = pe.transpose(ps[0:CAP, 7, t * P:(t + 1) * P], pick_g[:, t, 0:CAP], ident[:])
            ins.then_inc(e_pickT, 1)
            for k in range(KD):
                for t in range(NT):
                    ins = pe.matmul(ps[:, 2 + k // 4, (k % 4) * P:(k % 4) * P + CAP], hs[:, t, k * P:(k + 1) * P], pick[:, t, 0:CAP],
                                    start=(t == 0), stop=(t == NT - 1))
            ins.then_inc(e_xg, 1)
            pe.wait_ge(e_xg_done, n + 1)

            def gu_half(g, u):
                pos = epos("gu", 2 * g + u)
                wait_unit(pos, n)
                w = view(pos, 4, 2 * GW)
                for kk in range(4):
                    k = 4 * u + kk
                    ins = pe.matmul(ps[:, 4 + g % 2, :], xgT[:, k, :], w[:, kk, :], start=(k == 0), stop=(k == KD - 1))
                return ins

            def turn(g):
                pe.wait_ge(e_act_done, n * NG + (g + 1))
                if g:
                    pe.wait_ge(e_hT_done, n * NG + g)
                for f in range(2):
                    ins = pe.transpose(ps[:, 6, f * P:(f + 1) * P], e_h[:, g % 2, f * P:(f + 1) * P], ident[:])
                ins.then_inc(e_T, 1)

            def down(g):
                pos = epos("down", g)
                wait_unit(pos, n)
                pe.wait_ge(e_hT_done, n * NG + (g + 1))
                w = view(pos, 2, D)
                for f in range(2):
                    for half in range(2):
                        ins = pe.matmul(ps[:, half, :], e_hT[:, g % 2, f * P:(f + 1) * P], w[:, f, half * 512:(half + 1) * 512],
                                        start=(g == 0 and f == 0), stop=(g == NG - 1 and f == 1))
                ins.then_inc(e_down, 1)

            for g in range(NG):
                if g >= 2:
                    pe.wait_ge(e_act_done, n * NG + (g - 1))
                gu_half(g, 0).then_inc(e_gu_half, 1)
                if g:
                    turn(g - 1)
                gu_half(g, 1).then_inc(e_gu, 1)
                if g:
                    down(g - 1)
            turn(NG - 1)
            down(NG - 1)
            pe.wait_ge(e_y_low, n + 1)
            pe.wait_ge(e_y_high, n + 1)
            pe.wait_ge(e_pickT_done, n + 1)
            for t in range(NT):
                b = (2, 6)[t]
                for half in range(2):
                    ins = pe.matmul(ps[:, b + half, :], pick_gT[0:CAP, t * P:(t + 1) * P], ye[0:CAP, half * 512:(half + 1) * 512],
                                    start=True, stop=True)
                ins.then_inc(e_scat, 1)

        with pe.Fori(0, E) as e:
            expert_pass(e)
        passes = pe.alloc_register("passes_pe")
        pe.reg_mov(passes, E)
        with pe.Fori(0, E) as e:
            many = pe.value_load(counts[0:1, bass.ds(e, 1)], min_val=0, max_val=T)
            with pe.If(many > CAP):
                expert_pass(pe.snap(passes))
                pe.reg_add(passes, passes, 1)
        n = pe.snap(passes)
        pe.wait_ge(e_added, n * 2)
        ple(1, n)

    es.close()


_INS = ["x", "p", "positions", "norm_attn_a", "w_a_in", "norm_q_lat", "norm_kv_lat", "w_q_up", "w_kv_up", "qk_norm_q", "qk_norm_k",
        "w_a_out", "norm_kv_shared", "w_kv_shared", "norm_attn_b", "w_q_b", "w_o_b", "norm_ffn", "w_ffn_gu", "w_ffn_down",
        "w_router", "w_exp_gu", "w_exp_down", "norm_ple", "w_ple_gate", "w_ple_up"]


def kernel(**inputs):
    import numpy as _np
    import concourse.bacc as _bacc
    from concourse.bass_utils import run_bass_kernel_spmd as _run

    nc = _bacc.Bacc("TRN2", target_bir_lowering=False, num_devices=1)
    arrays, aps = {}, {}
    for name in _INS:
        v = _np.ascontiguousarray(inputs[name])
        arrays[f"in_{name}"] = v
        aps[name] = nc.dram_tensor(f"in_{name}", v.shape, mybir.dt.from_np(v.dtype), kind="ExternalInput").ap()
    out = nc.dram_tensor("out", (1, T, D), F32, kind="ExternalOutput").ap()
    build(nc, aps, out)
    r = _run(nc, [arrays], core_ids=[0])
    return r.results[0]["out"]
```

```python
from contextlib import ExitStack
import math

import numpy as np
import concourse.bass as bass
from concourse import mybir

F32 = mybir.dt.float32
F32R = mybir.dt.float32r
I32 = mybir.dt.int32
ALU = mybir.AluOpType
ACT = mybir.ActivationFunctionType
AX = mybir.AxisListType

P = 128
D = 1024
T = 256
NT = T // P
KD = D // P
EPS = 1e-6

HA, NOPE, ROPE, VD = 8, 64, 32, 64
HALF = ROPE // 2
QK = NOPE + ROPE
QL, KVL = 384, 256
NLAT = (QL + KVL) // P
ROPE_BASE = 10000.0

HB, G, HD = 16, 4, 64

FF = 2816
GW = 256
NG = FF // GW
NF = FF // P
E = 8
CAP = 128

SLOT = 2048
NSLOT = 11
NSPLIT = 3
NEG = -1.0e30

G_ATTN_A, G_FFN, G_PLE, G_KVS, G_ATTN_B, G_LAT = 0, 8, 24, 40, 48, 56
NGAIN = G_LAT + NLAT


def ring_plan():
    order = [("a_in", u) for u in range(3)] + [("q_up", 0), ("q_up", 1), ("kv_up", 0)]
    order += [("a_out", u) for u in range(2)]
    def swiglu(gu, down):
        units = []
        for g in range(NG):
            units += [(gu, 2 * g), (gu, 2 * g + 1)]
            if g:
                units.append((down, g - 1))
        return units + [(down, NG - 1)]

    order += swiglu("ffn_gu", "ffn_down")
    order += [("ple_up0", 0)] + [("ple_gate0", u) for u in range(4)]
    order += [("kv_shared", u) for u in range(2)] + [("q_b", u) for u in range(4)]
    order += [("o_b", u) for u in range(4)]
    front = len(order)
    expert = swiglu("gu", "down")
    assert len(expert) % NSLOT == 0
    tail = [("ple_up1", 0)] + [("ple_gate1", u) for u in range(4)]
    return order, expert, tail, front


def build(nc, a, out):
    order, expert_units, tail, FRONT = ring_plan()
    UNITS = len(expert_units)
    place = {k: i for i, k in enumerate(order)}
    eplace = {k: i for i, k in enumerate(expert_units)}
    tplace = {k: i for i, k in enumerate(tail)}

    es = ExitStack()

    def sb(name, shape, dt=F32, stack=None):
        return (stack or es).enter_context(nc.sbuf_tensor(name, shape, dt))

    def sem(name):
        return es.enter_context(nc.semaphore(name))

    ps = es.enter_context(nc.psum_tensor("ps", [P, 8, 512], F32))

    ring = sb("ring", [P, NSLOT, SLOT])
    h = sb("h", [P, NT, D])
    hs = sb("hs", [P, NT, D])
    hnT = sb("hnT", [P, KD, T])
    junk = sb("junk", [P, D])
    ident = sb("ident", [P, P])
    lower = sb("lower", [P, P])
    before = sb("before", [P, P])
    ones = sb("ones", [P, P])
    slot_no_i = sb("slot_no_i", [P, 2 * P], I32)
    slot_no = sb("slot_no", [P, 2 * P])
    earlier = sb("earlier", [P, E, E])
    gains_raw = sb("gains_raw", [NGAIN, P])
    gainT = sb("gainT", [P, NGAIN])
    pT = sb("pT", [P, 2, 2, T])
    wr = sb("wr", [P, KD, E])
    sumsq = sb("sumsq", [P, 6, NT])
    rstd = sb("rstd", [P, 6, NT])
    mean_sq = sb("mean_sq", [P, 8 * NT, 2 * HA])
    newton = sb("newton", [P, 2 * HA])

    ph = ExitStack()
    p_in = sb("p_in", [P, 2, NT, 256], F32, ph)
    maskA = sb("maskA", [P, 3 * P], F32, ph)
    rope_gain = sb("rope_gain", [P, 2, ROPE], F32, ph)
    nope_gain = sb("nope_gain", [QK, 2], F32, ph)
    rope_tab = sb("rope_tab", [P, 2, 4, NT, HALF], F32, ph)
    pos_i = sb("pos_i", [P, NT], I32, ph)
    pos_f = sb("pos_f", [P, NT], F32, ph)
    invf = sb("invf", [P, HALF], F32, ph)
    ang = sb("ang", [P, NT, HALF], F32, ph)
    trn = sb("trn", [P, 2, NT, HALF], F32, ph)
    red = sb("red", [P, 2, NT, HALF], F32, ph)
    sincos = sb("sincos", [P, 2, NT, HALF], F32, ph)
    lat_sq = sb("lat_sq", [P, NT, 2], F32, ph)
    lat_rstd = sb("lat_rstd", [P, NT, 2], F32, ph)
    lat = sb("lat", [P, NT, QL + KVL], F32, ph)
    latT = sb("latT", [P, NLAT, T], F32, ph)
    kpe = sb("kpe", [P, NT, ROPE], F32, ph)
    kpe_sq = sb("kpe_sq", [P, NT], F32, ph)
    kpe_rot = sb("kpe_rot", [P, NT, ROPE], F32, ph)
    qk = sb("qk", [P, 2, NT, HA, QK], F32, ph)
    va = sb("va", [P, NT, HA, VD], F32, ph)
    qk_sq = sb("qk_sq", [P, NT, 2 * HA], F32, ph)
    qk_rstd = sb("qk_rstd", [P, NT, 2 * HA], F32, ph)
    k_squares = sb("k_squares", [P, HA * NOPE], F32, ph)
    rot = sb("rot", [P, 4, HA, HALF], F32, ph)
    qkT = sb("qkT", [QK, 2, HA, T], F32, ph)
    probs = sb("probs", [P, 4, 2, 3 * P], F32, ph)
    row_max = sb("row_max", [P, 4, 2, 2], F32, ph)
    neg_max = sb("neg_max", [P, 4, 2, 2], F32, ph)
    row_sum = sb("row_sum", [P, 4, 2, 2], F32, ph)
    row_inv = sb("row_inv", [P, 4, 2, 2], F32, ph)
    probsT = sb("probsT", [P, 2, 2, 3 * P], F32, ph)
    oTA = sb("oTA", [P, 4, T], F32, ph)
    ph.close()
    ph = ExitStack()
    split_at = ph.enter_context(nc.sbuf_tensor("w_high", [P, NSPLIT, SLOT], F32R))
    w_high, w_low = split_at, sb("w_low", [P, NSPLIT, SLOT], F32R, ph)
    dense_parts = ExitStack()
    dn_high = sb("dn_high", [P, KD, T], F32R, dense_parts)
    dn_low = sb("dn_low", [P, KD, T], F32R, dense_parts)
    d_silu = sb("d_silu", [P, 2, T], F32, dense_parts)
    d_h = sb("d_h", [P, 2, T], F32, dense_parts)
    d_high = sb("d_high", [P, 2, T], F32R, dense_parts)
    d_low = sb("d_low", [P, 2, T], F32R, dense_parts)
    dense_parts.close()
    moe = ExitStack()
    lg = sb("lg", [P, NT, E], F32, moe)
    cmp_gt = sb("cmp_gt", [P, NT, E, E], F32, moe)
    cmp_eq = sb("cmp_eq", [P, NT, E, E], F32, moe)
    rank = sb("rank", [P, NT, E], F32, moe)
    top = sb("top", [P, NT], F32, moe)
    ntop = sb("ntop", [P, NT], F32, moe)
    picked = sb("picked", [P, NT, E], F32, moe)
    gexp = sb("gexp", [P, NT, E], F32, moe)
    gsum = sb("gsum", [P, NT], F32, moe)
    gate = sb("gate", [P, NT, E], F32, moe)
    slot_of = sb("slot_of", [P, NT, E + 1], F32, moe)
    counts = sb("counts", [P, E + 1], I32, moe)
    pick = sb("pick", [P, NT, P], F32, moe)
    pickT = sb("pickT", [P, T], F32R, moe)
    slot_gate = sb("slot_gate", [P, 1], F32, moe)
    xg_high = sb("xg_high", [P, KD, P], F32R, moe)
    xg_low = sb("xg_low", [P, KD, P], F32R, moe)
    e_silu = sb("e_silu", [P, 2, GW], F32, moe)
    e_h = sb("e_h", [P, 2, GW], F32, moe)
    eh_high = sb("eh_high", [P, 2, GW], F32R, moe)
    eh_low = sb("eh_low", [P, 2, GW], F32R, moe)
    ye_high = sb("ye_high", [P, D], F32R, moe)
    ye_low = sb("ye_low", [P, D], F32R, moe)
    moe.close()
    last = ExitStack()
    hn_high = sb("hn_high", [P, KD, T], F32R, last)
    hn_low = sb("hn_low", [P, KD, T], F32R, last)
    sig1 = sb("sig1", [P, NT, D], F32, last)
    last.close()
    ph.close()
    ph = ExitStack()
    sig0 = sb("sig0", [P, NT, D], F32, ph)
    ph.close()
    sig = (sig0, sig1)
    ph = ExitStack()
    hnT2 = sb("hnT2", [P, KD, T], F32, ph)
    negT = sb("negT", [P, P], F32, ph)
    qTB = sb("qTB", [P, KD, T], F32, ph)
    kTB = sb("kTB", [P, G, T], F32, ph)
    vB = sb("vB", [P, NT, G * HD], F32, ph)
    zm = sb("zm", [P, 3, 1536], F32, ph)
    sp = sb("sp", [P, 3, 1536], F32, ph)
    oTB = sb("oTB", [P, KD, T], F32, ph)
    ph.close()
    x_in = [sem(f"x_in{t}") for t in range(NT)]
    gains_in, qkg_in, pos_in, p_inS, wr_in = map(sem, ("gains_in", "qkg_in", "pos_in", "p_arrived", "wr_in"))
    landed = [sem(f"landed{i}") for i in range(NSLOT)]
    pool_chain, dve_chain, act_chain = map(sem, ("pool_chain", "dve_chain", "act_chain"))
    ident_ready, consts_ready, masks_b_ready = map(sem, ("ident_ready", "consts_ready", "masks_b_ready"))
    gains_T, gains_read, p_T, pT_done = map(sem, ("gains_T", "gains_read", "p_T", "pT_done"))
    sq_done, mean_ready, seed_ready, hs_done, hT_done, hnT_done, h_updated = map(
        sem, ("sq_done", "mean_ready", "seed_ready", "hs_done", "hT_done", "hnT_done", "h_updated"))
    angles_done, trig_done = map(sem, ("angles_done", "trig_done"))
    a_ready, lat_sq_done, lat_scaled, lat_T, latT_done = map(
        sem, ("a_ready", "lat_sq_done", "lat_scaled", "lat_T", "latT_done"))
    q_done, kv_done, kpe_copied, tab_done, q_squared, k_squared, squares_read, qk_ready = map(
        sem, ("q_done", "kv_done", "kpe_copied", "tab_done", "q_squared", "k_squared", "squares_read", "qk_ready"))
    qk_T, qT_done, kT_done = map(sem, ("qk_T", "qT_done", "kT_done"))
    sc_ready, sc_read, exp_done, probs_ready, probs_T, probsT_done, oA_ready, oTA_done, a_out_ready, o_b_ready = map(
        sem, ("sc_ready", "sc_read", "exp_done", "probs_ready", "probs_T", "probsT_done", "oA_ready", "oTA_done", "a_out_ready", "o_b_ready"))
    high_done, low_done = map(sem, ("high_done", "low_done"))
    hn_ready, hn_high_done, hn_low_done = map(sem, ("hn_ready", "hn_high_done", "hn_low_done"))
    d_gu_half, d_gu_first, d_gu, d_silu_done, d_act_done, d_high_done, d_low_done, d_down, d_sum_ready = map(
        sem, ("d_gu_half", "d_gu_first", "d_gu", "d_silu_done", "d_act_done", "d_high_done", "d_low_done", "d_down", "d_sum_ready"))
    gate_ready, gate1_used, up_ready, sig_done = map(sem, ("gate_ready", "gate1_used", "up_ready", "sig_done"))
    k_ready, v_ready, qB_ready, kTB_done, vB_done, qTB_done = map(sem, ("k_ready", "v_ready", "qB_ready", "kTB_done", "vB_done", "qTB_done"))
    z_ready, zm_done, ln_done, sp_done, sum_ready, w_done, att_done, oB_ready, oTB_done = map(
        sem, ("z_ready", "zm_done", "ln_done", "sp_done", "sum_ready", "w_done", "att_done", "oB_ready", "oTB_done"))
    lg_ready, top_found, top_done, gexp_done, picked_done, pos_ready, route_done = map(
        sem, ("lg_ready", "top_found", "top_done", "gexp_done", "picked_done", "pos_ready", "route_done"))
    e_pick, e_pickT, e_pickT_done, e_gate_done, e_xg, e_xg_full, e_xg_high, e_xg_low, e_gu_half, e_gu, e_silu_done, e_act_done = map(
        sem, ("e_pick", "e_pickT", "e_pickT_done", "e_gate_done", "e_xg", "e_xg_full", "e_xg_high", "e_xg_low", "e_gu_half", "e_gu", "e_silu_done", "e_act_done"))
    e_T, e_high_done, e_low_done, e_down, e_y_low, e_y_high, e_scat, e_added = map(
        sem, ("e_T", "e_high_done", "e_low_done", "e_down", "e_y_low", "e_y_high", "e_scat", "e_added"))
    out_sem = sem("out_stored")

    def slot_of_unit(pos):
        return ring[:, pos % NSLOT, :]

    def view(pos, k, n):
        return slot_of_unit(pos)[:, 0:k * n].rearrange("p (k n) -> p k n", k=k)

    def rows(w, k0, k1):
        return w.rearrange("(k p) n -> p k n", p=P)[:, k0:k1, :]

    def gu_rows(w, u):
        g, k0 = u // 2, (u % 2) * 4
        return w.rearrange("(k p) (s n) -> p k s n", p=P, s=2)[:, k0:k0 + 4, :, g * GW:(g + 1) * GW]

    DENSE = place[("ffn_gu", 0)]
    DENSE_END = DENSE + UNITS

    def raw_free(pos):
        if DENSE <= pos < DENSE_END:
            return low_done, pos - DENSE + 1
        return released(*order[pos])

    TWO_LOADS = ("ffn_gu", "gu", "ple_up1", "ple_gate1")

    def arrivals(units, slot, first=0):
        return sum(16 * (2 if name in TWO_LOADS else 1) for i, (name, _) in enumerate(units) if (first + i) % NSLOT == slot)

    def landed_wait(eng, pos, n=None, units=expert_units):
        slot = pos % NSLOT
        if n is None:
            eng.wait_ge(landed[slot], arrivals(order[:pos + 1], slot))
        else:
            eng.wait_ge(landed[slot], n * arrivals(expert_units, slot, FRONT)
                        + (arrivals(order, slot) + arrivals(units[:pos - FRONT + 1], slot, FRONT)))

    def unit_dma(sp_, name, u, pos, e=None):
        src3 = {
            "a_in": (a["w_a_in"][0], 3, QL + KVL + ROPE, KD), "q_up": (a["w_q_up"][0], 2, HA * QK, 3),
            "kv_up": (a["w_kv_up"][0], 2, HA * (NOPE + VD), 2), "a_out": (a["w_a_out"][0], 2, D, 4),
            "ffn_down": (a["w_ffn_down"][0], 2, D, NF), "ple_gate0": (a["w_ple_gate"][0], 2, D, KD),
            "ple_gate1": (a["w_ple_gate"][1], 2, D, KD), "ple_up0": (a["w_ple_up"][0], 2, D, 2),
            "ple_up1": (a["w_ple_up"][1], 2, D, 2), "kv_shared": (a["w_kv_shared"], 4, 2 * G * HD, KD),
            "q_b": (a["w_q_b"][0], 2, D, KD), "o_b": (a["w_o_b"][0], 2, D, KD),
        }
        if name in ("ffn_gu", "gu"):
            w = a["w_ffn_gu"][0] if name == "ffn_gu" else a["w_exp_gu"][0, bass.ds(e, 1)].rearrange("e k n -> (e k) n")
            dst, src = view(pos, 4, 2 * GW), gu_rows(w, u)
            for s in range(2):
                sp_.dma_start(dst[:, :, s * GW:(s + 1) * GW], src[:, :, s, :]).then_inc(landed[pos % NSLOT], 16)
            return
        elif name == "down":
            w = a["w_exp_down"][0, bass.ds(e, 1)].rearrange("e k n -> (e k) n")
            dst, src = view(pos, 2, D), rows(w, 2 * u, 2 * u + 2)
        else:
            w, per, n, kk = src3[name]
            k0, k1 = per * u, min(per * (u + 1), kk)
            dst, src = view(pos, k1 - k0, n), rows(w, k0, k1)
            if name in TWO_LOADS:
                for k in range(2):
                    sp_.dma_start(dst[:, k:k + 1], src[:, k:k + 1]).then_inc(landed[pos % NSLOT], 16)
                return
        sp_.dma_start(dst, src).then_inc(landed[pos % NSLOT], 16)

    def released(name, u):
        return {
            "a_in": (a_ready, NT), "q_up": (q_done, NT), "kv_up": (kv_done, NT), "a_out": (a_out_ready, NT),
            "ffn_gu": (d_gu if u % 2 else d_gu_half, u // 2 + 1), "ffn_down": (d_down, u + 1), "ple_gate0": (gate_ready, NT),
            "ple_up0": (up_ready, NT), "kv_shared": (v_ready, NT), "q_b": (qB_ready, 4), "o_b": (o_b_ready, NT),
            "gu": (e_gu if u % 2 else e_gu_half, u // 2 + 1), "down": (e_down, u + 1),
            "ple_up1": (up_ready, 2 * NT), "ple_gate1": (gate1_used, u + 1),
        }[name]

    def bc(ap, shape):
        return ap.to_broadcast(shape)

    def banks(b0, b1):
        return ps[:, b0:b1, :].rearrange("p b n -> p (b n)")

    block = es.enter_context(nc.Block())

    def r_lat(t):
        return NT + t

    def r_qk(t):
        return 2 * NT + t

    def norm_bank(k, t):
        return 2 if k == 3 and t else 4 + 2 * t

    def r_norm(k, t):
        return NT * k + t + (2 * NT if k else 0)

    G_TURN = 1
    G_PICK = 5

    def epos(name, u):
        return FRONT + eplace[(name, u)]

    @block.sync
    def _(sp_):
        for t in range(NT):
            sp_.dma_start(h[:, t, :], a["x"][0, t * P:(t + 1) * P, :]).then_inc(x_in[t], 16)
        for i, (w, n, r0) in enumerate((
            ("norm_attn_a", 8, G_ATTN_A), ("norm_ffn", 16, G_FFN), ("norm_ple", 16, G_PLE), ("norm_attn_b", 8, G_ATTN_B),
            ("norm_q_lat", 3, G_LAT), ("norm_kv_lat", 2, G_LAT + 3),
        )):
            sp_.dma_start(gains_raw[r0:r0 + n, :], a[w].rearrange("l (k d) -> (l k) d", d=P)).then_inc(gains_in, 16)
        sp_.dma_start(gains_raw[G_KVS:G_KVS + 8, :], a["norm_kv_shared"].rearrange("(k d) -> k d", d=P)).then_inc(gains_in, 16)
        sp_.dma_start(pos_i[:, :], a["positions"].rearrange("b (t p) -> p (b t)", p=P), allow_slow_non_contiguous=True).then_inc(pos_in, 16)
        for u in range(6):
            unit_dma(sp_, *order[u], u)
        for w, gain in enumerate((a["qk_norm_q"], a["qk_norm_k"])):
            sp_.dma_start(rope_gain[:, w, :], gain[:, NOPE:].to_broadcast([P, ROPE])).then_inc(qkg_in, 16)
            sp_.dma_start(nope_gain[0:NOPE, w:w + 1], gain[:, 0:NOPE].rearrange("o d -> d o"), allow_slow_non_contiguous=True).then_inc(qkg_in, 16)
        for i in range(2):
            sp_.dma_start(p_in[:, i], a["p"][i, 0].rearrange("(t p) c -> p t c", p=P)).then_inc(p_inS, 16)
        sp_.dma_start(wr[:, :, :], a["w_router"][0].rearrange("(k p) e -> p k e", p=P)).then_inc(wr_in, 16)
        for pos in range(6, FRONT):
            if pos >= NSLOT:
                sp_.wait_ge(*raw_free(pos - NSLOT))
            unit_dma(sp_, *order[pos], pos)

        def next_loads(n, units, e=None):
            for i, (name, u) in enumerate(units):
                sp_.wait_ge(low_done, n * UNITS + (UNITS + i - NSLOT + 1))
                unit_dma(sp_, name, u, FRONT + i, e)

        for i, (name, u) in enumerate(expert_units):
            if i < NSLOT:
                sp_.wait_ge(*raw_free(FRONT + i - NSLOT))
            else:
                sp_.wait_ge(low_done, UNITS + i - NSLOT + 1)
            unit_dma(sp_, name, u, FRONT + i, 0)
        with sp_.Fori(1, E) as e:
            next_loads(e, expert_units, e)
        sp_.wait_ge(route_done, 1)
        passes = sp_.alloc_register("passes_sp")
        sp_.reg_mov(passes, E)
        largest = sp_.value_load(counts[0:1, E:E + 1], min_val=0, max_val=T)
        with sp_.If(largest > CAP):
            with sp_.Fori(0, E) as e:
                many = sp_.value_load(counts[0:1, bass.ds(e, 1)], min_val=0, max_val=T)
                with sp_.If(many > CAP):
                    next_loads(sp_.snap(passes), expert_units, e)
                    sp_.reg_add(passes, passes, 1)
        next_loads(sp_.snap(passes), tail)
        for t in range(NT):
            sp_.wait_ge(h_updated, 8 + t + 1)
            sp_.dma_start(out[0, t * P:(t + 1) * P, :], h[:, t, :]).then_inc(out_sem, 16)
        sp_.wait_ge(out_sem, 16 * NT)

    @block.gpsimd
    def _(pool):
        chain = [0]

        def link(ins):
            chain[0] += 1
            ins.then_inc(pool_chain, 1)
            pool.wait_ge(pool_chain, chain[0])

        link(pool.memset(ident[:], 0.0))
        pool.affine_select(out=ident[:], in_=ident[:], compare_op=ALU.not_equal, fill=1.0, base=0,
                           pattern=[[-1, P]], channel_multiplier=1).then_inc(ident_ready, 1)
        link(pool.memset(ones[:], 1.0))
        link(pool.affine_select(out=lower[:], in_=ones[:], compare_op=ALU.is_ge, fill=0.0, base=0,
                                pattern=[[-1, P]], channel_multiplier=1))
        link(pool.tensor_scalar(before[:], lower[:], -1.0, 1.0, ALU.mult, ALU.add))
        link(pool.memset(nope_gain[NOPE:, :], 1.0))
        link(pool.memset(maskA[:], 0.0))
        for c in (0, 2):
            link(pool.affine_select(out=maskA[:, c * P:(c + 1) * P], in_=maskA[:, c * P:(c + 1) * P],
                                    compare_op=ALU.is_ge, fill=NEG, base=0, pattern=[[-1, P]], channel_multiplier=1))
        for i in range(HALF):
            f = np.exp(np.float32(np.float32(-math.log(ROPE_BASE)) * np.float32(i) / np.float32(HALF)), dtype=np.float32)
            link(pool.memset(invf[:, i:i + 1], float(f)))
        link(pool.iota(slot_no_i[:], pattern=[[1, 2 * P]], base=0, channel_multiplier=0))
        link(pool.tensor_copy(slot_no[:], slot_no_i[:]))
        link(pool.memset(earlier[:], 1.0))
        pool.affine_select(out=earlier[:], in_=earlier[:], compare_op=ALU.is_ge, fill=0.0, base=-1,
                           pattern=[[1, E], [-1, E]], channel_multiplier=0).then_inc(consts_ready, 1)

        pool.wait_ge(h_updated, 4)
        link(pool.memset(negT[:], 0.0))
        pool.affine_select(out=negT[:], in_=negT[:], compare_op=ALU.is_gt, fill=NEG, base=0,
                           pattern=[[1, P]], channel_multiplier=-1).then_inc(masks_b_ready, 1)

    @block.scalar
    def _(act):
        chain = [0]

        def link(ins):
            chain[0] += 1
            ins.then_inc(act_chain, 1)
            act.wait_ge(act_chain, chain[0])

        def load_ln_exp():
            act.preload_act_table_set("natural_log_exp_and_others")

        def rsqrt_seed(r, dst):
            act.wait_ge(mean_ready, r + 1)
            link(act.activation(dst, mean_sq[:, r, 0:dst.shape[1]], ACT.Ln))
            act.activation(dst, dst, ACT.Exp, scale=-0.5).then_inc(seed_ready, 1)

        def norm_tile(k, t):
            if k == 0:
                act.wait_ge(x_in[t], 16)
            elif k < 5:
                act.wait_ge(h_updated, 2 * (k - 1) + t + 1)
            if NT * k + t:
                act.wait_ge(sq_done, NT * k + t)
            act.activation(junk[:], h[:, t, :], ACT.Square, accum_out=sumsq[:, k, t:t + 1]).then_inc(sq_done, 1)
            rsqrt_seed(r_norm(k, t), rstd[:, k, t:t + 1])

        def norm(k):
            for t in range(NT):
                norm_tile(k, t)

        load_ln_exp()
        norm(0)
        act.wait_ge(angles_done, 1)
        act.activation(sincos[:].rearrange("p s t i -> p (s t i)"), red[:].rearrange("p s t i -> p (s t i)"), ACT.Sin).then_inc(trig_done, 1)
        load_ln_exp()
        for t in range(NT):
            act.wait_ge(a_ready, t + 1)
            if t:
                act.wait_ge(lat_sq_done, 3)
            act.activation(junk[:, 0:QL], ps[:, 2 * t, 0:QL], ACT.Square, accum_out=lat_sq[:, t, 0:1]).then_inc(lat_sq_done, 1)
            act.activation(junk[:, QL:QL + KVL], ps[:, 2 * t + 1, 0:KVL], ACT.Square, accum_out=lat_sq[:, t, 1:2]).then_inc(lat_sq_done, 1)
            act.activation(junk[:, QL + KVL:QL + KVL + ROPE], ps[:, 2 * t + 1, KVL:KVL + ROPE], ACT.Square,
                           accum_out=kpe_sq[:, t:t + 1]).then_inc(lat_sq_done, 1)
            rsqrt_seed(r_lat(t), lat_rstd[:, t, :])
        for i in range(2):
            act.wait_ge(p_T, i + 1)
            act.copy(pT[:, i].rearrange("p c t -> p (c t)"), ps[:, 6 + i, :]).then_inc(pT_done, 1)
        for t in range(NT):
            act.wait_ge(q_done, t + 1)
            act.wait_ge(lat_sq_done, 3 * NT)
            if t:
                act.wait_ge(squares_read, 2 * t)
            act.activation(junk[:, 0:HA * QK].rearrange("p (b c) -> p b c", b=2), ps[:, 2 * t:2 * t + 2, 0:4 * QK], ACT.Square).then_inc(q_squared, 1)
            act.wait_ge(kv_done, t + 1)
            kv = banks(4 + 2 * t, 6 + 2 * t).rearrange("p (h c) -> p h c", c=NOPE + VD)
            act.activation(k_squares[:].rearrange("p (h c) -> p h c", c=NOPE), kv[:, :, 0:NOPE], ACT.Square).then_inc(k_squared, 1)
            act.copy(va[:, t], kv[:, :, NOPE:])
            rsqrt_seed(r_qk(t), qk_rstd[:, t, :])
        act.wait_ge(qkg_in, 64)
        act.wait_ge(consts_ready, 1)
        for t in range(NT):
            act.wait_ge(qk_T, 2 * t + 1)
            for b in range(2):
                act.mul(qkT[:, 0, 4 * b:4 * b + 4, t * P:(t + 1) * P], ps[0:QK, 2 * t + b, :].rearrange("p (h n) -> p h n", h=4), nope_gain[:, 0:1])\
                   .then_inc(qT_done, 1)

        def highs(dst, i):
            for c in range(4):
                act.wait_ge(hn_ready, 4 * i + c + 1)
                t, half = c // 2, c % 2
                act.copy(dst[:, 4 * half:4 * half + 4, t * P:(t + 1) * P], hnT[:, 4 * half:4 * half + 4, t * P:(t + 1) * P]).then_inc(hn_high_done, 1)

        scale = 1.0 / math.sqrt(QK)

        def probs_copy(j):
            act.wait_ge(probs_T, j + 1)
            if j >= 2:
                act.wait_ge(oA_ready, j - 1)
            b = 2 * (j % 2)
            act.copy(probsT[:, j % 2], ps[:, b:b + 2, 0:3 * P]).then_inc(probsT_done, 1)

        def exps(j):
            act.wait_ge(sc_read, 2 * j + 2)
            for hh in range(2):
                for t, (c0, c1) in enumerate(((0, P), (P, 3 * P))):
                    s = probs[:, j, hh, c0:c1]
                    ins = act.activation(s, s, ACT.Exp, bias=neg_max[:, j, t, hh:hh + 1], scale=scale,
                                         accum_out=row_sum[:, j, t, hh:hh + 1])
            ins.then_inc(exp_done, 1)

        def outputs_copy(b):
            act.wait_ge(oA_ready, 2 * b + 2)
            act.copy(oTA[:, 2 * b:2 * b + 2, :].rearrange("p c t -> p (c t)"), ps[:, 4 + b, :]).then_inc(oTA_done, 1)

        exps(0)
        exps(1)
        probs_copy(0)
        exps(2)
        probs_copy(1)
        exps(3)
        probs_copy(2)
        outputs_copy(0)
        probs_copy(3)
        outputs_copy(1)
        norm(1)
        act.preload_act_table(ACT.Silu)
        highs(dn_high, 0)

        def high(i, n=None, units=expert_units):
            pos = DENSE + i if n is None else FRONT + i
            landed_wait(act, pos, n, units)
            if n is None:
                if i >= NSPLIT:
                    act.wait_ge(*released(*order[pos - NSPLIT]))
            elif i >= NSPLIT:
                s, count = released(*units[i - NSPLIT])
                if units is tail:
                    act.wait_ge(s, count)
                else:
                    act.wait_ge(s, n * NG + count)
            elif not (isinstance(n, int) and n == 0):
                s, count = released(*expert_units[i - NSPLIT])
                act.wait_ge(s, (n - 1) * NG + count if isinstance(n, int) else n * NG + (count - NG))
            act.copy(w_high[:, i % NSPLIT, :], slot_of_unit(pos)).then_inc(high_done, 1)

        high(0)
        high(1)
        for g in range(NG):
            if g < NG - 1:
                high(3 * g + 2)
            for f in range(2):
                act.wait_ge(d_gu if f else d_gu_first, g + 1)
                if g:
                    act.wait_ge(d_act_done, 2 * g + f - 1)
                act.activation(d_silu[:, f, :], ps[:, 4 + 2 * f, 0:T], ACT.Silu).then_inc(d_silu_done, 1)
            if g < NG - 1:
                high(3 * g + 3)
            for f in range(2):
                act.wait_ge(d_act_done, 2 * g + f + 1)
                if g:
                    act.wait_ge(d_down, g)
                act.copy(d_high[:, f, :], d_h[:, f, :]).then_inc(d_high_done, 1)
            high(3 * g + 4 if g < NG - 1 else UNITS - 1)
        load_ln_exp()
        norm(2)
        act.preload_act_table(ACT.Sigmoid)

        def sigmoid(i, t):
            act.wait_ge(gate_ready, 2 * i + t + 1)
            act.activation(sig[i][:, t, :], banks(4 + 2 * t, 6 + 2 * t), ACT.Sigmoid).then_inc(sig_done, 1)

        for t in range(NT):
            sigmoid(0, t)
            load_ln_exp()
            norm_tile(3, t)
            if t == 0:
                act.preload_act_table(ACT.Sigmoid)
        act.wait_ge(v_ready, NT)
        act.copy(vB[:].rearrange("p t d -> p (t d)"), ps[:, 1, :]).then_inc(vB_done, 1)
        for b in range(4):
            act.wait_ge(qB_ready, b + 1)
            act.mul(qTB[:, 2 * b:2 * b + 2, :].rearrange("p c t -> p (c t)"), ps[:, 4 + b, :], HD ** -0.5).then_inc(qTB_done, 1)

        def soft(g):
            act.wait_ge(zm_done, g + 1)
            if g >= 3:
                act.wait_ge(oB_ready, g - 2)
            link(act.activation(sp[:, g % 3], zm[:, g % 3], ACT.Abs))
            link(act.activation(sp[:, g % 3], sp[:, g % 3], ACT.Exp, scale=-1.0))
            act.activation(sp[:, g % 3], sp[:, g % 3], ACT.Ln, bias=1.0).then_inc(ln_done, 1)

        def weights_of(g):
            act.wait_ge(w_done, g + 1)
            act.activation(sp[:, g % 3], zm[:, g % 3], ACT.Exp).then_inc(att_done, 1)

        for step in range(G + 2):
            if step >= 2:
                weights_of(step - 2)
            if step < G:
                soft(step)
        act.wait_ge(oB_ready, G)
        high(0, 0)
        high(1, 0)
        norm(4)
        for t in range(NT):
            act.wait_ge(top_done, t + 1)
            act.activation(gexp[:, t, :], lg[:, t, :], ACT.Exp, bias=ntop[:, t:t + 1]).then_inc(gexp_done, 1)

        def xg_high_part(k, half):
            act.wait_ge(e_xg_full, k * 2 + (half + 1))
            act.copy(xg_high[:, 4 * half:4 * half + 4, :], junk[:, half * 512:(half + 1) * 512].rearrange("p (k n) -> p k n", k=4))\
               .then_inc(e_xg_high, 1)

        def expert_pass(n, upcoming):
            for g in range(NG):
                if g:
                    turned_high(n, g - 1)
                high(3 * g + 2, n)
                act.wait_ge(e_gu, n * NG + (g + 1))
                if g >= 2:
                    act.wait_ge(e_act_done, n * NG + (g - 1))
                act.activation(e_silu[:, g % 2, :], ps[:, 4 + g % 2, 0:GW], ACT.Silu).then_inc(e_silu_done, 1)
                if g < NG - 1:
                    high(3 * g + 3, n)
                    high(3 * g + 4, n)
                if g == G_TURN:
                    act.wait_ge(e_pickT, n + 1)
                    act.copy(pickT[:, :], ps[:, 7, 0:T]).then_inc(e_pickT_done, 1)
            turned_high(n, NG - 1)
            high(0, n + 1)
            high(1, n + 1)
            if upcoming is not None:
                xg_high_part(upcoming, 0)
            act.wait_ge(e_down, n * NG + NG)
            act.wait_ge(e_gate_done, n + 1)
            for half in range(2):
                act.mul(ye_high[:, half * 512:(half + 1) * 512], ps[:, half, :], slot_gate[:, 0:1]).then_inc(e_y_high, 1)
            if upcoming is not None:
                xg_high_part(upcoming, 1)

        def turned_high(n, g):
            act.wait_ge(e_T, n * NG + (g + 1))
            if g >= 2:
                act.wait_ge(e_down, n * NG + (g - 1))
            act.copy(eh_high[:, g % 2, :], ps[:, 6, 0:GW]).then_inc(e_high_done, 1)

        act.preload_act_table(ACT.Silu)
        for half in range(2):
            xg_high_part(0, half)
        with act.Fori(0, E) as e:
            expert_pass(e, e + 1)
        act.wait_ge(route_done, 1)
        passes = act.alloc_register("passes_act")
        act.reg_mov(passes, E)
        largest = act.value_load(counts[0:1, E:E + 1], min_val=0, max_val=T)
        with act.If(largest > CAP):
            with act.Fori(0, E) as e:
                many = act.value_load(counts[0:1, bass.ds(e, 1)], min_val=0, max_val=T)
                with act.If(many > CAP):
                    n = act.snap(passes)
                    for half in range(2):
                        xg_high_part(n + 1, half)
                    expert_pass(n, None)
                    act.reg_add(passes, passes, 1)
        n = act.snap(passes)
        load_ln_exp()
        for t in range(NT):
            act.wait_ge(e_added, n * 2 - (1 - t))
            norm_tile(5, t)
        highs(hn_high, 1)
        for i in range(2, 5):
            high(i, n, tail)
        act.preload_act_table(ACT.Sigmoid)
        for t in range(NT):
            sigmoid(1, t)

    @block.vector
    def _(dve):
        chain = [0]

        def link(ins):
            chain[0] += 1
            ins.then_inc(dve_chain, 1)
            dve.wait_ge(dve_chain, chain[0])

        dve.wait_ge(pos_in, 16)
        dve.wait_ge(consts_ready, 1)
        link(dve.tensor_copy(pos_f[:], pos_i[:]))
        for t in range(NT):
            link(dve.tensor_scalar(ang[:, t, :], invf[:], pos_f[:, t:t + 1], None, ALU.mult))
        PI1, PI2 = 6.28125, float(np.float32(0.0019340515136718750))
        PI3 = float(np.float32(2 * math.pi - PI1 - PI2))
        MAGIC = 1.5 * 2 ** 23
        af = ang[:].rearrange("p t i -> p (t i)")
        for s, quarter in enumerate((0.0, 0.25)):
            n = trn[:, s].rearrange("p t i -> p (t i)")
            r = red[:, s].rearrange("p t i -> p (t i)")
            link(dve.tensor_scalar(n, af, 1.0 / (2 * math.pi), quarter, ALU.mult, ALU.add))
            link(dve.tensor_scalar(n, n, MAGIC, None, ALU.add))
            link(dve.tensor_scalar(n, n, MAGIC, None, ALU.subtract))
            link(dve.scalar_tensor_tensor(out=r, in0=n, scalar=-PI1, in1=af, op0=ALU.mult, op1=ALU.add))
            link(dve.scalar_tensor_tensor(out=r, in0=n, scalar=-PI2, in1=r, op0=ALU.mult, op1=ALU.add))
            link(dve.scalar_tensor_tensor(out=r, in0=n, scalar=-PI3, in1=r, op0=ALU.mult, op1=ALU.add))
            if s:
                link(dve.tensor_scalar(r, r, math.pi / 2, None, ALU.add))
        rf = red[:].rearrange("p s t i -> p (s t i)")
        PIF = 3.1415925
        dve.tensor_scalar(rf, rf, PIF, -PIF, ALU.min, ALU.max).then_inc(angles_done, 1)

        dve.wait_ge(gains_T, 1)
        dve.tensor_copy(gainT[:], ps[:, 0, 0:NGAIN]).then_inc(gains_read, 1)
        dve.wait_ge(gains_read, 1)

        def means(r, parts):
            c = 0
            for src, width in parts:
                n = src.shape[1]
                ins = dve.tensor_scalar(mean_sq[:, r, c:c + n], src, 1.0 / width, EPS, ALU.mult, ALU.add)
                c += n
            ins.then_inc(mean_ready, 1)

        def refine(r, y):
            m, w = mean_sq[:, r, 0:y.shape[1]], newton[:, 0:y.shape[1]]
            dve.wait_ge(seed_ready, r + 1)
            link(dve.tensor_tensor(w, y, y, ALU.mult))
            link(dve.tensor_tensor(w, w, m, ALU.mult))
            link(dve.tensor_scalar(w, w, -0.5, 1.5, ALU.mult, ALU.add))
            link(dve.tensor_tensor(y, y, w, ALU.mult))

        def norm(k, gain, update, dst=hnT, gain2=None, signal=hnT_done, then=None):
            def root(t):
                refine(r_norm(k, t), rstd[:, k, t:t + 1])
                dve.tensor_scalar(hs[:, t, :], h[:, t, :], rstd[:, k, t:t + 1], None, ALU.mult).then_inc(hs_done, 1)

            def mean(t):
                dve.wait_ge(sq_done, NT * k + t + 1)
                means(r_norm(k, t), ((sumsq[:, k, t:t + 1], D),))

            def turned(t):
                for half in range(2):
                    f = 2 * t + half
                    dve.wait_ge(hT_done, 4 * k + f + 1)
                    src = ps[:, norm_bank(k, t) + half, :].rearrange("p (c n) -> p c n", c=4)
                    for d, g in ((dst, gain), (hnT2, gain2)):
                        if g is None:
                            continue
                        gg = bc(gainT[:, g + 4 * half:g + 4 * half + 4].unsqueeze(2), [P, 4, P])
                        ins = dve.tensor_tensor(d[:, 4 * half:4 * half + 4, t * P:(t + 1) * P], src, gg, ALU.mult)
                    ins.then_inc(signal, 1)

            update(0)
            mean(0)
            root(0)
            update(1)
            mean(1)
            turned(0)
            root(1)
            if then is not None:
                then(0)
            turned(1)
            if then is not None:
                then(1)

        def no_update(t):
            pass

        norm(0, G_ATTN_A, no_update)
        dve.wait_ge(qkg_in, 64)
        dve.wait_ge(trig_done, 1)
        for w in range(2):
            for i, (trig, g0) in enumerate(((1, 0), (0, HALF), (1, HALF), (0, 0))):
                ins = dve.tensor_tensor(rope_tab[:, w, i], sincos[:, trig], bc(rope_gain[:, w, g0:g0 + HALF].unsqueeze(1), [P, NT, HALF]), ALU.mult)
        ins.then_inc(tab_done, 1)
        for t in range(NT):
            dve.wait_ge(lat_sq_done, 3 * (t + 1))
            means(r_lat(t), ((lat_sq[:, t, 0:1], QL), (lat_sq[:, t, 1:2], KVL)))
            refine(r_lat(t), lat_rstd[:, t, :])
            dve.tensor_copy(kpe[:, t, :], ps[:, 2 * t + 1, KVL:KVL + ROPE]).then_inc(kpe_copied, 1)
            dve.tensor_scalar(lat[:, t, 0:QL], ps[:, 2 * t, 0:QL], lat_rstd[:, t, 0:1], None, ALU.mult)
            dve.tensor_scalar(lat[:, t, QL:], ps[:, 2 * t + 1, 0:KVL], lat_rstd[:, t, 1:2], None, ALU.mult).then_inc(lat_scaled, 1)
        dve.wait_ge(tab_done, 1)

        def rotate(x1, x2, y1, y2, tab, tmp, shape):
            for i, x in enumerate((x1, x2, x2, x1)):
                ins = dve.tensor_tensor(tmp[i], x, tab[i] if shape is None else bc(tab[i].unsqueeze(1), shape), ALU.mult)
            link(ins)
            dve.tensor_tensor(y1, tmp[0], tmp[1], ALU.subtract)
            return dve.tensor_tensor(y2, tmp[2], tmp[3], ALU.add)

        for t in range(NT):
            dve.wait_ge(lat_T, t + 1)
            dve.tensor_tensor(latT[:, 0:4, t * P:(t + 1) * P], ps[:, 4 + 2 * t, :].rearrange("p (c n) -> p c n", c=4),
                              bc(gainT[:, G_LAT:G_LAT + 4].unsqueeze(2), [P, 4, P]), ALU.mult)
            dve.tensor_scalar(latT[:, 4, t * P:(t + 1) * P], ps[:, 5 + 2 * t, 0:P], gainT[:, G_LAT + 4:G_LAT + 5], None,
                              ALU.mult).then_inc(latT_done, 1)
            dve.wait_ge(kpe_copied, t + 1)
            if t:
                dve.wait_ge(kpe_copied, NT + t)
            rotate(kpe[:, t, 0:HALF], kpe[:, t, HALF:], kpe_rot[:, t, 0:HALF], kpe_rot[:, t, HALF:],
                   [rope_tab[:, 1, i, t] for i in range(4)], [rot[:, i, 0, :] for i in range(4)], None).then_inc(kpe_copied, 1)
        dve.wait_ge(kpe_copied, 2 * NT)
        for t in range(NT):
            dve.wait_ge(q_squared, t + 1)
            dve.tensor_reduce(qk_sq[:, t, 0:HA], junk[:, 0:HA * QK].rearrange("p (h c) -> p h c", c=QK), AX.X, ALU.add).then_inc(squares_read, 1)
            dve.wait_ge(k_squared, t + 1)
            dve.tensor_reduce(qk_sq[:, t, HA:], k_squares[:].rearrange("p (h c) -> p h c", c=NOPE), AX.X, ALU.add).then_inc(squares_read, 1)
            dve.wait_ge(squares_read, 2 * t + 2)
            link(dve.tensor_scalar(qk_sq[:, t, HA:], qk_sq[:, t, HA:], kpe_sq[:, t:t + 1], None, ALU.add))
            means(r_qk(t), ((qk_sq[:, t, :], QK),))
            refine(r_qk(t), qk_rstd[:, t, :])
            q, k = qk[:, 0, t], qk[:, 1, t]
            link(dve.tensor_tensor(q.rearrange("p (b h) c -> p b h c", b=2), ps[:, 2 * t:2 * t + 2, 0:4 * QK].rearrange("p b (h c) -> p b h c", c=QK),
                                   bc(qk_rstd[:, t, 0:HA].rearrange("p (b h) -> p b h", b=2).unsqueeze(3), [P, 2, 4, QK]), ALU.mult))
            x1, x2 = q[:, :, NOPE:NOPE + HALF], q[:, :, NOPE + HALF:]
            rotate(x1, x2, x1, x2, [rope_tab[:, 0, i, t] for i in range(4)], [rot[:, i] for i in range(4)], [P, HA, HALF]).then_inc(qk_ready, 1)
            kv = banks(4 + 2 * t, 6 + 2 * t).rearrange("p (h c) -> p h c", c=NOPE + VD)
            rk = qk_rstd[:, t, HA:].unsqueeze(2)
            dve.tensor_tensor(k[:, :, 0:NOPE], kv[:, :, 0:NOPE], bc(rk, [P, HA, NOPE]), ALU.mult)
            dve.tensor_tensor(k[:, :, NOPE:], bc(kpe_rot[:, t, :].unsqueeze(1), [P, HA, ROPE]), bc(rk, [P, HA, ROPE]), ALU.mult).then_inc(qk_ready, 1)
            if t < NT - 1:
                dve.wait_ge(qk_ready, 2 * t + 1)
        for t in range(NT):
            dve.wait_ge(qk_T, 2 * t + 2)
            for b in range(2):
                dve.tensor_scalar(qkT[:, 1, 4 * b:4 * b + 4, t * P:(t + 1) * P], ps[0:QK, 4 + 2 * t + b, :].rearrange("p (h n) -> p h n", h=4),
                                  nope_gain[:, 1:2], None, ALU.mult).then_inc(kT_done, 1)

        def mask_max(j):
            dve.wait_ge(sc_ready, j + 1)
            b = 2 * j
            s = probs[:, j]
            dve.tensor_tensor(s, ps[:, b:b + 2, 0:3 * P], bc(maskA[:].unsqueeze(1), [P, 2, 3 * P]), ALU.add).then_inc(sc_read, 1)
            dve.wait_ge(sc_read, 2 * j + 1)
            dve.tensor_reduce(row_max[:, j, 0, :], s[:, :, 0:P], AX.X, ALU.max)
            link(dve.tensor_reduce(row_max[:, j, 1, :], s[:, :, P:], AX.X, ALU.max))
            dve.tensor_scalar(neg_max[:, j], row_max[:, j], -1.0 / math.sqrt(QK), None, ALU.mult).then_inc(sc_read, 1)

        def normalise(j):
            dve.wait_ge(exp_done, j + 1)
            link(dve.reciprocal(row_inv[:, j], row_sum[:, j]))
            for hh in range(2):
                for t, (c0, c1) in enumerate(((0, P), (P, 3 * P))):
                    s = probs[:, j, hh, c0:c1]
                    ins = dve.tensor_scalar(s, s, row_inv[:, j, t, hh:hh + 1], None, ALU.mult)
            ins.then_inc(probs_ready, 1)

        for j in range(5):
            if j < 4:
                mask_max(j)
            if j:
                normalise(j - 1)

        def add_to_h(ready):
            def update(t):
                dve.wait_ge(ready, t + 1)
                dve.tensor_tensor(h[:, t, :], h[:, t, :], banks(2 * t, 2 * t + 2), ALU.add).then_inc(h_updated, 1)
            return update

        def low(i, n=None, units=None):
            pos = DENSE + i if n is None else FRONT + i
            dve.wait_ge(high_done, i + 1 if n is None else n * UNITS + (UNITS + i + 1))
            dve.tensor_tensor(w_low[:, i % NSPLIT, :], slot_of_unit(pos), w_high[:, i % NSPLIT, :].bitcast(F32), ALU.subtract)\
               .then_inc(low_done, 1)

        def lows(high_part, dst, i):
            def of_tile(t):
                for half in range(2):
                    dve.wait_ge(hn_high_done, 4 * i + 2 * t + half + 1)
                    at = (slice(None), slice(4 * half, 4 * half + 4), slice(t * P, (t + 1) * P))
                    dve.tensor_tensor(dst[at], hnT[at], high_part[at].bitcast(F32), ALU.subtract).then_inc(hn_low_done, 1)
            return of_tile

        norm(1, G_FFN, add_to_h(a_out_ready), signal=hn_ready, then=lows(dn_high, dn_low, 0))
        low(0)
        low(1)
        for g in range(NG):
            if g < NG - 1:
                low(3 * g + 2)
            for f in range(2):
                dve.wait_ge(d_silu_done, 2 * g + f + 1)
                if g:
                    dve.wait_ge(d_low_done, 2 * g - 1 + f)
                dve.tensor_tensor(d_h[:, f, :], d_silu[:, f, :], ps[:, 5 + 2 * f, 0:T], ALU.mult).then_inc(d_act_done, 1)
            if g < NG - 1:
                low(3 * g + 3)
            for f in range(2):
                dve.wait_ge(d_high_done, 2 * g + f + 1)
                dve.tensor_tensor(d_low[:, f, :], d_h[:, f, :], d_high[:, f, :].bitcast(F32), ALU.subtract).then_inc(d_low_done, 1)
            low(3 * g + 4 if g < NG - 1 else UNITS - 1)
        norm(2, G_PLE, add_to_h(d_sum_ready))

        def ple(i):
            def update(t):
                dve.wait_ge(up_ready, 2 * i + t + 1)
                dve.wait_ge(sig_done, 2 * i + t + 1)
                link(dve.tensor_tensor(sig[i][:, t, :], sig[i][:, t, :], banks(2 * t, 2 * t + 2), ALU.mult))
                dve.tensor_tensor(h[:, t, :], h[:, t, :], sig[i][:, t, :], ALU.add).then_inc(h_updated, 1)
            return update

        norm(3, G_ATTN_B, ple(0), hnT, G_KVS)
        dve.wait_ge(k_ready, NT)
        for g in range(G):
            src = ps[HD * (g % 2):HD * (g % 2) + HD, 0, (g // 2) * T:(g // 2 + 1) * T]
            dve.tensor_copy(kTB[0:HD, g, :], src)
            ins = dve.tensor_copy(kTB[HD:2 * HD, g, :], src)
        ins.then_inc(kTB_done, 1)
        dve.wait_ge(masks_b_ready, 1)

        def mask_z(g):
            dve.wait_ge(z_ready, g + 1)
            if g >= 3:
                dve.wait_ge(att_done, g - 2)
            dve.tensor_tensor(zm[:, g % 3, 0:1024].rearrange("p (b q) -> p b q", q=P), banks(0, 2).rearrange("p (b q) -> p b q", q=P),
                              bc(negT[:].unsqueeze(1), [P, 8, P]), ALU.add)
            dve.tensor_copy(zm[:, g % 3, 1024:].rearrange("p (b q) -> p b q", b=2), ps[:, 2:4, 0:256]).then_inc(zm_done, 1)

        def softplus(g):
            dve.wait_ge(ln_done, g + 1)
            dve.scalar_tensor_tensor(out=sp[:, g % 3], in0=zm[:, g % 3], scalar=0.0, in1=sp[:, g % 3],
                                     op0=ALU.max, op1=ALU.add).then_inc(sp_done, 1)

        def log_weights(g):
            dve.wait_ge(sum_ready, g + 1)
            dve.tensor_tensor(zm[:, g % 3, :], zm[:, g % 3, :], banks(4, 7), ALU.subtract).then_inc(w_done, 1)

        def out_heads(g):
            dve.wait_ge(oB_ready, g + 1)
            for t in range(NT):
                ins = dve.tensor_copy(oTB[:, 2 * g:2 * g + 2, t * P:(t + 1) * P],
                                      ps[:, 7, t * 256:(t + 1) * 256].rearrange("p (c q) -> p c q", c=2))
            ins.then_inc(oTB_done, 1)

        for step in range(G + 2):
            if step >= 2:
                log_weights(step - 2)
            if 1 <= step <= G:
                softplus(step - 1)
            if step < G:
                mask_z(step)
            if step >= 2:
                out_heads(step - 2)
        low(0, 0)
        low(1, 0)
        norm(4, G_FFN + 8, add_to_h(o_b_ready))

        for t in range(NT):
            dve.wait_ge(lg_ready, t + 1)
            link(dve.tensor_copy(lg[:, t, :], ps[:, t, 0:E]))
            dve.tensor_reduce(top[:, t:t + 1], lg[:, t, :], AX.X, ALU.max).then_inc(top_found, 1)
            other = bc(lg[:, t, :].unsqueeze(1), [P, E, E])
            own = bc(lg[:, t, :].unsqueeze(2), [P, E, E])
            dve.tensor_tensor(cmp_gt[:, t], other, own, ALU.is_gt)
            link(dve.tensor_tensor(cmp_eq[:, t], other, own, ALU.is_equal))
            dve.wait_ge(top_found, t + 1)
            dve.tensor_scalar(ntop[:, t:t + 1], top[:, t:t + 1], -1.0, None, ALU.mult).then_inc(top_done, 1)
            link(dve.tensor_tensor(cmp_eq[:, t], cmp_eq[:, t], earlier[:], ALU.mult))
            link(dve.tensor_tensor(cmp_gt[:, t], cmp_gt[:, t], cmp_eq[:, t], ALU.add))
            link(dve.tensor_reduce(rank[:, t, :], cmp_gt[:, t], AX.X, ALU.add))
            dve.tensor_scalar(picked[:, t, :], rank[:, t, :], 2.0, None, ALU.is_lt).then_inc(picked_done, 1)
        dve.wait_ge(gexp_done, NT)
        dve.wait_ge(picked_done, NT)
        link(dve.tensor_tensor(gexp[:], gexp[:], picked[:], ALU.mult))
        link(dve.tensor_reduce(gsum[:], gexp[:], AX.X, ALU.add))
        link(dve.reciprocal(gsum[:], gsum[:]))
        dve.tensor_tensor(gate[:], gexp[:], bc(gsum[:].unsqueeze(2), [P, NT, E]), ALU.mult)
        dve.wait_ge(pos_ready, 1)
        link(dve.memset(slot_of[:], 0.0))
        link(dve.scalar_tensor_tensor(out=slot_of[:, :, 0:E], in0=ps[:, 3, 0:NT * E].rearrange("p (t e) -> p t e", t=NT), scalar=1.0,
                                      in1=picked[:], op0=ALU.add, op1=ALU.mult))
        link(dve.tensor_scalar(slot_of[:], slot_of[:], -1.0, None, ALU.add))
        dve.tensor_reduce(counts[:, E:], ps[:, 2, 0:E], AX.X, ALU.max)
        dve.tensor_copy(counts[:, 0:E], ps[:, 2, 0:E]).then_inc(route_done, 1)

        def picks(e, base):
            for t in range(NT):
                ins = dve.tensor_scalar(pick[:, t, :], slot_no[:, base:base + CAP], slot_of[:, t, bass.ds(e, 1)], None, ALU.is_equal)
            ins.then_inc(e_pick, 1)

        def gained(k, half):
            dve.wait_ge(e_xg, k * 2 + (half + 1))
            gg = bc(gainT[:, G_FFN + 8 + 4 * half:G_FFN + 12 + 4 * half].unsqueeze(2), [P, 4, P])
            dve.tensor_tensor(junk[:, half * 512:(half + 1) * 512].rearrange("p (c n) -> p c n", c=4),
                              ps[:, 2 + half, :].rearrange("p (c n) -> p c n", c=4), gg, ALU.mult).then_inc(e_xg_full, 1)

        def xg_low_part(k, half):
            dve.wait_ge(e_xg_high, k * 2 + (half + 1))
            chunks = slice(4 * half, 4 * half + 4)
            dve.tensor_tensor(xg_low[:, chunks, :], junk[:, half * 512:(half + 1) * 512].rearrange("p (k n) -> p k n", k=4),
                              xg_high[:, chunks, :].bitcast(F32), ALU.subtract).then_inc(e_xg_low, 1)

        def expert_pass(n, e, k):
            for g in range(NG):
                if g:
                    turned_low(n, g - 1)
                low(3 * g + 2, n)
                dve.wait_ge(e_silu_done, n * NG + (g + 1))
                if g >= 2:
                    dve.wait_ge(e_T, n * NG + (g - 1))
                dve.tensor_tensor(e_h[:, g % 2, :], e_silu[:, g % 2, :], ps[:, 4 + g % 2, GW:2 * GW], ALU.mult).then_inc(e_act_done, 1)
                if g < NG - 1:
                    low(3 * g + 3, n)
                    low(3 * g + 4, n)
                if g == G_PICK:
                    dve.wait_ge(e_pickT_done, n + 1)
                    dve.tensor_copy(slot_gate[:], ps[:, 7, bass.ds(e + T, 1)]).then_inc(e_gate_done, 1)
                if g == G_PICK and k is not None:
                    picks(e + 1, 0)
            turned_low(n, NG - 1)
            low(0, n + 1)
            if k is not None:
                gained(k, 0)
                xg_low_part(k, 0)
            for half in range(2):
                cols = slice(half * 512, (half + 1) * 512)
                dve.wait_ge(e_y_high, n * 2 + (half + 1))
                dve.scalar_tensor_tensor(out=ye_low[:, cols], in0=ps[:, half, :], scalar=slot_gate[:, 0:1], in1=ye_high[:, cols].bitcast(F32),
                                         op0=ALU.mult, op1=ALU.subtract).then_inc(e_y_low, 1)
            if k is not None:
                gained(k, 1)
            low(1, n + 1)
            if k is not None:
                xg_low_part(k, 1)
            for t in range(NT):
                dve.wait_ge(e_scat, n * 2 + (t + 1))
                b = (6, 0)[t]
                dve.tensor_tensor(h[:, t, :], h[:, t, :], banks(b, b + 2), ALU.add).then_inc(e_added, 1)

        def turned_low(n, g):
            dve.wait_ge(e_high_done, n * NG + (g + 1))
            dve.tensor_tensor(eh_low[:, g % 2, :], ps[:, 6, 0:GW], eh_high[:, g % 2, :].bitcast(F32), ALU.subtract).then_inc(e_low_done, 1)

        picks(0, 0)
        for half in range(2):
            gained(0, half)
            xg_low_part(0, half)
        dve.wait_ge(route_done, 1)
        with dve.Fori(0, E) as e:
            expert_pass(e, e, e + 1)
        passes = dve.alloc_register("passes_dve")
        dve.reg_mov(passes, E)
        largest = dve.value_load(counts[0:1, E:E + 1], min_val=0, max_val=T)
        with dve.If(largest > CAP):
            with dve.Fori(0, E) as e:
                many = dve.value_load(counts[0:1, bass.ds(e, 1)], min_val=0, max_val=T)
                with dve.If(many > CAP):
                    n = dve.snap(passes)
                    picks(e, CAP)
                    for half in range(2):
                        gained(n + 1, half)
                        xg_low_part(n + 1, half)
                    expert_pass(n, e, None)
                    dve.reg_add(passes, passes, 1)
        n = dve.snap(passes)
        norm(5, G_PLE + 8, no_update, signal=hn_ready, then=lows(hn_high, hn_low, 1))
        for i in range(2, 5):
            low(i, n)
        for t in range(NT):
            ple(1)(t)

    @block.tensor
    def _(pe):
        def wait_unit(pos):
            landed_wait(pe, pos)

        pe.wait_ge(ident_ready, 1)
        pe.wait_ge(gains_in, 16 * 7)
        pe.transpose(ps[:, 0, 0:NGAIN], gains_raw[:, :], ident[0:NGAIN, 0:NGAIN]).then_inc(gains_T, 1)

        def turn_tile(k, t):
            pe.wait_ge(hs_done, NT * k + t + 1)
            for half in range(2):
                for c in range(4):
                    kk = 4 * half + c
                    ins = pe.transpose(ps[:, norm_bank(k, t) + half, c * P:(c + 1) * P], hs[:, t, kk * P:(kk + 1) * P], ident[:])
                ins.then_inc(hT_done, 1)

        def wait_turned(k, t):
            if k in (1, 5):
                pe.wait_ge(hn_low_done, (0 if k == 1 else 4) + 2 * t + 2)
            else:
                pe.wait_ge(hnT_done, 4 * k + 2 * t + 2 - (4 if k > 1 else 0))

        def norm(k):
            for t in range(NT):
                turn_tile(k, t)
            wait_turned(k, NT - 1)

        for t in range(NT):
            turn_tile(0, t)
        pe.wait_ge(gains_read, 1)
        wa = [view(place[("a_in", k // 3)], min(3, KD - k // 3 * 3), QL + KVL + ROPE)[:, k % 3] for k in range(KD)]
        for t in range(NT):
            wait_turned(0, t)
            for k in range(KD):
                if t == 0 and k % 3 == 0:
                    wait_unit(place[("a_in", k // 3)])
                lhsT = hnT[:, k, t * P:(t + 1) * P]
                pe.matmul(ps[:, 2 * t, 0:QL], lhsT, wa[k][:, 0:QL], start=(k == 0), stop=(k == KD - 1))
                ins = pe.matmul(ps[:, 2 * t + 1, 0:KVL + ROPE], lhsT, wa[k][:, QL:], start=(k == 0), stop=(k == KD - 1))
            ins.then_inc(a_ready, 1)
        pe.wait_ge(p_inS, 32)
        for i in range(2):
            for c in range(2):
                for t in range(NT):
                    ins = pe.transpose(ps[:, 6 + i, c * T + t * P:c * T + (t + 1) * P], p_in[:, i, t, c * P:(c + 1) * P], ident[:])
            ins.then_inc(p_T, 1)
        pq = [place[("q_up", 0)], place[("q_up", 1)]]
        pk = place[("kv_up", 0)]
        wq = [view(pq[0], 2, HA * QK)[:, 0], view(pq[0], 2, HA * QK)[:, 1], view(pq[1], 1, HA * QK)[:, 0]]
        wkv = view(pk, 2, HA * (NOPE + VD))
        for t in range(NT):
            pe.wait_ge(lat_scaled, t + 1)
            if t:
                pe.wait_ge(pT_done, 2)
            for c in range(NLAT):
                b = 4 + 2 * t + c // 4
                ins = pe.transpose(ps[:, b, (c % 4) * P:(c % 4 + 1) * P], lat[:, t, c * P:(c + 1) * P], ident[:])
            ins.then_inc(lat_T, 1)
            if t == 0:
                for pos in pq + [pk]:
                    wait_unit(pos)
            pe.wait_ge(latT_done, t + 1)
            for half in range(2):
                for k in range(3):
                    ins = pe.matmul(ps[:, 2 * t + half, 0:4 * QK], latT[:, k, t * P:(t + 1) * P],
                                    wq[k][:, half * 4 * QK:(half + 1) * 4 * QK], start=(k == 0), stop=(k == 2))
            ins.then_inc(q_done, 1)
            for half in range(2):
                for k in range(2):
                    ins = pe.matmul(ps[:, 4 + 2 * t + half, :], latT[:, 3 + k, t * P:(t + 1) * P],
                                    wkv[:, k, half * 512:(half + 1) * 512], start=(k == 0), stop=(k == 1))
            ins.then_inc(kv_done, 1)
        for t in range(NT):
            for w in range(2):
                pe.wait_ge(qk_ready, 2 * t + w + 1)
                for hd in range(HA):
                    ins = pe.transpose(ps[0:QK, 4 * w + 2 * t + hd // 4, (hd % 4) * P:(hd % 4 + 1) * P], qk[:, w, t, hd, :], ident[:])
                ins.then_inc(qk_T, 1)

        def scores(j):
            pe.wait_ge(qT_done, 3 if j == 0 else 4)
            pe.wait_ge(kT_done, 3 if j == 0 else 4)
            for hh in range(2):
                hd, b = 2 * j + hh, 2 * j + hh
                pe.matmul(ps[:, b, 0:P], qkT[:, 0, hd, 0:P], qkT[:, 1, hd, 0:P], start=True, stop=True)
                ins = pe.matmul(ps[:, b, P:3 * P], qkT[:, 0, hd, P:], qkT[:, 1, hd, :], start=True, stop=True)
            ins.then_inc(sc_ready, 1)

        def turn_probs(j):
            pe.wait_ge(probs_ready, j + 1)
            if j >= 2:
                pe.wait_ge(probsT_done, j - 1)
            for hh in range(2):
                for c in range(3):
                    ins = pe.transpose(ps[:, 2 * (j % 2) + hh, c * P:(c + 1) * P], probs[:, j, hh, c * P:(c + 1) * P], ident[:])
            ins.then_inc(probs_T, 1)

        def outputs(j):
            pe.wait_ge(probsT_done, j + 1)
            pe.wait_ge(sc_read, 5)
            b, col = 4 + j // 2, (j % 2) * T
            for hh in range(2):
                hd = 2 * j + hh
                o = ps[hh * VD:(hh + 1) * VD, b, col:col + T]
                pt = probsT[:, j % 2, hh]
                pe.matmul(o[:, 0:P], va[:, 0, hd, :], pt[:, 0:P], start=True, stop=True)
                pe.matmul(o[:, P:], va[:, 0, hd, :], pt[:, P:2 * P], start=True, stop=False)
                ins = pe.matmul(o[:, P:], va[:, 1, hd, :], pt[:, 2 * P:], start=False, stop=True)
            ins.then_inc(oA_ready, 1)

        for j in range(4):
            scores(j)
        turn_probs(0)
        for j in range(1, 4):
            turn_probs(j)
            outputs(j - 1)
        outputs(3)

        def project_tile(name, t, b0, src, nk, ready):
            for k in range(nk):
                pos = place[(name, k // 2)]
                if t == 0 and k % 2 == 0:
                    wait_unit(pos)
                for half in range(2):
                    ins = pe.matmul(ps[:, b0 + half, :], src[:, k, t * P:(t + 1) * P], view(pos, 2, D)[:, k % 2, half * 512:(half + 1) * 512],
                                    start=(k == 0), stop=(k == nk - 1))
            ins.then_inc(ready, 1)

        pe.wait_ge(probsT_done, 4)
        pe.wait_ge(oTA_done, 2)
        for t in range(NT):
            project_tile("a_out", t, 2 * t, oTA, 4, a_out_ready)

        norm(1)

        def passes3(out, high_l, low_l, high_r, low_r, first, last):
            pe.matmul(out, high_l, high_r, start=first, stop=False)
            pe.matmul(out, high_l, low_r, start=False, stop=False)
            return pe.matmul(out, low_l, high_r, start=False, stop=last)

        def parts(i, k, n):
            return [w[:, i % NSPLIT, 0:k * n].rearrange("p (k n) -> p k n", k=k) for w in (w_high, w_low)]

        def d_gate_up(i, u, g):
            pe.wait_ge(low_done, i + 1)
            wh, wl = parts(i, 4, 2 * GW)
            for f in range(2):
                if u == 0 and g:
                    pe.wait_ge(d_act_done, 2 * (g - 1) + f + 1)
                for s in range(2):
                    cols = slice(s * GW + f * P, s * GW + (f + 1) * P)
                    for kk in range(4):
                        k = 4 * u + kk
                        ins = passes3(ps[:, 4 + 2 * f + s, 0:T], wh[:, kk, cols], wl[:, kk, cols], dn_high[:, k, :], dn_low[:, k, :],
                                      k == 0, k == KD - 1)
                if u == 0 and f == 1:
                    ins.then_inc(d_gu_half, 1)
                if u == 1:
                    ins.then_inc(d_gu if f else d_gu_first, 1)

        def d_down_part(i, g):
            pe.wait_ge(low_done, i + 1)
            wh, wl = parts(i, 2, D)
            def product(f, t, last=False):
                tok = slice(t * P, (t + 1) * P)
                for half in range(2):
                    cols = slice(half * 512, (half + 1) * 512)
                    ins = passes3(ps[:, 2 * t + half, :], d_high[:, f, tok], d_low[:, f, tok], wh[:, f, cols], wl[:, f, cols],
                                  g == 0 and f == 0, last)
                return ins

            if g < NG - 1:
                for f in range(2):
                    pe.wait_ge(d_low_done, 2 * g + f + 1)
                    for t in range(NT):
                        ins = product(f, t)
                ins.then_inc(d_down, 1)
            else:
                pe.wait_ge(d_low_done, 2 * NG)
                for t in range(NT):
                    product(0, t)
                    product(1, t, last=True).then_inc(d_sum_ready, 1)

        for i, (name, u) in enumerate(order[DENSE:DENSE_END]):
            if name == "ffn_gu":
                d_gate_up(i, u % 2, u // 2)
            else:
                d_down_part(i, u)

        def ple_up(i, w, t):
            for half in range(2):
                for c in range(2):
                    ins = pe.matmul(ps[:, 2 * t + half, :], pT[:, i, c, t * P:(t + 1) * P], w[:, c, half * 512:(half + 1) * 512],
                                    start=(c == 0), stop=(c == 1))
            ins.then_inc(up_ready, 1)

        wait_unit(place[("ple_up0", 0)])
        for t in range(NT):
            pe.wait_ge(h_updated, 2 + t + 1)
            ple_up(0, view(place[("ple_up0", 0)], 2, D), t)
            turn_tile(2, t)
        for t in range(NT):
            wait_turned(2, t)
            project_tile("ple_gate0", t, 4 + 2 * t, hnT, KD, gate_ready)

        pkv = [place[("kv_shared", u)] for u in range(2)]
        pqb = [place[("q_b", u)] for u in range(4)]
        for t in range(NT):
            turn_tile(3, t)
            wait_turned(3, t)
            tok = slice(t * P, (t + 1) * P)
            for pos in (pkv if t == 0 else ()):
                wait_unit(pos)
            for c in range(2):
                for k in range(KD):
                    ins = pe.matmul(ps[:, 0, c * T + t * P:c * T + (t + 1) * P], view(pkv[k // 4], 4, 512)[:, k % 4, c * P:(c + 1) * P],
                                    hnT2[:, k, tok], start=(k == 0), stop=(k == KD - 1))
            ins.then_inc(k_ready, 1)
            for k in range(KD):
                ins = pe.matmul(ps[:, 1, t * 256:(t + 1) * 256], hnT2[:, k, tok], view(pkv[k // 4], 4, 512)[:, k % 4, 256:512],
                                start=(k == 0), stop=(k == KD - 1))
            ins.then_inc(v_ready, 1)
            for pos in (pqb if t == 0 else ()):
                wait_unit(pos)
            for c in range(KD):
                for k in range(KD):
                    ins = pe.matmul(ps[:, 4 + c // 2, (c % 2) * T + t * P:(c % 2) * T + (t + 1) * P],
                                    view(pqb[k // 2], 2, D)[:, k % 2, c * P:(c + 1) * P], hnT[:, k, tok], start=(k == 0), stop=(k == KD - 1))
                if t and c % 2:
                    ins.then_inc(qB_ready, 1)

        def z_scores(g):
            pe.wait_ge(qTB_done, g + 1)
            if g:
                pe.wait_ge(zm_done, g)
            for t in range(NT):
                for par in range(2):
                    r = slice(par * HD, (par + 1) * HD)
                    pe.matmul(ps[:, par, t * 256:(t + 1) * 256], kTB[r, g, t * P:(t + 1) * P], qTB[r, 2 * g:2 * g + 2, t * P:(t + 1) * P],
                              start=True, stop=True)
            for par in range(2):
                r = slice(par * HD, (par + 1) * HD)
                ins = pe.matmul(ps[:, 2 + par, 0:256], kTB[r, g, 0:P], qTB[r, 2 * g:2 * g + 2, P:T], start=True, stop=True)
            ins.then_inc(z_ready, 1)

        def key_sums(g):
            pe.wait_ge(sp_done, g + 1)
            if g:
                pe.wait_ge(w_done, g)
            else:
                pe.wait_ge(qTB_done, 4)
            s = sp[:, g % 3]
            for par in range(2):
                pe.matmul(ps[:, 4 + par, :], lower[:], s[:, par * 512:(par + 1) * 512], start=True, stop=True)
            for par in range(2):
                pe.matmul(ps[:, 6, par * 256:(par + 1) * 256], lower[:], s[:, 1024 + par * 256:1024 + (par + 1) * 256], start=True, stop=False)
                ins = pe.matmul(ps[:, 6, par * 256:(par + 1) * 256], ones[:], s[:, par * 512 + 256:(par + 1) * 512], start=False, stop=True)
            ins.then_inc(sum_ready, 1)

        def heads(g):
            pe.wait_ge(att_done, g + 1)
            if g:
                pe.wait_ge(oTB_done, g)
            s = sp[:, g % 3]
            vt = [vB[:, t, g * HD:(g + 1) * HD] for t in range(NT)]
            for par in range(2):
                r = slice(par * HD, (par + 1) * HD)
                pe.matmul(ps[r, 7, 0:256], vt[0], s[:, par * 512:par * 512 + 256], start=True, stop=True)
                pe.matmul(ps[r, 7, 256:512], vt[1], s[:, par * 512 + 256:(par + 1) * 512], start=True, stop=False)
                ins = pe.matmul(ps[r, 7, 256:512], vt[0], s[:, 1024 + par * 256:1024 + (par + 1) * 256], start=False, stop=True)
            ins.then_inc(oB_ready, 1)

        pe.wait_ge(kTB_done, 1)
        pe.wait_ge(vB_done, 1)
        for step in range(G + 2):
            if step < G:
                z_scores(step)
            if step >= 2:
                heads(step - 2)
            if 1 <= step <= G:
                key_sums(step - 1)
        pe.wait_ge(oTB_done, G)
        pe.wait_ge(zm_done, G)
        for t in range(NT):
            project_tile("o_b", t, 2 * t, oTB, KD, o_b_ready)

        pe.wait_ge(wr_in, 16)
        for t in range(NT):
            turn_tile(4, t)
            wait_turned(4, t)
            for k in range(KD):
                ins = pe.matmul(ps[:, t, 0:E], hnT[:, k, t * P:(t + 1) * P], wr[:, k, :], start=(k == 0), stop=(k == KD - 1))
            ins.then_inc(lg_ready, 1)
        pe.wait_ge(consts_ready, 1)
        pe.wait_ge(picked_done, NT)
        pe.matmul(ps[:, 3, 0:E], before[:], picked[:, 0, :], start=True, stop=True)
        pe.matmul(ps[:, 3, E:2 * E], before[:], picked[:, 1, :], start=True, stop=False)
        pe.matmul(ps[:, 3, E:2 * E], ones[:], picked[:, 0, :], start=False, stop=True)
        pe.matmul(ps[:, 2, 0:E], ones[:], picked[:, 0, :], start=True, stop=False)
        pe.matmul(ps[:, 2, 0:E], ones[:], picked[:, 1, :], start=False, stop=True).then_inc(pos_ready, 1)
        pe.wait_ge(route_done, 1)

        def gather(k, half):
            pe.wait_ge(e_pick, k + 1)
            for c in range(4 * half, 4 * half + 4):
                for t in range(NT):
                    ins = pe.matmul(ps[:, 2 + half, (c % 4) * P:(c % 4 + 1) * P], hs[:, t, c * P:(c + 1) * P], pick[:, t, :],
                                    start=(t == 0), stop=(t == NT - 1))
            ins.then_inc(e_xg, 1)

        def expert_pass(n, own, upcoming):
            def unit(name, u):
                i = eplace[(name, u)]
                pe.wait_ge(low_done, n * UNITS + (UNITS + i + 1))
                return i

            def gu_half(g, u):
                wh, wl = parts(unit("gu", 2 * g + u), 4, 2 * GW)
                if g == 0:
                    pe.wait_ge(e_xg_low, own * 2 + (u + 1))
                for kk in range(4):
                    k = 4 * u + kk
                    ins = passes3(ps[:, 4 + g % 2, :], xg_high[:, k, :], xg_low[:, k, :], wh[:, kk, :], wl[:, kk, :], k == 0, k == KD - 1)
                return ins

            def turn(g):
                pe.wait_ge(e_act_done, n * NG + (g + 1))
                if g:
                    pe.wait_ge(e_low_done, n * NG + g)
                for f in range(2):
                    ins = pe.transpose(ps[:, 6, f * P:(f + 1) * P], e_h[:, g % 2, f * P:(f + 1) * P], ident[:])
                ins.then_inc(e_T, 1)

            def down(g):
                wh, wl = parts(unit("down", g), 2, D)
                pe.wait_ge(e_low_done, n * NG + (g + 1))
                for f in range(2):
                    cols = slice(f * P, (f + 1) * P)
                    for half in range(2):
                        half_cols = slice(half * 512, (half + 1) * 512)
                        ins = passes3(ps[:, half, :], eh_high[:, g % 2, cols], eh_low[:, g % 2, cols], wh[:, f, half_cols], wl[:, f, half_cols],
                                      g == 0 and f == 0, g == NG - 1 and f == 1)
                ins.then_inc(e_down, 1)

            for g in range(NG):
                if g >= 2:
                    pe.wait_ge(e_act_done, n * NG + (g - 1))
                gu_half(g, 0).then_inc(e_gu_half, 1)
                if g:
                    turn(g - 1)
                gu_half(g, 1).then_inc(e_gu, 1)
                if g:
                    down(g - 1)
                if g == G_TURN:
                    for t in range(NT):
                        pe.transpose(ps[:, 7, t * P:(t + 1) * P], pick[:, t, :], ident[:])
                    for t in range(NT):
                        ins = pe.matmul(ps[:, 7, T:T + E], pick[:, t, :], gate[:, t, :], start=(t == 0), stop=(t == NT - 1))
                    ins.then_inc(e_pickT, 1)
            turn(NG - 1)
            if upcoming is not None:
                gather(upcoming, 0)
            down(NG - 1)
            if upcoming is not None:
                gather(upcoming, 1)
            pe.wait_ge(e_pickT_done, n + 1)
            for half in range(2):
                pe.wait_ge(e_y_low, n * 2 + (half + 1))
                cols = slice(half * 512, (half + 1) * 512)
                for t in range(NT):
                    out_bank, slots = ps[:, (6, 0)[t] + half, :], pickT[:, t * P:(t + 1) * P]
                    pe.matmul(out_bank, slots, ye_high[:, cols], start=True, stop=False)
                    ins = pe.matmul(out_bank, slots, ye_low[:, cols], start=False, stop=True)
                    if half:
                        ins.then_inc(e_scat, 1)

        for half in range(2):
            gather(0, half)
        with pe.Fori(0, E) as e:
            expert_pass(e, e, e + 1)
        passes = pe.alloc_register("passes_pe")
        pe.reg_mov(passes, E)
        largest = pe.value_load(counts[0:1, E:E + 1], min_val=0, max_val=T)
        with pe.If(largest > CAP):
            with pe.Fori(0, E) as e:
                many = pe.value_load(counts[0:1, bass.ds(e, 1)], min_val=0, max_val=T)
                with pe.If(many > CAP):
                    n = pe.snap(passes)
                    for half in range(2):
                        gather(n + 1, half)
                    expert_pass(n, n + 1, None)
                    pe.reg_add(passes, passes, 1)
        n = pe.snap(passes)
        pe.wait_ge(high_done, n * UNITS + (UNITS + 1))
        landed_wait(pe, FRONT, n, tail)
        pe.wait_ge(e_added, n * 2)
        for t in range(NT):
            ple_up(1, view(FRONT, 2, D), t)
            turn_tile(5, t)
        for u in range(4):
            i = tplace[("ple_gate1", u)]
            pe.wait_ge(low_done, n * UNITS + (UNITS + i + 1))
            wh, wl = parts(i, 2, D)
            for t in range(NT):
                if u == 0:
                    wait_turned(5, t)
                tok = slice(t * P, (t + 1) * P)
                for kk in range(2):
                    k = 2 * u + kk
                    for half in range(2):
                        cols = slice(half * 512, (half + 1) * 512)
                        ins = passes3(ps[:, 4 + 2 * t + half, :], hn_high[:, k, tok], hn_low[:, k, tok], wh[:, kk, cols], wl[:, kk, cols],
                                      k == 0, k == KD - 1)
                if u == 3:
                    ins.then_inc(gate_ready, 1)
            if u < 3:
                ins.then_inc(gate1_used, 1)

    es.close()


_INS = ["x", "p", "positions", "norm_attn_a", "w_a_in", "norm_q_lat", "norm_kv_lat", "w_q_up", "w_kv_up", "qk_norm_q", "qk_norm_k",
        "w_a_out", "norm_kv_shared", "w_kv_shared", "norm_attn_b", "w_q_b", "w_o_b", "norm_ffn", "w_ffn_gu", "w_ffn_down",
        "w_router", "w_exp_gu", "w_exp_down", "norm_ple", "w_ple_gate", "w_ple_up"]


def kernel(**inputs):
    import numpy as _np
    import concourse.bacc as _bacc
    from concourse.bass_utils import run_bass_kernel_spmd as _run

    nc = _bacc.Bacc("TRN2", target_bir_lowering=False, num_devices=1)
    arrays, aps = {}, {}
    for name in _INS:
        v = _np.ascontiguousarray(inputs[name])
        arrays[f"in_{name}"] = v
        aps[name] = nc.dram_tensor(f"in_{name}", v.shape, mybir.dt.from_np(v.dtype), kind="ExternalInput").ap()
    out = nc.dram_tensor("out", (1, T, D), F32, kind="ExternalOutput").ap()
    build(nc, aps, out)
    r = _run(nc, [arrays], core_ids=[0])
    return r.results[0]["out"]
```

```python
from contextlib import ExitStack
import math

import numpy as np
import concourse.bass as bass
from concourse import mybir

F32 = mybir.dt.float32
F32R = mybir.dt.float32r
I32 = mybir.dt.int32
ALU = mybir.AluOpType
ACT = mybir.ActivationFunctionType
AX = mybir.AxisListType

P = 128
D = 1024
T = 256
NT = T // P
KD = D // P
EPS = 1e-6

HA, NOPE, ROPE, VD = 8, 64, 32, 64
HALF = ROPE // 2
QK = NOPE + ROPE
QL, KVL = 384, 256
NLAT = (QL + KVL) // P
ROPE_BASE = 10000.0

HB, G, HD = 16, 4, 64

FF = 2816
GW = 256
NG = FF // GW
NF = FF // P
E = 8
CAP = 128

SLOT = 2048
NSLOT = 11
NSPLIT = 3
NEG = -1.0e30

G_ATTN_A, G_FFN, G_PLE, G_KVS, G_ATTN_B, G_LAT = 0, 8, 24, 40, 48, 56
NGAIN = G_LAT + NLAT


def ring_plan():
    order = [("a_in", u) for u in range(3)] + [("q_up", 0), ("q_up", 1), ("kv_up", 0)]
    order += [("a_out", u) for u in range(2)]
    def swiglu(gu, down):
        units = []
        for g in range(NG):
            units += [(gu, 2 * g), (gu, 2 * g + 1)]
            if g:
                units.append((down, g - 1))
        return units + [(down, NG - 1)]

    order += swiglu("ffn_gu", "ffn_down")
    order += [("ple_up0", 0)] + [("ple_gate0", u) for u in range(4)]
    order += [("kv_shared", u) for u in range(2)] + [("q_b", u) for u in range(4)]
    order += [("o_b", u) for u in range(4)]
    front = len(order)
    expert = swiglu("gu", "down")
    assert len(expert) % NSLOT == 0
    tail = [("ple_up1", 0)] + [("ple_gate1", u) for u in range(4)]
    return order, expert, tail, front


def build(nc, a, out):
    order, expert_units, tail, FRONT = ring_plan()
    UNITS = len(expert_units)
    place = {k: i for i, k in enumerate(order)}
    eplace = {k: i for i, k in enumerate(expert_units)}
    tplace = {k: i for i, k in enumerate(tail)}

    es = ExitStack()

    def sb(name, shape, dt=F32, stack=None):
        return (stack or es).enter_context(nc.sbuf_tensor(name, shape, dt))

    def sem(name):
        return es.enter_context(nc.semaphore(name))

    ps = es.enter_context(nc.psum_tensor("ps", [P, 8, 512], F32))

    ring = sb("ring", [P, NSLOT, SLOT])
    h = sb("h", [P, NT, D])
    hs = sb("hs", [P, NT, D])
    hnT = sb("hnT", [P, KD, T])
    junk = sb("junk", [P, D])
    ident = sb("ident", [P, P])
    lower = sb("lower", [P, P])
    before = sb("before", [P, P])
    ones = sb("ones", [P, P])
    slot_no_i = sb("slot_no_i", [P, 2 * P], I32)
    slot_no = sb("slot_no", [P, 2 * P])
    earlier = sb("earlier", [P, E, E])
    gains_raw = sb("gains_raw", [NGAIN, P])
    gainT = sb("gainT", [P, NGAIN])
    pT = sb("pT", [P, 2, 2, T])
    wr = sb("wr", [P, KD, E])
    ffn_gain = sb("ffn_gain", [P, D])
    sumsq = sb("sumsq", [P, 6, NT])
    rstd = sb("rstd", [P, 6, NT])
    mean_sq = sb("mean_sq", [P, 9 * NT, HA])
    newton = sb("newton", [P, HA])

    ph = ExitStack()
    p_in = sb("p_in", [P, 2, NT, 256], F32, ph)
    maskA = sb("maskA", [P, 3 * P], F32, ph)
    rope_gain = sb("rope_gain", [P, 2, ROPE], F32, ph)
    nope_gain = sb("nope_gain", [QK, 2], F32, ph)
    rope_tab = sb("rope_tab", [P, 2, 4, NT, HALF], F32, ph)
    pos_i = sb("pos_i", [P, NT], I32, ph)
    pos_f = sb("pos_f", [P, NT], F32, ph)
    invf = sb("invf", [P, HALF], F32, ph)
    ang = sb("ang", [P, NT, HALF], F32, ph)
    trn = sb("trn", [P, 2, NT, HALF], F32, ph)
    red = sb("red", [P, 2, NT, HALF], F32, ph)
    sincos = sb("sincos", [P, 2, NT, HALF], F32, ph)
    lat_sq = sb("lat_sq", [P, NT, 2], F32, ph)
    lat_rstd = sb("lat_rstd", [P, NT, 2], F32, ph)
    lat = sb("lat", [P, NT, QL + KVL], F32, ph)
    latT = sb("latT", [P, NLAT, T], F32, ph)
    kpe = sb("kpe", [P, NT, ROPE], F32, ph)
    kpe_sq = sb("kpe_sq", [P, NT], F32, ph)
    kpe_rot = sb("kpe_rot", [P, NT, ROPE], F32, ph)
    qk = sb("qk", [P, 2, NT, HA, QK], F32, ph)
    va = sb("va", [P, NT, HA, VD], F32, ph)
    qk_sq = sb("qk_sq", [P, 2, NT, HA], F32, ph)
    qk_rstd = sb("qk_rstd", [P, 2, NT, HA], F32, ph)
    k_squares = sb("k_squares", [P, HA * NOPE], F32, ph)
    rot = sb("rot", [P, 4, HA, HALF], F32, ph)
    qkT = sb("qkT", [QK, 2, HA, T], F32, ph)
    probs = sb("probs", [P, 4, 2, 3 * P], F32, ph)
    row_max = sb("row_max", [P, 4, 2, 2], F32, ph)
    neg_max = sb("neg_max", [P, 4, 2, 2], F32, ph)
    row_sum = sb("row_sum", [P, 4, 2, 2], F32, ph)
    row_inv = sb("row_inv", [P, 4, 2, 2], F32, ph)
    probsT = sb("probsT", [P, 2, 2, 3 * P], F32, ph)
    oTA = sb("oTA", [P, 4, T], F32, ph)
    ph.close()
    ph = ExitStack()
    w_high = sb("w_high", [P, NSPLIT, SLOT], F32R, ph)
    w_low = sb("w_low", [P, NSPLIT, SLOT], F32R, ph)
    dense_parts = ExitStack()
    dn_high = sb("dn_high", [P, KD, T], F32R, dense_parts)
    dn_low = sb("dn_low", [P, KD, T], F32R, dense_parts)
    d_silu = sb("d_silu", [P, 2, T], F32, dense_parts)
    d_h = sb("d_h", [P, 2, T], F32, dense_parts)
    d_high = sb("d_high", [P, 2, T], F32R, dense_parts)
    d_low = sb("d_low", [P, 2, T], F32R, dense_parts)
    dense_parts.close()
    moe = ExitStack()
    lg = sb("lg", [P, NT, E], F32, moe)
    cmp_gt = sb("cmp_gt", [P, NT, E, E], F32, moe)
    cmp_eq = sb("cmp_eq", [P, NT, E, E], F32, moe)
    rank = sb("rank", [P, NT, E], F32, moe)
    top = sb("top", [P, NT], F32, moe)
    ntop = sb("ntop", [P, NT], F32, moe)
    picked = sb("picked", [P, NT, E], F32, moe)
    gexp = sb("gexp", [P, NT, E], F32, moe)
    gsum = sb("gsum", [P, NT], F32, moe)
    gate = sb("gate", [P, NT, E], F32, moe)
    slot_of = sb("slot_of", [P, NT, E + 1], F32, moe)
    counts = sb("counts", [P, E + 1], I32, moe)
    pick = sb("pick", [P, NT, P], F32, moe)
    pickT = sb("pickT", [P, T], F32R, moe)
    slot_gate = sb("slot_gate", [P, 1], F32, moe)
    xg_high = sb("xg_high", [P, KD, P], F32R, moe)
    xg_low = sb("xg_low", [P, KD, P], F32R, moe)
    e_silu = sb("e_silu", [P, 2, GW], F32, moe)
    e_h = sb("e_h", [P, 2, GW], F32, moe)
    eh_high = sb("eh_high", [P, 2, GW], F32R, moe)
    eh_low = sb("eh_low", [P, 2, GW], F32R, moe)
    ye_high = sb("ye_high", [P, D], F32R, moe)
    ye_low = sb("ye_low", [P, D], F32R, moe)
    moe.close()
    last = ExitStack()
    hn_high = sb("hn_high", [P, KD, T], F32R, last)
    hn_low = sb("hn_low", [P, KD, T], F32R, last)
    sig1 = sb("sig1", [P, NT, D], F32, last)
    last.close()
    ph.close()
    ph = ExitStack()
    hnT2 = sb("hnT2", [P, KD, T], F32, ph)
    negT = sb("negT", [P, P], F32, ph)
    qTB = sb("qTB", [P, KD, T], F32, ph)
    kTB = sb("kTB", [P, G, T], F32, ph)
    vB = sb("vB", [P, NT, G * HD], F32, ph)
    gates = ExitStack()
    sig0 = sb("sig0", [P, NT, D], F32, gates)
    gates.close()
    zm = sb("zm", [P, 3, 1536], F32, ph)
    sp = sb("sp", [P, 3, 1536], F32, ph)
    oTB = sb("oTB", [P, KD, T], F32, ph)
    ph.close()
    x_in = [sem(f"x_in{t}") for t in range(NT)]
    gains_in, ffn_gain_in, qkg_in, pos_in, p_inS, wr_in = map(sem, ("gains_in", "ffn_gain_in", "qkg_in", "pos_in", "p_arrived", "wr_in"))
    landed = [sem(f"landed{i}") for i in range(NSLOT)]
    pool_chain, dve_chain, act_chain = map(sem, ("pool_chain", "dve_chain", "act_chain"))
    ident_ready, consts_ready, masks_b_ready = map(sem, ("ident_ready", "consts_ready", "masks_b_ready"))
    gains_T, gains_read, p_T, pT_done = map(sem, ("gains_T", "gains_read", "p_T", "pT_done"))
    sq_done, mean_ready, seed_ready, hs_done, hT_done, hnT_done, h_updated = map(
        sem, ("sq_done", "mean_ready", "seed_ready", "hs_done", "hT_done", "hnT_done", "h_updated"))
    angles_done, trig_done = map(sem, ("angles_done", "trig_done"))
    a_ready, lat_sq_done, lat_scaled, lat_T, latT_done = map(
        sem, ("a_ready", "lat_sq_done", "lat_scaled", "lat_T", "latT_done"))
    q_done, kv_done, kpe_copied, tab_done, q_squared, k_squared, squares_read, qk_ready = map(
        sem, ("q_done", "kv_done", "kpe_copied", "tab_done", "q_squared", "k_squared", "squares_read", "qk_ready"))
    qk_T, qT_done, kT_done, kT_high_done = map(sem, ("qk_T", "qT_done", "kT_done", "kT_high_done"))
    sc_ready, sc_read, exp_done, probs_ready, probs_T, probsT_done, oA_ready, oTA_done, a_out_ready, o_b_ready = map(
        sem, ("sc_ready", "sc_read", "exp_done", "probs_ready", "probs_T", "probsT_done", "oA_ready", "oTA_done", "a_out_ready", "o_b_ready"))
    high_done, low_done = map(sem, ("high_done", "low_done"))
    hn_ready, hn_high_done, hn_low_done = map(sem, ("hn_ready", "hn_high_done", "hn_low_done"))
    d_gu_half, d_gu_first, d_gu, d_silu_done, d_act_done, d_high_done, d_low_done, d_down, d_sum_ready = map(
        sem, ("d_gu_half", "d_gu_first", "d_gu", "d_silu_done", "d_act_done", "d_high_done", "d_low_done", "d_down", "d_sum_ready"))
    gate_ready, gate1_used, up_ready, sig_done = map(sem, ("gate_ready", "gate1_used", "up_ready", "sig_done"))
    k_ready, v_ready, qB_ready, kTB_done, vB_done, qTB_done = map(sem, ("k_ready", "v_ready", "qB_ready", "kTB_done", "vB_done", "qTB_done"))
    z_ready, zm_done, ln_done, sp_done, sum_ready, w_done, att_done, oB_ready, oTB_done = map(
        sem, ("z_ready", "zm_done", "ln_done", "sp_done", "sum_ready", "w_done", "att_done", "oB_ready", "oTB_done"))
    lg_ready, top_found, top_done, gexp_done, picked_done, pos_ready, route_done = map(
        sem, ("lg_ready", "top_found", "top_done", "gexp_done", "picked_done", "pos_ready", "route_done"))
    e_pick, e_pickT, e_pickT_done, e_gate_done, e_xg, e_xg_high, e_xg_low, e_gu_half, e_gu, e_silu_done, e_act_done = map(
        sem, ("e_pick", "e_pickT", "e_pickT_done", "e_gate_done", "e_xg", "e_xg_high", "e_xg_low", "e_gu_half", "e_gu", "e_silu_done", "e_act_done"))
    e_T, e_high_done, e_low_done, e_down, e_y_low, e_y_high, e_scat, e_added = map(
        sem, ("e_T", "e_high_done", "e_low_done", "e_down", "e_y_low", "e_y_high", "e_scat", "e_added"))
    out_sem = sem("out_stored")

    def slot_of_unit(pos):
        return ring[:, pos % NSLOT, :]

    def view(pos, k, n):
        return slot_of_unit(pos)[:, 0:k * n].rearrange("p (k n) -> p k n", k=k)

    def rows(w, k0, k1):
        return w.rearrange("(k p) n -> p k n", p=P)[:, k0:k1, :]

    def gu_rows(w, u):
        g, k0 = u // 2, (u % 2) * 4
        return w.rearrange("(k p) (s n) -> p k s n", p=P, s=2)[:, k0:k0 + 4, :, g * GW:(g + 1) * GW]

    DENSE = place[("ffn_gu", 0)]
    DENSE_END = DENSE + UNITS

    def raw_free(pos):
        if DENSE <= pos < DENSE_END:
            return low_done, pos - DENSE + 1
        return released(*order[pos])

    TWO_LOADS = ("ffn_gu", "gu", "ple_up1", "ple_gate1")

    def arrivals(units, slot, first=0):
        return sum(16 * (2 if name in TWO_LOADS else 1) for i, (name, _) in enumerate(units) if (first + i) % NSLOT == slot)

    def landed_wait(eng, pos, n=None, units=expert_units):
        slot = pos % NSLOT
        if n is None:
            eng.wait_ge(landed[slot], arrivals(order[:pos + 1], slot))
        else:
            eng.wait_ge(landed[slot], n * arrivals(expert_units, slot, FRONT)
                        + (arrivals(order, slot) + arrivals(units[:pos - FRONT + 1], slot, FRONT)))

    def unit_dma(sp_, name, u, pos, e=None):
        src3 = {
            "a_in": (a["w_a_in"][0], 3, QL + KVL + ROPE, KD), "q_up": (a["w_q_up"][0], 2, HA * QK, 3),
            "kv_up": (a["w_kv_up"][0], 2, HA * (NOPE + VD), 2), "a_out": (a["w_a_out"][0], 2, D, 4),
            "ffn_down": (a["w_ffn_down"][0], 2, D, NF), "ple_gate0": (a["w_ple_gate"][0], 2, D, KD),
            "ple_gate1": (a["w_ple_gate"][1], 2, D, KD), "ple_up0": (a["w_ple_up"][0], 2, D, 2),
            "ple_up1": (a["w_ple_up"][1], 2, D, 2), "kv_shared": (a["w_kv_shared"], 4, 2 * G * HD, KD),
            "q_b": (a["w_q_b"][0], 2, D, KD), "o_b": (a["w_o_b"][0], 2, D, KD),
        }
        if name in ("ffn_gu", "gu"):
            w = a["w_ffn_gu"][0] if name == "ffn_gu" else a["w_exp_gu"][0, bass.ds(e, 1)].rearrange("e k n -> (e k) n")
            dst, src = view(pos, 4, 2 * GW), gu_rows(w, u)
            for s in range(2):
                sp_.dma_start(dst[:, :, s * GW:(s + 1) * GW], src[:, :, s, :]).then_inc(landed[pos % NSLOT], 16)
            return
        elif name == "down":
            w = a["w_exp_down"][0, bass.ds(e, 1)].rearrange("e k n -> (e k) n")
            dst, src = view(pos, 2, D), rows(w, 2 * u, 2 * u + 2)
        else:
            w, per, n, kk = src3[name]
            k0, k1 = per * u, min(per * (u + 1), kk)
            dst, src = view(pos, k1 - k0, n), rows(w, k0, k1)
            if name in TWO_LOADS:
                for k in range(2):
                    sp_.dma_start(dst[:, k:k + 1], src[:, k:k + 1]).then_inc(landed[pos % NSLOT], 16)
                return
        sp_.dma_start(dst, src).then_inc(landed[pos % NSLOT], 16)

    def released(name, u):
        return {
            "a_in": (a_ready, NT), "q_up": (q_done, NT), "kv_up": (kv_done, NT), "a_out": (a_out_ready, NT),
            "ffn_gu": (d_gu if u % 2 else d_gu_half, u // 2 + 1), "ffn_down": (d_down, u + 1), "ple_gate0": (gate_ready, NT),
            "ple_up0": (up_ready, NT), "kv_shared": (v_ready, NT), "q_b": (qB_ready, 4), "o_b": (o_b_ready, NT),
            "gu": (e_gu if u % 2 else e_gu_half, u // 2 + 1), "down": (e_down, u + 1),
            "ple_up1": (up_ready, 2 * NT), "ple_gate1": (gate1_used, u + 1),
        }[name]

    def bc(ap, shape):
        return ap.to_broadcast(shape)

    def banks(b0, b1):
        return ps[:, b0:b1, :].rearrange("p b n -> p (b n)")

    block = es.enter_context(nc.Block())

    def r_lat(t):
        return NT + t

    def r_qk(w, t):
        return (2 + w) * NT + t

    def norm_bank(k, t):
        return 2 if k == 3 and t else 4 + 2 * t

    def r_norm(k, t):
        return NT * k + t + (3 * NT if k else 0)

    G_TURN = 1
    G_PICK = 5

    @block.sync
    def _(sp_):
        for t in range(NT):
            sp_.dma_start(h[:, t, :], a["x"][0, t * P:(t + 1) * P, :]).then_inc(x_in[t], 16)
        for i, (w, n, r0) in enumerate((
            ("norm_attn_a", 8, G_ATTN_A), ("norm_ffn", 16, G_FFN), ("norm_ple", 16, G_PLE), ("norm_attn_b", 8, G_ATTN_B),
            ("norm_q_lat", 3, G_LAT), ("norm_kv_lat", 2, G_LAT + 3),
        )):
            sp_.dma_start(gains_raw[r0:r0 + n, :], a[w].rearrange("l (k d) -> (l k) d", d=P)).then_inc(gains_in, 16)
        sp_.dma_start(gains_raw[G_KVS:G_KVS + 8, :], a["norm_kv_shared"].rearrange("(k d) -> k d", d=P)).then_inc(gains_in, 16)
        sp_.dma_start(pos_i[:, :], a["positions"].rearrange("b (t p) -> p (b t)", p=P), allow_slow_non_contiguous=True).then_inc(pos_in, 16)
        for u in range(6):
            unit_dma(sp_, *order[u], u)
        for w, gain in enumerate((a["qk_norm_q"], a["qk_norm_k"])):
            sp_.dma_start(rope_gain[:, w, :], gain[:, NOPE:].to_broadcast([P, ROPE])).then_inc(qkg_in, 16)
            sp_.dma_start(nope_gain[0:NOPE, w:w + 1], gain[:, 0:NOPE].rearrange("o d -> d o"), allow_slow_non_contiguous=True).then_inc(qkg_in, 16)
        for i in range(2):
            sp_.dma_start(p_in[:, i], a["p"][i, 0].rearrange("(t p) c -> p t c", p=P)).then_inc(p_inS, 16)
        sp_.dma_start(ffn_gain[:, :], a["norm_ffn"][1:2, :].to_broadcast([P, D])).then_inc(ffn_gain_in, 16)
        sp_.dma_start(wr[:, :, :], a["w_router"][0].rearrange("(k p) e -> p k e", p=P)).then_inc(wr_in, 16)
        for pos in range(6, FRONT):
            if pos >= NSLOT:
                sp_.wait_ge(*raw_free(pos - NSLOT))
            unit_dma(sp_, *order[pos], pos)

        def next_loads(n, units, e=None):
            for i, (name, u) in enumerate(units):
                sp_.wait_ge(low_done, n * UNITS + (UNITS + i - NSLOT + 1))
                unit_dma(sp_, name, u, FRONT + i, e)

        for i, (name, u) in enumerate(expert_units):
            if i < NSLOT:
                sp_.wait_ge(*raw_free(FRONT + i - NSLOT))
            else:
                sp_.wait_ge(low_done, UNITS + i - NSLOT + 1)
            unit_dma(sp_, name, u, FRONT + i, 0)
        with sp_.Fori(1, E) as e:
            next_loads(e, expert_units, e)
        sp_.wait_ge(route_done, 1)
        passes = sp_.alloc_register("passes_sp")
        sp_.reg_mov(passes, E)
        largest = sp_.value_load(counts[0:1, E:E + 1], min_val=0, max_val=T)
        with sp_.If(largest > CAP):
            with sp_.Fori(0, E) as e:
                many = sp_.value_load(counts[0:1, bass.ds(e, 1)], min_val=0, max_val=T)
                with sp_.If(many > CAP):
                    next_loads(sp_.snap(passes), expert_units, e)
                    sp_.reg_add(passes, passes, 1)
        next_loads(sp_.snap(passes), tail)
        for t in range(NT):
            for half in range(2):
                cols = slice(half * 512, (half + 1) * 512)
                sp_.wait_ge(h_updated, 8 + 2 * t + half + 1)
                sp_.dma_start(out[0, t * P:(t + 1) * P, cols], h[:, t, cols]).then_inc(out_sem, 16)
        sp_.wait_ge(out_sem, 16 * 2 * NT)

    @block.gpsimd
    def _(pool):
        chain = [0]

        def link(ins):
            chain[0] += 1
            ins.then_inc(pool_chain, 1)
            pool.wait_ge(pool_chain, chain[0])

        link(pool.memset(ident[:], 0.0))
        pool.affine_select(out=ident[:], in_=ident[:], compare_op=ALU.not_equal, fill=1.0, base=0,
                           pattern=[[-1, P]], channel_multiplier=1).then_inc(ident_ready, 1)
        link(pool.memset(ones[:], 1.0))
        link(pool.affine_select(out=lower[:], in_=ones[:], compare_op=ALU.is_ge, fill=0.0, base=0,
                                pattern=[[-1, P]], channel_multiplier=1))
        link(pool.tensor_scalar(before[:], lower[:], -1.0, 1.0, ALU.mult, ALU.add))
        link(pool.memset(nope_gain[NOPE:, :], 1.0))
        link(pool.memset(maskA[:], 0.0))
        for c in (0, 2):
            link(pool.affine_select(out=maskA[:, c * P:(c + 1) * P], in_=maskA[:, c * P:(c + 1) * P],
                                    compare_op=ALU.is_ge, fill=NEG, base=0, pattern=[[-1, P]], channel_multiplier=1))
        for i in range(HALF):
            f = np.exp(np.float32(np.float32(-math.log(ROPE_BASE)) * np.float32(i) / np.float32(HALF)), dtype=np.float32)
            link(pool.memset(invf[:, i:i + 1], float(f)))
        link(pool.iota(slot_no_i[:], pattern=[[1, 2 * P]], base=0, channel_multiplier=0))
        link(pool.tensor_copy(slot_no[:], slot_no_i[:]))
        link(pool.memset(earlier[:], 1.0))
        pool.affine_select(out=earlier[:], in_=earlier[:], compare_op=ALU.is_ge, fill=0.0, base=-1,
                           pattern=[[1, E], [-1, E]], channel_multiplier=0).then_inc(consts_ready, 1)

        pool.wait_ge(h_updated, 4)
        link(pool.memset(negT[:], 0.0))
        pool.affine_select(out=negT[:], in_=negT[:], compare_op=ALU.is_gt, fill=NEG, base=0,
                           pattern=[[1, P]], channel_multiplier=-1).then_inc(masks_b_ready, 1)

    @block.scalar
    def _(act):
        chain = [0]

        def link(ins):
            chain[0] += 1
            ins.then_inc(act_chain, 1)
            act.wait_ge(act_chain, chain[0])

        def load_ln_exp():
            act.preload_act_table_set("natural_log_exp_and_others")

        def rsqrt_seed(r, dst):
            act.wait_ge(mean_ready, r + 1)
            link(act.activation(dst, mean_sq[:, r, 0:dst.shape[1]], ACT.Ln))
            act.activation(dst, dst, ACT.Exp, scale=-0.5).then_inc(seed_ready, 1)

        def norm_tile(k, t):
            if k == 0:
                act.wait_ge(x_in[t], 16)
            elif k < 5:
                act.wait_ge(h_updated, 2 * (k - 1) + t + 1)
            if NT * k + t:
                act.wait_ge(sq_done, NT * k + t)
            act.activation(junk[:], h[:, t, :], ACT.Square, accum_out=sumsq[:, k, t:t + 1]).then_inc(sq_done, 1)
            rsqrt_seed(r_norm(k, t), rstd[:, k, t:t + 1])

        def norm(k):
            for t in range(NT):
                norm_tile(k, t)

        load_ln_exp()
        norm(0)
        act.wait_ge(angles_done, 1)
        act.activation(sincos[:].rearrange("p s t i -> p (s t i)"), red[:].rearrange("p s t i -> p (s t i)"), ACT.Sin).then_inc(trig_done, 1)
        load_ln_exp()
        for t in range(NT):
            act.wait_ge(a_ready, t + 1)
            if t:
                act.wait_ge(lat_sq_done, 3)
            act.activation(junk[:, 0:QL], ps[:, 2 * t, 0:QL], ACT.Square, accum_out=lat_sq[:, t, 0:1]).then_inc(lat_sq_done, 1)
            act.activation(junk[:, QL:QL + KVL], ps[:, 2 * t + 1, 0:KVL], ACT.Square, accum_out=lat_sq[:, t, 1:2]).then_inc(lat_sq_done, 1)
            act.activation(junk[:, QL + KVL:QL + KVL + ROPE], ps[:, 2 * t + 1, KVL:KVL + ROPE], ACT.Square,
                           accum_out=kpe_sq[:, t:t + 1]).then_inc(lat_sq_done, 1)
            rsqrt_seed(r_lat(t), lat_rstd[:, t, :])
        for i in range(2):
            act.wait_ge(p_T, i + 1)
            act.copy(pT[:, i].rearrange("p c t -> p (c t)"), ps[:, 6 + i, :]).then_inc(pT_done, 1)
        for t in range(NT):
            act.wait_ge(q_done, t + 1)
            act.wait_ge(lat_sq_done, 3 * NT)
            if t:
                act.wait_ge(squares_read, t)
            act.activation(junk[:, 0:HA * QK].rearrange("p (b c) -> p b c", b=2), ps[:, 2 * t:2 * t + 2, 0:4 * QK], ACT.Square).then_inc(q_squared, 1)
            rsqrt_seed(r_qk(0, t), qk_rstd[:, 0, t, :])
        act.wait_ge(qkg_in, 64)
        act.wait_ge(consts_ready, 1)

        def turned_queries(t):
            act.wait_ge(qk_T, t + 1)
            for b in range(2):
                act.mul(qkT[:, 0, 4 * b:4 * b + 4, t * P:(t + 1) * P], ps[0:QK, 2 * t + b, :].rearrange("p (h n) -> p h n", h=4), nope_gain[:, 0:1])\
                   .then_inc(qT_done, 1)

        for t in range(NT):
            act.wait_ge(kv_done, t + 1)
            if t:
                act.wait_ge(squares_read, NT + t)
            kv = banks(4 + 2 * t, 6 + 2 * t).rearrange("p (h c) -> p h c", c=NOPE + VD)
            act.activation(k_squares[:].rearrange("p (h c) -> p h c", c=NOPE), kv[:, :, 0:NOPE], ACT.Square).then_inc(k_squared, 1)
            act.copy(va[:, t], kv[:, :, NOPE:])
            rsqrt_seed(r_qk(1, t), qk_rstd[:, 1, t, :])
            turned_queries(t)
        for t in range(NT):
            act.wait_ge(qk_T, NT + t + 1)
            act.mul(qkT[:, 1, 4:8, t * P:(t + 1) * P], ps[0:QK, 5 + 2 * t, :].rearrange("p (h n) -> p h n", h=4), nope_gain[:, 1:2]).then_inc(kT_high_done, 1)

        def highs(dst, i):
            for c in range(4):
                act.wait_ge(hn_ready, 4 * i + c + 1)
                t, half = c // 2, c % 2
                act.copy(dst[:, 4 * half:4 * half + 4, t * P:(t + 1) * P], hnT[:, 4 * half:4 * half + 4, t * P:(t + 1) * P]).then_inc(hn_high_done, 1)

        scale = 1.0 / math.sqrt(QK)

        def probs_copy(j):
            act.wait_ge(probs_T, j + 1)
            if j >= 2:
                act.wait_ge(oA_ready, j - 1)
            b = 2 * (j % 2)
            act.copy(probsT[:, j % 2], ps[:, b:b + 2, 0:3 * P]).then_inc(probsT_done, 1)

        def exps(j):
            act.wait_ge(sc_read, 2 * j + 2)
            for hh in range(2):
                for t, (c0, c1) in enumerate(((0, P), (P, 3 * P))):
                    s = probs[:, j, hh, c0:c1]
                    ins = act.activation(s, s, ACT.Exp, bias=neg_max[:, j, t, hh:hh + 1], scale=scale,
                                         accum_out=row_sum[:, j, t, hh:hh + 1])
            ins.then_inc(exp_done, 1)

        def outputs_copy(b):
            act.wait_ge(oA_ready, 2 * b + 2)
            act.copy(oTA[:, 2 * b:2 * b + 2, :].rearrange("p c t -> p (c t)"), ps[:, 4 + b, :]).then_inc(oTA_done, 1)

        def high(i, n=None, units=expert_units):
            pos = DENSE + i if n is None else FRONT + i
            landed_wait(act, pos, n, units)
            if n is None:
                if i >= NSPLIT:
                    act.wait_ge(*released(*order[pos - NSPLIT]))
            elif i >= NSPLIT:
                s, count = released(*units[i - NSPLIT])
                if units is tail:
                    act.wait_ge(s, count)
                else:
                    act.wait_ge(s, n * NG + count)
            elif not (isinstance(n, int) and n == 0):
                s, count = released(*expert_units[i - NSPLIT])
                act.wait_ge(s, (n - 1) * NG + count if isinstance(n, int) else n * NG + (count - NG))
            act.copy(w_high[:, i % NSPLIT, :], slot_of_unit(pos)).then_inc(high_done, 1)

        exps(0)
        exps(1)
        probs_copy(0)
        exps(2)
        probs_copy(1)
        exps(3)
        probs_copy(2)
        outputs_copy(0)
        probs_copy(3)
        outputs_copy(1)
        act.wait_ge(oA_ready, 4)
        for i in range(3):
            high(i)
        norm(1)
        act.preload_act_table(ACT.Silu)
        highs(dn_high, 0)

        for g in range(NG):
            if g:
                high(3 * g + 2)
            for f in range(2):
                act.wait_ge(d_gu if f else d_gu_first, g + 1)
                if g:
                    act.wait_ge(d_act_done, 2 * g + f - 1)
                act.activation(d_silu[:, f, :], ps[:, 4 + 2 * f, 0:T], ACT.Silu).then_inc(d_silu_done, 1)
            if g < NG - 1:
                high(3 * g + 3)
            for f in range(2):
                act.wait_ge(d_act_done, 2 * g + f + 1)
                if g:
                    act.wait_ge(d_down, g)
                act.copy(d_high[:, f, :], d_h[:, f, :]).then_inc(d_high_done, 1)
            if g < NG - 1:
                high(3 * g + 4)
        load_ln_exp()
        norm(2)
        act.preload_act_table(ACT.Sigmoid)

        for t in range(NT):
            act.wait_ge(gate_ready, t + 1)
            act.activation(sig0[:, t, :], banks(4 + 2 * t, 6 + 2 * t), ACT.Sigmoid).then_inc(sig_done, 1)
            load_ln_exp()
            norm_tile(3, t)
            if t == 0:
                act.preload_act_table(ACT.Sigmoid)
        act.wait_ge(v_ready, NT)
        act.copy(vB[:].rearrange("p t d -> p (t d)"), ps[:, 1, :]).then_inc(vB_done, 1)

        def queries_copy(b):
            act.wait_ge(qB_ready, b + 1)
            act.mul(qTB[:, 2 * b:2 * b + 2, :].rearrange("p c t -> p (c t)"), ps[:, 4 + b, :], HD ** -0.5).then_inc(qTB_done, 1)

        def soft(g):
            act.wait_ge(zm_done, g + 1)
            if g >= 3:
                act.wait_ge(oB_ready, g - 2)
            link(act.activation(sp[:, g % 3], zm[:, g % 3], ACT.Abs))
            link(act.activation(sp[:, g % 3], sp[:, g % 3], ACT.Exp, scale=-1.0))
            act.activation(sp[:, g % 3], sp[:, g % 3], ACT.Ln, bias=1.0).then_inc(ln_done, 1)

        def weights_of(g):
            act.wait_ge(w_done, g + 1)
            act.activation(sp[:, g % 3], zm[:, g % 3], ACT.Exp).then_inc(att_done, 1)

        queries_copy(0)
        queries_copy(1)
        soft(0)
        queries_copy(2)
        queries_copy(3)
        for step in range(1, G + 2):
            if step >= 2:
                weights_of(step - 2)
            if step < G:
                soft(step)
        act.wait_ge(oB_ready, G)
        for i in range(NSPLIT):
            high(i, 0)
        norm(4)
        for t in range(NT):
            act.wait_ge(top_done, t + 1)
            act.activation(gexp[:, t, :], lg[:, t, :], ACT.Exp, bias=ntop[:, t:t + 1]).then_inc(gexp_done, 1)

        def xg_high_part(k, half):
            act.wait_ge(e_xg, k * 2 + (half + 1))
            act.copy(xg_high[:, 4 * half:4 * half + 4, :], ps[:, 2 + half, :].rearrange("p (k n) -> p k n", k=4))\
               .then_inc(e_xg_high, 1)

        def expert_pass(n, upcoming):
            for g in range(NG):
                if g:
                    turned_high(n, g - 1)
                    high(3 * g + 2, n)
                else:
                    high(3, n)
                act.wait_ge(e_gu, n * NG + (g + 1))
                if g >= 2:
                    act.wait_ge(e_act_done, n * NG + (g - 1))
                act.activation(e_silu[:, g % 2, :], ps[:, 4 + g % 2, 0:GW], ACT.Silu).then_inc(e_silu_done, 1)
                if 0 < g < NG - 1:
                    high(3 * g + 3, n)
                if g < NG - 1:
                    high(3 * g + 4, n)
                if g == G_TURN:
                    act.wait_ge(e_pickT, n + 1)
                    act.copy(pickT[:, :], ps[:, 7, 0:T]).then_inc(e_pickT_done, 1)
            high(0, n + 1)
            turned_high(n, NG - 1)
            if upcoming is not None:
                xg_high_part(upcoming, 0)
            high(1, n + 1)
            act.wait_ge(e_down, n * NG + NG)
            act.wait_ge(e_gate_done, n + 1)
            for half in range(2):
                act.mul(ye_high[:, half * 512:(half + 1) * 512], ps[:, half, :], slot_gate[:, 0:1]).then_inc(e_y_high, 1)
            if upcoming is not None:
                xg_high_part(upcoming, 1)
            high(2, n + 1)

        def turned_high(n, g):
            act.wait_ge(e_T, n * NG + (g + 1))
            if g >= 2:
                act.wait_ge(e_down, n * NG + (g - 1))
            act.copy(eh_high[:, g % 2, :], ps[:, 6, 0:GW]).then_inc(e_high_done, 1)

        act.preload_act_table(ACT.Silu)
        for half in range(2):
            xg_high_part(0, half)
        with act.Fori(0, E) as e:
            expert_pass(e, e + 1)
        act.wait_ge(route_done, 1)
        passes = act.alloc_register("passes_act")
        act.reg_mov(passes, E)
        largest = act.value_load(counts[0:1, E:E + 1], min_val=0, max_val=T)
        with act.If(largest > CAP):
            with act.Fori(0, E) as e:
                many = act.value_load(counts[0:1, bass.ds(e, 1)], min_val=0, max_val=T)
                with act.If(many > CAP):
                    n = act.snap(passes)
                    for half in range(2):
                        xg_high_part(n + 1, half)
                    expert_pass(n, None)
                    act.reg_add(passes, passes, 1)
        n = act.snap(passes)
        load_ln_exp()
        for t in range(NT):
            act.wait_ge(e_added, n * 2 - (1 - t))
            norm_tile(5, t)
        highs(hn_high, 1)
        for i in range(NSPLIT, len(tail)):
            high(i, n, tail)
        act.preload_act_table(ACT.Sigmoid)
        for t in range(NT):
            for half in range(2):
                act.wait_ge(gate_ready, NT + 2 * t + half + 1)
                act.activation(sig1[:, t, half * 512:(half + 1) * 512], ps[:, 4 + 2 * t + half, :], ACT.Sigmoid).then_inc(sig_done, 1)

    @block.vector
    def _(dve):
        chain = [0]

        def link(ins):
            chain[0] += 1
            ins.then_inc(dve_chain, 1)
            dve.wait_ge(dve_chain, chain[0])


        def means(r, parts):
            c = 0
            for src, width in parts:
                n = src.shape[1]
                ins = dve.tensor_scalar(mean_sq[:, r, c:c + n], src, 1.0 / width, EPS, ALU.mult, ALU.add)
                c += n
            ins.then_inc(mean_ready, 1)

        def correction(r, y):
            m, w = mean_sq[:, r, 0:y.shape[1]], newton[:, 0:y.shape[1]]
            dve.wait_ge(seed_ready, r + 1)
            if y.shape[1] == 1:
                link(dve.tensor_scalar(w, y, y, m, ALU.mult, ALU.mult))
            else:
                link(dve.tensor_tensor(w, y, y, ALU.mult))
                link(dve.tensor_tensor(w, w, m, ALU.mult))
            link(dve.tensor_scalar(w, w, -0.5, 1.5, ALU.mult, ALU.add))
            return w

        def refine(r, y):
            link(dve.tensor_tensor(y, y, correction(r, y), ALU.mult))

        def norm(k, gain, update, dst=hnT, gain2=None, signal=hnT_done, then=None, early=False):
            def root(t):
                r = rstd[:, k, t:t + 1]
                if gain is None:
                    refine(r_norm(k, t), r)
                    ins = dve.scalar_tensor_tensor(out=hs[:, t, :], in0=h[:, t, :], scalar=r, in1=ffn_gain[:], op0=ALU.mult, op1=ALU.mult)
                else:
                    ins = dve.tensor_scalar(hs[:, t, :], h[:, t, :], correction(r_norm(k, t), r), r, ALU.mult, ALU.mult)
                ins.then_inc(hs_done, 1)

            def mean(t):
                dve.wait_ge(sq_done, NT * k + t + 1)
                means(r_norm(k, t), ((sumsq[:, k, t:t + 1], D),))

            def turned(t):
                for half in range(2):
                    f = 2 * t + half
                    dve.wait_ge(hT_done, 4 * k + f + 1)
                    src = ps[:, norm_bank(k, t) + half, :].rearrange("p (c n) -> p c n", c=4)
                    if gain is None:
                        ins = dve.tensor_copy(dst[:, 4 * half:4 * half + 4, t * P:(t + 1) * P], src)
                    for d, g in ((dst, gain), (hnT2, gain2)):
                        if g is None:
                            continue
                        gg = bc(gainT[:, g + 4 * half:g + 4 * half + 4].unsqueeze(2), [P, 4, P])
                        ins = dve.tensor_tensor(d[:, 4 * half:4 * half + 4, t * P:(t + 1) * P], src, gg, ALU.mult)
                    ins.then_inc(signal, 1)

            update(0)
            mean(0)
            root(0)
            if early:
                turned(0)
            update(1)
            mean(1)
            root(1)
            if not early:
                turned(0)
            if then is not None:
                then(0)
            turned(1)
            if then is not None:
                then(1)

        def gains(t):
            if t:
                dve.wait_ge(gains_T, 1)
                dve.tensor_copy(gainT[:], ps[:, 0, 0:NGAIN]).then_inc(gains_read, 1)
                dve.wait_ge(gains_read, 1)

        norm(0, G_ATTN_A, gains)
        dve.wait_ge(pos_in, 16)
        dve.wait_ge(consts_ready, 1)
        link(dve.tensor_copy(pos_f[:], pos_i[:]))
        for t in range(NT):
            link(dve.tensor_scalar(ang[:, t, :], invf[:], pos_f[:, t:t + 1], None, ALU.mult))
        PI1, PI2 = 6.28125, float(np.float32(0.0019340515136718750))
        PI3 = float(np.float32(2 * math.pi - PI1 - PI2))
        MAGIC = 1.5 * 2 ** 23
        af = ang[:].rearrange("p t i -> p (t i)")
        for s, quarter in enumerate((0.0, 0.25)):
            n = trn[:, s].rearrange("p t i -> p (t i)")
            r = red[:, s].rearrange("p t i -> p (t i)")
            link(dve.tensor_scalar(n, af, 1.0 / (2 * math.pi), quarter, ALU.mult, ALU.add))
            link(dve.tensor_scalar(n, n, MAGIC, None, ALU.add))
            link(dve.tensor_scalar(n, n, MAGIC, None, ALU.subtract))
            link(dve.scalar_tensor_tensor(out=r, in0=n, scalar=-PI1, in1=af, op0=ALU.mult, op1=ALU.add))
            link(dve.scalar_tensor_tensor(out=r, in0=n, scalar=-PI2, in1=r, op0=ALU.mult, op1=ALU.add))
            link(dve.scalar_tensor_tensor(out=r, in0=n, scalar=-PI3, in1=r, op0=ALU.mult, op1=ALU.add))
            if s:
                link(dve.tensor_scalar(r, r, math.pi / 2, None, ALU.add))
        rf = red[:].rearrange("p s t i -> p (s t i)")
        PIF = 3.1415925
        dve.tensor_scalar(rf, rf, PIF, -PIF, ALU.min, ALU.max).then_inc(angles_done, 1)

        dve.wait_ge(qkg_in, 64)
        dve.wait_ge(trig_done, 1)
        for w in range(2):
            for i, (trig, g0) in enumerate(((1, 0), (0, HALF), (1, HALF), (0, 0))):
                ins = dve.tensor_tensor(rope_tab[:, w, i], sincos[:, trig], bc(rope_gain[:, w, g0:g0 + HALF].unsqueeze(1), [P, NT, HALF]), ALU.mult)
        ins.then_inc(tab_done, 1)
        dve.wait_ge(tab_done, 1)

        def rotate(x1, x2, y1, y2, tab, tmp, shape):
            for i, x in enumerate((x1, x2, x2, x1)):
                ins = dve.tensor_tensor(tmp[i], x, tab[i] if shape is None else bc(tab[i].unsqueeze(1), shape), ALU.mult)
            link(ins)
            dve.tensor_tensor(y1, tmp[0], tmp[1], ALU.subtract)
            return dve.tensor_tensor(y2, tmp[2], tmp[3], ALU.add)

        for t in range(NT):
            dve.wait_ge(lat_sq_done, 3 * (t + 1))
            means(r_lat(t), ((lat_sq[:, t, 0:1], QL), (lat_sq[:, t, 1:2], KVL)))
            refine(r_lat(t), lat_rstd[:, t, :])
            dve.tensor_copy(kpe[:, t, :], ps[:, 2 * t + 1, KVL:KVL + ROPE]).then_inc(kpe_copied, 1)
            dve.tensor_scalar(lat[:, t, 0:QL], ps[:, 2 * t, 0:QL], lat_rstd[:, t, 0:1], None, ALU.mult)
            dve.tensor_scalar(lat[:, t, QL:], ps[:, 2 * t + 1, 0:KVL], lat_rstd[:, t, 1:2], None, ALU.mult).then_inc(lat_scaled, 1)
            dve.wait_ge(kpe_copied, 2 * t + 1)
            rotate(kpe[:, t, 0:HALF], kpe[:, t, HALF:], kpe_rot[:, t, 0:HALF], kpe_rot[:, t, HALF:],
                   [rope_tab[:, 1, i, t] for i in range(4)], [rot[:, i, 0, :] for i in range(4)], None).then_inc(kpe_copied, 1)
            if t < NT - 1:
                dve.wait_ge(kpe_copied, 2 * t + 2)
            dve.wait_ge(lat_T, t + 1)
            dve.tensor_tensor(latT[:, 0:4, t * P:(t + 1) * P], ps[:, 4 + 2 * t, :].rearrange("p (c n) -> p c n", c=4),
                              bc(gainT[:, G_LAT:G_LAT + 4].unsqueeze(2), [P, 4, P]), ALU.mult)
            dve.tensor_scalar(latT[:, 4, t * P:(t + 1) * P], ps[:, 5 + 2 * t, 0:P], gainT[:, G_LAT + 4:G_LAT + 5], None,
                              ALU.mult).then_inc(latT_done, 1)
        dve.wait_ge(kpe_copied, 2 * NT)
        for t in range(NT):
            dve.wait_ge(q_squared, t + 1)
            dve.tensor_reduce(qk_sq[:, 0, t, :], junk[:, 0:HA * QK].rearrange("p (h c) -> p h c", c=QK), AX.X, ALU.add).then_inc(squares_read, 1)
            dve.wait_ge(squares_read, t + 1)
            means(r_qk(0, t), ((qk_sq[:, 0, t, :], QK),))
            refine(r_qk(0, t), qk_rstd[:, 0, t, :])
            q = qk[:, 0, t]
            link(dve.tensor_tensor(q.rearrange("p (b h) c -> p b h c", b=2), ps[:, 2 * t:2 * t + 2, 0:4 * QK].rearrange("p b (h c) -> p b h c", c=QK),
                                   bc(qk_rstd[:, 0, t, :].rearrange("p (b h) -> p b h", b=2).unsqueeze(3), [P, 2, 4, QK]), ALU.mult))
            x1, x2 = q[:, :, NOPE:NOPE + HALF], q[:, :, NOPE + HALF:]
            rotate(x1, x2, x1, x2, [rope_tab[:, 0, i, t] for i in range(4)], [rot[:, i] for i in range(4)], [P, HA, HALF]).then_inc(qk_ready, 1)
            if t < NT - 1:
                dve.wait_ge(qk_ready, t + 1)
        for t in range(NT):
            dve.wait_ge(k_squared, t + 1)
            dve.tensor_reduce(qk_sq[:, 1, t, :], k_squares[:].rearrange("p (h c) -> p h c", c=NOPE), AX.X, ALU.add).then_inc(squares_read, 1)
            dve.wait_ge(squares_read, NT + t + 1)
            link(dve.tensor_scalar(qk_sq[:, 1, t, :], qk_sq[:, 1, t, :], kpe_sq[:, t:t + 1], None, ALU.add))
            means(r_qk(1, t), ((qk_sq[:, 1, t, :], QK),))
            refine(r_qk(1, t), qk_rstd[:, 1, t, :])
            k = qk[:, 1, t]
            kv = banks(4 + 2 * t, 6 + 2 * t).rearrange("p (h c) -> p h c", c=NOPE + VD)
            rk = qk_rstd[:, 1, t, :].unsqueeze(2)
            dve.tensor_tensor(k[:, :, 0:NOPE], kv[:, :, 0:NOPE], bc(rk, [P, HA, NOPE]), ALU.mult)
            dve.tensor_tensor(k[:, :, NOPE:], bc(kpe_rot[:, t, :].unsqueeze(1), [P, HA, ROPE]), bc(rk, [P, HA, ROPE]), ALU.mult).then_inc(qk_ready, 1)
        for t in range(NT):
            dve.wait_ge(qk_T, NT + t + 1)
            dve.tensor_scalar(qkT[:, 1, 0:4, t * P:(t + 1) * P], ps[0:QK, 4 + 2 * t, :].rearrange("p (h n) -> p h n", h=4),
                              nope_gain[:, 1:2], None, ALU.mult).then_inc(kT_done, 1)

        def mask_max(j):
            dve.wait_ge(sc_ready, j + 1)
            b = 2 * j
            s = probs[:, j]
            dve.tensor_tensor(s, ps[:, b:b + 2, 0:3 * P], bc(maskA[:].unsqueeze(1), [P, 2, 3 * P]), ALU.add).then_inc(sc_read, 1)
            dve.wait_ge(sc_read, 2 * j + 1)
            dve.tensor_reduce(row_max[:, j, 0, :], s[:, :, 0:P], AX.X, ALU.max)
            link(dve.tensor_reduce(row_max[:, j, 1, :], s[:, :, P:], AX.X, ALU.max))
            dve.tensor_scalar(neg_max[:, j], row_max[:, j], -1.0 / math.sqrt(QK), None, ALU.mult).then_inc(sc_read, 1)

        def normalise(j):
            dve.wait_ge(exp_done, j + 1)
            link(dve.reciprocal(row_inv[:, j], row_sum[:, j]))
            for hh in range(2):
                for t, (c0, c1) in enumerate(((0, P), (P, 3 * P))):
                    s = probs[:, j, hh, c0:c1]
                    ins = dve.tensor_scalar(s, s, row_inv[:, j, t, hh:hh + 1], None, ALU.mult)
            ins.then_inc(probs_ready, 1)

        for j in range(5):
            if j < 4:
                mask_max(j)
            if j:
                normalise(j - 1)

        def add_to_h(ready):
            def update(t):
                dve.wait_ge(ready, t + 1)
                dve.tensor_tensor(h[:, t, :], h[:, t, :], banks(2 * t, 2 * t + 2), ALU.add).then_inc(h_updated, 1)
            return update

        def low(i, n=None, units=None):
            pos = DENSE + i if n is None else FRONT + i
            dve.wait_ge(high_done, i + 1 if n is None else n * UNITS + (UNITS + i + 1))
            dve.tensor_tensor(w_low[:, i % NSPLIT, :], slot_of_unit(pos), w_high[:, i % NSPLIT, :].bitcast(F32), ALU.subtract)\
               .then_inc(low_done, 1)

        def lows(high_part, dst, i):
            def of_tile(t):
                for half in range(2):
                    dve.wait_ge(hn_high_done, 4 * i + 2 * t + half + 1)
                    at = (slice(None), slice(4 * half, 4 * half + 4), slice(t * P, (t + 1) * P))
                    dve.tensor_tensor(dst[at], hnT[at], high_part[at].bitcast(F32), ALU.subtract).then_inc(hn_low_done, 1)
            return of_tile

        low(0)
        low(1)
        norm(1, G_FFN, add_to_h(a_out_ready), signal=hn_ready, then=lows(dn_high, dn_low, 0), early=True)
        for g in range(NG):
            low(3 * g + 2)
            for f in range(2):
                dve.wait_ge(d_silu_done, 2 * g + f + 1)
                if g:
                    dve.wait_ge(d_low_done, 2 * g - 1 + f)
                dve.tensor_tensor(d_h[:, f, :], d_silu[:, f, :], ps[:, 5 + 2 * f, 0:T], ALU.mult).then_inc(d_act_done, 1)
            if g < NG - 1:
                low(3 * g + 3)
            for f in range(2):
                dve.wait_ge(d_high_done, 2 * g + f + 1)
                dve.tensor_tensor(d_low[:, f, :], d_h[:, f, :], d_high[:, f, :].bitcast(F32), ALU.subtract).then_inc(d_low_done, 1)
            if g < NG - 1:
                low(3 * g + 4)
        norm(2, G_PLE, add_to_h(d_sum_ready))

        def gated_input(t):
            dve.wait_ge(up_ready, t + 1)
            dve.wait_ge(sig_done, t + 1)
            link(dve.tensor_tensor(sig0[:, t, :], sig0[:, t, :], banks(2 * t, 2 * t + 2), ALU.mult))
            dve.tensor_tensor(h[:, t, :], h[:, t, :], sig0[:, t, :], ALU.add).then_inc(h_updated, 1)

        norm(3, G_ATTN_B, gated_input, hnT, G_KVS, early=True)
        dve.wait_ge(k_ready, NT)
        for g in range(G):
            src = ps[HD * (g % 2):HD * (g % 2) + HD, 0, (g // 2) * T:(g // 2 + 1) * T]
            dve.tensor_copy(kTB[0:HD, g, :], src)
            ins = dve.tensor_copy(kTB[HD:2 * HD, g, :], src)
        ins.then_inc(kTB_done, 1)
        dve.wait_ge(masks_b_ready, 1)

        def mask_z(g):
            dve.wait_ge(z_ready, g + 1)
            if g >= 3:
                dve.wait_ge(att_done, g - 2)
            dve.tensor_tensor(zm[:, g % 3, 0:1024].rearrange("p (b q) -> p b q", q=P), banks(0, 2).rearrange("p (b q) -> p b q", q=P),
                              bc(negT[:].unsqueeze(1), [P, 8, P]), ALU.add)
            dve.tensor_copy(zm[:, g % 3, 1024:].rearrange("p (b q) -> p b q", b=2), ps[:, 2:4, 0:256]).then_inc(zm_done, 1)

        def softplus(g):
            dve.wait_ge(ln_done, g + 1)
            dve.scalar_tensor_tensor(out=sp[:, g % 3], in0=zm[:, g % 3], scalar=0.0, in1=sp[:, g % 3],
                                     op0=ALU.max, op1=ALU.add).then_inc(sp_done, 1)

        def log_weights(g):
            dve.wait_ge(sum_ready, g + 1)
            dve.tensor_tensor(zm[:, g % 3, :], zm[:, g % 3, :], banks(4, 7), ALU.subtract).then_inc(w_done, 1)

        def out_heads(g):
            dve.wait_ge(oB_ready, g + 1)
            for t in range(NT):
                ins = dve.tensor_copy(oTB[:, 2 * g:2 * g + 2, t * P:(t + 1) * P],
                                      ps[:, 7, t * 256:(t + 1) * 256].rearrange("p (c q) -> p c q", c=2))
            ins.then_inc(oTB_done, 1)

        for step in range(G + 2):
            if step >= 2:
                log_weights(step - 2)
            if 1 <= step <= G:
                softplus(step - 1)
            if step < G:
                mask_z(step)
            if step >= 2:
                out_heads(step - 2)
        for i in range(NSPLIT):
            low(i, 0)
        dve.wait_ge(ffn_gain_in, 16)
        norm(4, None, add_to_h(o_b_ready), early=True)

        for t in range(NT):
            dve.wait_ge(lg_ready, t + 1)
            link(dve.tensor_copy(lg[:, t, :], ps[:, t, 0:E]))
            dve.tensor_reduce(top[:, t:t + 1], lg[:, t, :], AX.X, ALU.max).then_inc(top_found, 1)
            other = bc(lg[:, t, :].unsqueeze(1), [P, E, E])
            own = bc(lg[:, t, :].unsqueeze(2), [P, E, E])
            dve.tensor_tensor(cmp_gt[:, t], other, own, ALU.is_gt)
            link(dve.tensor_tensor(cmp_eq[:, t], other, own, ALU.is_equal))
            dve.wait_ge(top_found, t + 1)
            dve.tensor_scalar(ntop[:, t:t + 1], top[:, t:t + 1], -1.0, None, ALU.mult).then_inc(top_done, 1)
            link(dve.tensor_tensor(cmp_eq[:, t], cmp_eq[:, t], earlier[:], ALU.mult))
            link(dve.tensor_tensor(cmp_gt[:, t], cmp_gt[:, t], cmp_eq[:, t], ALU.add))
            link(dve.tensor_reduce(rank[:, t, :], cmp_gt[:, t], AX.X, ALU.add))
            dve.tensor_scalar(picked[:, t, :], rank[:, t, :], 2.0, None, ALU.is_lt).then_inc(picked_done, 1)
        dve.wait_ge(gexp_done, NT)
        dve.wait_ge(picked_done, NT)
        link(dve.tensor_tensor(gexp[:], gexp[:], picked[:], ALU.mult))
        link(dve.tensor_reduce(gsum[:], gexp[:], AX.X, ALU.add))
        link(dve.reciprocal(gsum[:], gsum[:]))
        dve.tensor_tensor(gate[:], gexp[:], bc(gsum[:].unsqueeze(2), [P, NT, E]), ALU.mult)
        dve.wait_ge(pos_ready, 1)
        link(dve.memset(slot_of[:], 0.0))
        link(dve.scalar_tensor_tensor(out=slot_of[:, :, 0:E], in0=ps[:, 3, 0:NT * E].rearrange("p (t e) -> p t e", t=NT), scalar=1.0,
                                      in1=picked[:], op0=ALU.add, op1=ALU.mult))
        link(dve.tensor_scalar(slot_of[:], slot_of[:], -1.0, None, ALU.add))
        dve.tensor_reduce(counts[:, E:], ps[:, 2, 0:E], AX.X, ALU.max)
        dve.tensor_copy(counts[:, 0:E], ps[:, 2, 0:E]).then_inc(route_done, 1)

        def picks(e, base):
            for t in range(NT):
                ins = dve.tensor_scalar(pick[:, t, :], slot_no[:, base:base + CAP], slot_of[:, t, bass.ds(e, 1)], None, ALU.is_equal)
            ins.then_inc(e_pick, 1)

        def xg_low_part(k, half):
            dve.wait_ge(e_xg_high, k * 2 + (half + 1))
            chunks = slice(4 * half, 4 * half + 4)
            dve.tensor_tensor(xg_low[:, chunks, :], ps[:, 2 + half, :].rearrange("p (k n) -> p k n", k=4),
                              xg_high[:, chunks, :].bitcast(F32), ALU.subtract).then_inc(e_xg_low, 1)

        def expert_pass(n, e, k):
            for g in range(NG):
                if g:
                    turned_low(n, g - 1)
                if 0 < g < NG - 1:
                    low(3 * g + 2, n)
                dve.wait_ge(e_silu_done, n * NG + (g + 1))
                if g >= 2:
                    dve.wait_ge(e_T, n * NG + (g - 1))
                dve.tensor_tensor(e_h[:, g % 2, :], e_silu[:, g % 2, :], ps[:, 4 + g % 2, GW:2 * GW], ALU.mult).then_inc(e_act_done, 1)
                if g == NG - 1:
                    low(UNITS - 1, n)
                if g < NG - 1:
                    low(3 * g + 3, n)
                    low(3 * g + 4, n)
                if g == G_PICK:
                    dve.wait_ge(e_pickT_done, n + 1)
                    dve.tensor_copy(slot_gate[:], ps[:, 7, bass.ds(e + T, 1)]).then_inc(e_gate_done, 1)
                if g == G_PICK and k is not None:
                    picks(e + 1, 0)
            turned_low(n, NG - 1)
            low(0, n + 1)
            if k is not None:
                xg_low_part(k, 0)
            for half in range(2):
                cols = slice(half * 512, (half + 1) * 512)
                dve.wait_ge(e_y_high, n * 2 + (half + 1))
                dve.scalar_tensor_tensor(out=ye_low[:, cols], in0=ps[:, half, :], scalar=slot_gate[:, 0:1], in1=ye_high[:, cols].bitcast(F32),
                                         op0=ALU.mult, op1=ALU.subtract).then_inc(e_y_low, 1)
            low(1, n + 1)
            if k is not None:
                xg_low_part(k, 1)
            for t in range(NT):
                dve.wait_ge(e_scat, n * 2 + (t + 1))
                b = (0, 6)[t]
                dve.tensor_tensor(h[:, t, :], h[:, t, :], banks(b, b + 2), ALU.add).then_inc(e_added, 1)
                if t == 0:
                    low(2, n + 1)

        def turned_low(n, g):
            dve.wait_ge(e_high_done, n * NG + (g + 1))
            dve.tensor_tensor(eh_low[:, g % 2, :], ps[:, 6, 0:GW], eh_high[:, g % 2, :].bitcast(F32), ALU.subtract).then_inc(e_low_done, 1)

        picks(0, 0)
        for half in range(2):
            xg_low_part(0, half)
        dve.wait_ge(route_done, 1)
        with dve.Fori(0, E) as e:
            expert_pass(e, e, e + 1)
        passes = dve.alloc_register("passes_dve")
        dve.reg_mov(passes, E)
        largest = dve.value_load(counts[0:1, E:E + 1], min_val=0, max_val=T)
        with dve.If(largest > CAP):
            with dve.Fori(0, E) as e:
                many = dve.value_load(counts[0:1, bass.ds(e, 1)], min_val=0, max_val=T)
                with dve.If(many > CAP):
                    n = dve.snap(passes)
                    picks(e, CAP)
                    for half in range(2):
                        xg_low_part(n + 1, half)
                    expert_pass(n, e, None)
                    dve.reg_add(passes, passes, 1)
        n = dve.snap(passes)
        norm(5, G_PLE + 8, lambda t: None, signal=hn_ready, then=lows(hn_high, hn_low, 1))
        for i in range(NSPLIT, len(tail)):
            low(i, n)
        for t in range(NT):
            dve.wait_ge(up_ready, NT + t + 1)
            for half in range(2):
                cols = slice(half * 512, (half + 1) * 512)
                dve.wait_ge(sig_done, NT + 2 * t + half + 1)
                link(dve.tensor_tensor(sig1[:, t, cols], sig1[:, t, cols], ps[:, 2 * t + half, :], ALU.mult))
                dve.tensor_tensor(h[:, t, cols], h[:, t, cols], sig1[:, t, cols], ALU.add).then_inc(h_updated, 1)

    @block.tensor
    def _(pe):
        def wait_unit(pos):
            landed_wait(pe, pos)

        pe.wait_ge(ident_ready, 1)
        pe.wait_ge(gains_in, 16 * 7)
        pe.transpose(ps[:, 0, 0:NGAIN], gains_raw[:, :], ident[0:NGAIN, 0:NGAIN]).then_inc(gains_T, 1)

        def turn_tile(k, t):
            pe.wait_ge(hs_done, NT * k + t + 1)
            for half in range(2):
                for c in range(4):
                    kk = 4 * half + c
                    ins = pe.transpose(ps[:, norm_bank(k, t) + half, c * P:(c + 1) * P], hs[:, t, kk * P:(kk + 1) * P], ident[:])
                ins.then_inc(hT_done, 1)

        def wait_turned(k, t):
            if k in (1, 5):
                pe.wait_ge(hn_low_done, (0 if k == 1 else 4) + 2 * t + 2)
            else:
                pe.wait_ge(hnT_done, 4 * k + 2 * t + 2 - (4 if k > 1 else 0))

        def norm(k):
            for t in range(NT):
                turn_tile(k, t)
            wait_turned(k, NT - 1)

        for t in range(NT):
            turn_tile(0, t)
        pe.wait_ge(gains_read, 1)
        wa = [view(place[("a_in", k // 3)], min(3, KD - k // 3 * 3), QL + KVL + ROPE)[:, k % 3] for k in range(KD)]
        for t in range(NT):
            wait_turned(0, t)
            for k in range(KD):
                if t == 0 and k % 3 == 0:
                    wait_unit(place[("a_in", k // 3)])
                lhsT = hnT[:, k, t * P:(t + 1) * P]
                pe.matmul(ps[:, 2 * t, 0:QL], lhsT, wa[k][:, 0:QL], start=(k == 0), stop=(k == KD - 1))
                ins = pe.matmul(ps[:, 2 * t + 1, 0:KVL + ROPE], lhsT, wa[k][:, QL:], start=(k == 0), stop=(k == KD - 1))
            ins.then_inc(a_ready, 1)
        pq = [place[("q_up", 0)], place[("q_up", 1)]]
        pk = place[("kv_up", 0)]
        wq = [view(pq[0], 2, HA * QK)[:, 0], view(pq[0], 2, HA * QK)[:, 1], view(pq[1], 1, HA * QK)[:, 0]]
        wkv = view(pk, 2, HA * (NOPE + VD))

        def turn_latents(t):
            pe.wait_ge(lat_scaled, t + 1)
            if t:
                pe.wait_ge(pT_done, 2)
            for c in range(NLAT):
                b = 4 + 2 * t + c // 4
                ins = pe.transpose(ps[:, b, (c % 4) * P:(c % 4 + 1) * P], lat[:, t, c * P:(c + 1) * P], ident[:])
            ins.then_inc(lat_T, 1)

        def queries(t):
            pe.wait_ge(latT_done, t + 1)
            for half in range(2):
                for k in range(3):
                    ins = pe.matmul(ps[:, 2 * t + half, 0:4 * QK], latT[:, k, t * P:(t + 1) * P],
                                    wq[k][:, half * 4 * QK:(half + 1) * 4 * QK], start=(k == 0), stop=(k == 2))
            ins.then_inc(q_done, 1)

        def keys_values(t):
            for half in range(2):
                for k in range(2):
                    ins = pe.matmul(ps[:, 4 + 2 * t + half, :], latT[:, 3 + k, t * P:(t + 1) * P],
                                    wkv[:, k, half * 512:(half + 1) * 512], start=(k == 0), stop=(k == 1))
            ins.then_inc(kv_done, 1)

        def turn_heads(w, t):
            pe.wait_ge(qk_ready, NT * w + t + 1)
            for hd in range(HA):
                ins = pe.transpose(ps[0:QK, 4 * w + 2 * t + hd // 4, (hd % 4) * P:(hd % 4 + 1) * P], qk[:, w, t, hd, :], ident[:])
            ins.then_inc(qk_T, 1)

        turn_latents(0)
        pe.wait_ge(p_inS, 32)
        for i in range(2):
            for c in range(2):
                for t in range(NT):
                    ins = pe.transpose(ps[:, 6 + i, c * T + t * P:c * T + (t + 1) * P], p_in[:, i, t, c * P:(c + 1) * P], ident[:])
            ins.then_inc(p_T, 1)
        for pos in pq + [pk]:
            wait_unit(pos)
        queries(0)
        turn_latents(1)
        queries(1)
        keys_values(0)
        turn_heads(0, 0)
        keys_values(1)
        turn_heads(0, 1)
        turn_heads(1, 0)
        turn_heads(1, 1)

        def scores(j):
            pe.wait_ge(qT_done, 3 if j == 0 else 4)
            pe.wait_ge(kT_done, NT)
            if j >= 2:
                pe.wait_ge(kT_high_done, NT)
            for hh in range(2):
                hd, b = 2 * j + hh, 2 * j + hh
                pe.matmul(ps[:, b, 0:P], qkT[:, 0, hd, 0:P], qkT[:, 1, hd, 0:P], start=True, stop=True)
                ins = pe.matmul(ps[:, b, P:3 * P], qkT[:, 0, hd, P:], qkT[:, 1, hd, :], start=True, stop=True)
            ins.then_inc(sc_ready, 1)

        def turn_probs(j):
            pe.wait_ge(probs_ready, j + 1)
            if j >= 2:
                pe.wait_ge(probsT_done, j - 1)
            for hh in range(2):
                for c in range(3):
                    ins = pe.transpose(ps[:, 2 * (j % 2) + hh, c * P:(c + 1) * P], probs[:, j, hh, c * P:(c + 1) * P], ident[:])
            ins.then_inc(probs_T, 1)

        def outputs(j):
            pe.wait_ge(probsT_done, j + 1)
            pe.wait_ge(sc_read, 5)
            b, col = 4 + j // 2, (j % 2) * T
            for hh in range(2):
                hd = 2 * j + hh
                o = ps[hh * VD:(hh + 1) * VD, b, col:col + T]
                pt = probsT[:, j % 2, hh]
                pe.matmul(o[:, 0:P], va[:, 0, hd, :], pt[:, 0:P], start=True, stop=True)
                pe.matmul(o[:, P:], va[:, 0, hd, :], pt[:, P:2 * P], start=True, stop=False)
                ins = pe.matmul(o[:, P:], va[:, 1, hd, :], pt[:, 2 * P:], start=False, stop=True)
            ins.then_inc(oA_ready, 1)

        for j in range(4):
            scores(j)
        turn_probs(0)
        for j in range(1, 4):
            turn_probs(j)
            outputs(j - 1)
        outputs(3)

        def project_tile(name, t, b0, src, nk, ready, k0=0, k1=None):
            for k in range(k0, nk if k1 is None else k1):
                pos = place[(name, k // 2)]
                if t == 0 and k % 2 == 0:
                    wait_unit(pos)
                for half in range(2):
                    ins = pe.matmul(ps[:, b0 + half, :], src[:, k, t * P:(t + 1) * P], view(pos, 2, D)[:, k % 2, half * 512:(half + 1) * 512],
                                    start=(k == 0), stop=(k == nk - 1))
            if k == nk - 1:
                ins.then_inc(ready, 1)

        pe.wait_ge(probsT_done, 4)
        pe.wait_ge(oTA_done, 2)
        project_tile("a_out", 0, 0, oTA, 4, a_out_ready)
        project_tile("a_out", 1, 2, oTA, 4, a_out_ready, k1=3)
        turn_tile(1, 0)
        project_tile("a_out", 1, 2, oTA, 4, a_out_ready, k0=3)
        turn_tile(1, 1)
        wait_turned(1, 1)

        def passes3(out, high_l, low_l, high_r, low_r, first, last):
            pe.matmul(out, high_l, high_r, start=first, stop=False)
            pe.matmul(out, high_l, low_r, start=False, stop=False)
            return pe.matmul(out, low_l, high_r, start=False, stop=last)

        def parts(i, k, n):
            return [w[:, i % NSPLIT, 0:k * n].rearrange("p (k n) -> p k n", k=k) for w in (w_high, w_low)]

        def d_gate_up(i, u, g):
            pe.wait_ge(low_done, i + 1)
            wh, wl = parts(i, 4, 2 * GW)
            for f in range(2):
                if u == 0 and g:
                    pe.wait_ge(d_act_done, 2 * (g - 1) + f + 1)
                for s in range(2):
                    cols = slice(s * GW + f * P, s * GW + (f + 1) * P)
                    for kk in range(4):
                        k = 4 * u + kk
                        ins = passes3(ps[:, 4 + 2 * f + s, 0:T], wh[:, kk, cols], wl[:, kk, cols], dn_high[:, k, :], dn_low[:, k, :],
                                      k == 0, k == KD - 1)
                if u == 0 and f == 1:
                    ins.then_inc(d_gu_half, 1)
                if u == 1:
                    ins.then_inc(d_gu if f else d_gu_first, 1)

        def d_down_part(i, g):
            pe.wait_ge(low_done, i + 1)
            wh, wl = parts(i, 2, D)
            def product(f, t, last=False):
                tok = slice(t * P, (t + 1) * P)
                for half in range(2):
                    cols = slice(half * 512, (half + 1) * 512)
                    ins = passes3(ps[:, 2 * t + half, :], d_high[:, f, tok], d_low[:, f, tok], wh[:, f, cols], wl[:, f, cols],
                                  g == 0 and f == 0, last)
                return ins

            if g < NG - 1:
                for f in range(2):
                    pe.wait_ge(d_low_done, 2 * g + f + 1)
                    for t in range(NT):
                        ins = product(f, t)
                ins.then_inc(d_down, 1)
            else:
                pe.wait_ge(d_low_done, 2 * NG)
                for t in range(NT):
                    product(0, t)
                    product(1, t, last=True).then_inc(d_sum_ready, 1)

        for i, (name, u) in enumerate(order[DENSE:DENSE_END]):
            if name == "ffn_gu":
                d_gate_up(i, u % 2, u // 2)
            else:
                d_down_part(i, u)

        def ple_up(i, w, t):
            for half in range(2):
                for c in range(2):
                    ins = pe.matmul(ps[:, 2 * t + half, :], pT[:, i, c, t * P:(t + 1) * P], w[:, c, half * 512:(half + 1) * 512],
                                    start=(c == 0), stop=(c == 1))
            ins.then_inc(up_ready, 1)

        wait_unit(place[("ple_up0", 0)])
        for t in range(NT):
            pe.wait_ge(h_updated, 2 + t + 1)
            ple_up(0, view(place[("ple_up0", 0)], 2, D), t)
            turn_tile(2, t)
        wait_turned(2, 0)
        project_tile("ple_gate0", 0, 4, hnT, KD, gate_ready)
        wait_turned(2, 1)
        project_tile("ple_gate0", 1, 6, hnT, KD, gate_ready, k1=5)
        turn_tile(3, 0)
        project_tile("ple_gate0", 1, 6, hnT, KD, gate_ready, k0=5)

        def z_scores(g):
            pe.wait_ge(qTB_done, g + 1)
            if g == 0:
                pe.wait_ge(kTB_done, 1)
                pe.wait_ge(vB_done, 1)
            else:
                pe.wait_ge(zm_done, g)
            for t in range(NT):
                for par in range(2):
                    r = slice(par * HD, (par + 1) * HD)
                    pe.matmul(ps[:, par, t * 256:(t + 1) * 256], kTB[r, g, t * P:(t + 1) * P], qTB[r, 2 * g:2 * g + 2, t * P:(t + 1) * P],
                              start=True, stop=True)
            for par in range(2):
                r = slice(par * HD, (par + 1) * HD)
                ins = pe.matmul(ps[:, 2 + par, 0:256], kTB[r, g, 0:P], qTB[r, 2 * g:2 * g + 2, P:T], start=True, stop=True)
            ins.then_inc(z_ready, 1)

        pkv = [place[("kv_shared", u)] for u in range(2)]
        pqb = [place[("q_b", u)] for u in range(4)]
        for t in range(NT):
            if t:
                turn_tile(3, t)
            wait_turned(3, t)
            tok = slice(t * P, (t + 1) * P)
            for pos in (pkv if t == 0 else ()):
                wait_unit(pos)
            for c in range(2):
                for k in range(KD):
                    ins = pe.matmul(ps[:, 0, c * T + t * P:c * T + (t + 1) * P], view(pkv[k // 4], 4, 512)[:, k % 4, c * P:(c + 1) * P],
                                    hnT2[:, k, tok], start=(k == 0), stop=(k == KD - 1))
            ins.then_inc(k_ready, 1)
            for k in range(KD):
                ins = pe.matmul(ps[:, 1, t * 256:(t + 1) * 256], hnT2[:, k, tok], view(pkv[k // 4], 4, 512)[:, k % 4, 256:512],
                                start=(k == 0), stop=(k == KD - 1))
            ins.then_inc(v_ready, 1)
            for pos in (pqb if t == 0 else ()):
                wait_unit(pos)
            if t == 0:
                pe.wait_ge(sig_done, NT)
            for c in range(KD):
                for k in range(KD):
                    ins = pe.matmul(ps[:, 4 + c // 2, (c % 2) * T + t * P:(c % 2) * T + (t + 1) * P],
                                    view(pqb[k // 2], 2, D)[:, k % 2, c * P:(c + 1) * P], hnT[:, k, tok], start=(k == 0), stop=(k == KD - 1))
                if t and c % 2:
                    ins.then_inc(qB_ready, 1)
                if t and c in (3, 5):
                    z_scores(c // 2 - 1)

        def key_sums(g):
            pe.wait_ge(sp_done, g + 1)
            if g:
                pe.wait_ge(w_done, g)
            else:
                pe.wait_ge(qTB_done, 4)
            s = sp[:, g % 3]
            for par in range(2):
                pe.matmul(ps[:, 4 + par, :], lower[:], s[:, par * 512:(par + 1) * 512], start=True, stop=True)
            for par in range(2):
                pe.matmul(ps[:, 6, par * 256:(par + 1) * 256], lower[:], s[:, 1024 + par * 256:1024 + (par + 1) * 256], start=True, stop=False)
                ins = pe.matmul(ps[:, 6, par * 256:(par + 1) * 256], ones[:], s[:, par * 512 + 256:(par + 1) * 512], start=False, stop=True)
            ins.then_inc(sum_ready, 1)

        def heads(g):
            pe.wait_ge(att_done, g + 1)
            if g:
                pe.wait_ge(oTB_done, g)
            s = sp[:, g % 3]
            vt = [vB[:, t, g * HD:(g + 1) * HD] for t in range(NT)]
            for par in range(2):
                r = slice(par * HD, (par + 1) * HD)
                pe.matmul(ps[r, 7, 0:256], vt[0], s[:, par * 512:par * 512 + 256], start=True, stop=True)
                pe.matmul(ps[r, 7, 256:512], vt[1], s[:, par * 512 + 256:(par + 1) * 512], start=True, stop=False)
                ins = pe.matmul(ps[r, 7, 256:512], vt[0], s[:, 1024 + par * 256:1024 + (par + 1) * 256], start=False, stop=True)
            ins.then_inc(oB_ready, 1)

        for step in range(1, G + 1):
            if 2 <= step < G:
                z_scores(step)
            if step == G:
                pe.wait_ge(zm_done, G)
                pe.wait_ge(oTB_done, 2)
                project_tile("o_b", 0, 0, oTB, KD, o_b_ready, k1=4)
            if step >= 2:
                heads(step - 2)
            key_sums(step - 1)
        project_tile("o_b", 1, 2, oTB, KD, o_b_ready, k1=4)
        heads(G - 1)
        pe.wait_ge(oTB_done, 3)
        project_tile("o_b", 0, 0, oTB, KD, o_b_ready, k0=4, k1=6)
        pe.wait_ge(oTB_done, G)
        project_tile("o_b", 0, 0, oTB, KD, o_b_ready, k0=6)
        project_tile("o_b", 1, 2, oTB, KD, o_b_ready, k0=4, k1=7)
        turn_tile(4, 0)
        project_tile("o_b", 1, 2, oTB, KD, o_b_ready, k0=7)

        pe.wait_ge(wr_in, 16)
        for t in range(NT):
            if t:
                turn_tile(4, t)
            wait_turned(4, t)
            for k in range(KD):
                ins = pe.matmul(ps[:, t, 0:E], hnT[:, k, t * P:(t + 1) * P], wr[:, k, :], start=(k == 0), stop=(k == KD - 1))
            ins.then_inc(lg_ready, 1)
        pe.wait_ge(consts_ready, 1)
        pe.wait_ge(picked_done, NT)
        pe.matmul(ps[:, 3, 0:E], before[:], picked[:, 0, :], start=True, stop=True)
        pe.matmul(ps[:, 3, E:2 * E], before[:], picked[:, 1, :], start=True, stop=False)
        pe.matmul(ps[:, 3, E:2 * E], ones[:], picked[:, 0, :], start=False, stop=True)
        pe.matmul(ps[:, 2, 0:E], ones[:], picked[:, 0, :], start=True, stop=False)
        pe.matmul(ps[:, 2, 0:E], ones[:], picked[:, 1, :], start=False, stop=True).then_inc(pos_ready, 1)
        pe.wait_ge(route_done, 1)

        def gather(k, half):
            pe.wait_ge(e_pick, k + 1)
            for c in range(4 * half, 4 * half + 4):
                for t in range(NT):
                    ins = pe.matmul(ps[:, 2 + half, (c % 4) * P:(c % 4 + 1) * P], hs[:, t, c * P:(c + 1) * P], pick[:, t, :],
                                    start=(t == 0), stop=(t == NT - 1))
            ins.then_inc(e_xg, 1)

        def expert_pass(n, own, upcoming):
            def unit(name, u):
                i = eplace[(name, u)]
                pe.wait_ge(low_done, n * UNITS + (UNITS + i + 1))
                return i

            def gu_half(g, u):
                wh, wl = parts(unit("gu", 2 * g + u), 4, 2 * GW)
                if g == 0:
                    pe.wait_ge(e_xg_low, own * 2 + (u + 1))
                for kk in range(4):
                    k = 4 * u + kk
                    ins = passes3(ps[:, 4 + g % 2, :], xg_high[:, k, :], xg_low[:, k, :], wh[:, kk, :], wl[:, kk, :], k == 0, k == KD - 1)
                return ins

            def turn(g):
                pe.wait_ge(e_act_done, n * NG + (g + 1))
                if g:
                    pe.wait_ge(e_low_done, n * NG + g)
                for f in range(2):
                    ins = pe.transpose(ps[:, 6, f * P:(f + 1) * P], e_h[:, g % 2, f * P:(f + 1) * P], ident[:])
                ins.then_inc(e_T, 1)

            def down(g):
                wh, wl = parts(unit("down", g), 2, D)
                pe.wait_ge(e_low_done, n * NG + (g + 1))
                for f in range(2):
                    cols = slice(f * P, (f + 1) * P)
                    for half in range(2):
                        half_cols = slice(half * 512, (half + 1) * 512)
                        ins = passes3(ps[:, half, :], eh_high[:, g % 2, cols], eh_low[:, g % 2, cols], wh[:, f, half_cols], wl[:, f, half_cols],
                                      g == 0 and f == 0, g == NG - 1 and f == 1)
                ins.then_inc(e_down, 1)

            for g in range(NG):
                if g >= 2:
                    pe.wait_ge(e_act_done, n * NG + (g - 1))
                gu_half(g, 0).then_inc(e_gu_half, 1)
                if g:
                    turn(g - 1)
                gu_half(g, 1).then_inc(e_gu, 1)
                if g:
                    down(g - 1)
                if g == G_TURN:
                    for t in range(NT):
                        pe.transpose(ps[:, 7, t * P:(t + 1) * P], pick[:, t, :], ident[:])
                    for t in range(NT):
                        ins = pe.matmul(ps[:, 7, T:T + E], pick[:, t, :], gate[:, t, :], start=(t == 0), stop=(t == NT - 1))
                    ins.then_inc(e_pickT, 1)
            turn(NG - 1)
            if upcoming is not None:
                gather(upcoming, 0)
            down(NG - 1)
            if upcoming is not None:
                gather(upcoming, 1)
            pe.wait_ge(e_pickT_done, n + 1)
            for half in range(2):
                pe.wait_ge(e_y_low, n * 2 + (half + 1))
                cols = slice(half * 512, (half + 1) * 512)
                for t in range(NT):
                    out_bank, slots = ps[:, (0, 6)[t] + half, :], pickT[:, t * P:(t + 1) * P]
                    pe.matmul(out_bank, slots, ye_high[:, cols], start=True, stop=False)
                    ins = pe.matmul(out_bank, slots, ye_low[:, cols], start=False, stop=True)
                    if half:
                        ins.then_inc(e_scat, 1)

        for half in range(2):
            gather(0, half)
        with pe.Fori(0, E) as e:
            expert_pass(e, e, e + 1)
        passes = pe.alloc_register("passes_pe")
        pe.reg_mov(passes, E)
        largest = pe.value_load(counts[0:1, E:E + 1], min_val=0, max_val=T)
        with pe.If(largest > CAP):
            with pe.Fori(0, E) as e:
                many = pe.value_load(counts[0:1, bass.ds(e, 1)], min_val=0, max_val=T)
                with pe.If(many > CAP):
                    n = pe.snap(passes)
                    for half in range(2):
                        gather(n + 1, half)
                    expert_pass(n, n + 1, None)
                    pe.reg_add(passes, passes, 1)
        n = pe.snap(passes)
        pe.wait_ge(high_done, n * UNITS + (UNITS + 1))
        landed_wait(pe, FRONT, n, tail)
        for t in range(NT):
            if t == 0:
                pe.wait_ge(e_added, n * 2 - 1)
            ple_up(1, view(FRONT, 2, D), t)
            turn_tile(5, t)
        for u in range(4):
            i = tplace[("ple_gate1", u)]
            pe.wait_ge(low_done, n * UNITS + (UNITS + i + 1))
            wh, wl = parts(i, 2, D)
            for t in range(NT):
                if u == 0:
                    wait_turned(5, t)
                tok = slice(t * P, (t + 1) * P)
                for half in range(2):
                    cols = slice(half * 512, (half + 1) * 512)
                    for kk in range(2):
                        k = 2 * u + kk
                        ins = passes3(ps[:, 4 + 2 * t + half, :], hn_high[:, k, tok], hn_low[:, k, tok], wh[:, kk, cols], wl[:, kk, cols],
                                      k == 0, k == KD - 1)
                    if u == 3:
                        ins.then_inc(gate_ready, 1)
            if u < 3:
                ins.then_inc(gate1_used, 1)

    es.close()


_INS = ["x", "p", "positions", "norm_attn_a", "w_a_in", "norm_q_lat", "norm_kv_lat", "w_q_up", "w_kv_up", "qk_norm_q", "qk_norm_k",
        "w_a_out", "norm_kv_shared", "w_kv_shared", "norm_attn_b", "w_q_b", "w_o_b", "norm_ffn", "w_ffn_gu", "w_ffn_down",
        "w_router", "w_exp_gu", "w_exp_down", "norm_ple", "w_ple_gate", "w_ple_up"]


def kernel(**inputs):
    import numpy as _np
    import concourse.bacc as _bacc
    from concourse.bass_utils import run_bass_kernel_spmd as _run

    nc = _bacc.Bacc("TRN2", target_bir_lowering=False, num_devices=1)
    arrays, aps = {}, {}
    for name in _INS:
        v = _np.ascontiguousarray(inputs[name])
        arrays[f"in_{name}"] = v
        aps[name] = nc.dram_tensor(f"in_{name}", v.shape, mybir.dt.from_np(v.dtype), kind="ExternalInput").ap()
    out = nc.dram_tensor("out", (1, T, D), F32, kind="ExternalOutput").ap()
    build(nc, aps, out)
    r = _run(nc, [arrays], core_ids=[0])
    return r.results[0]["out"]
```
